# Optimizing a Trainium2 kernel written in Bass

```python
import math
import jax, jax.numpy as jnp
from jax import lax
import numpy as np

D_MODEL = 1024
BATCH = 1
SEQ = 256
DEPTH = 2

MEM_LEN = 256
EPS = 1e-6
Q_BLOCK = 128

A_HEADS = 8
A_QK_DIM = 64
A_V_DIM = 2 * A_QK_DIM
A_WIDTH = A_HEADS * A_V_DIM
B_WIDTH = D_MODEL // 2
CONV_W = 3
C_HEADS = 12
C_DIM = 128
C_WIDTH = C_HEADS * C_DIM
X_HEADS = 4
X_DIM = 128
X_WIDTH = X_HEADS * X_DIM

EVEN_MIX = A_WIDTH + B_WIDTH + X_WIDTH
ODD_MIX = C_WIDTH + X_WIDTH
EVEN_IN = 4 * A_WIDTH + 4 * B_WIDTH + 2 * X_WIDTH
ODD_IN = 4 * C_WIDTH + C_HEADS + 2 * X_WIDTH


def rms_norm(x, g):
    xf = x.astype(jnp.float32)
    y = xf * lax.rsqrt(jnp.mean(xf * xf, axis=-1, keepdims=True) + EPS)
    return (y * g.astype(jnp.float32)).astype(x.dtype)

def alibi_slopes(n_heads):
    return jnp.asarray(np.array([2.0 ** (-8.0 * (i + 1) / n_heads) for i in range(n_heads)], dtype=np.float32))

def sweep_query_blocks(block_fn, *q_arrays):
    seq = q_arrays[0].shape[2]
    nb = seq // Q_BLOCK

    def split(a):
        a = a.reshape(a.shape[:2] + (nb, Q_BLOCK) + a.shape[3:])
        return jnp.moveaxis(a, 2, 0)

    starts = jnp.arange(nb, dtype=jnp.int32) * Q_BLOCK
    out = lax.map(lambda args: block_fn(args[0], *args[1:]), (starts,) + tuple(split(a) for a in q_arrays))
    out = jnp.moveaxis(out, 0, 2)
    return out.reshape(out.shape[:2] + (seq,) + out.shape[4:])

def differential_attention(q, k, v, q_g, k_g, lam_params, out_g, lam_init):
    bsz, seq, _ = q.shape
    q = rms_norm(q.reshape(bsz, seq, A_HEADS, 2, A_QK_DIM), q_g).transpose(0, 2, 3, 1, 4)
    k = rms_norm(k.reshape(bsz, seq, A_HEADS, 2, A_QK_DIM), k_g).transpose(0, 2, 3, 1, 4)
    v = v.reshape(bsz, seq, A_HEADS, A_V_DIM).transpose(0, 2, 1, 3)
    lp = lam_params.astype(jnp.float32)
    lam = jnp.exp(jnp.sum(lp[0] * lp[1])) - jnp.exp(jnp.sum(lp[2] * lp[3])) + lam_init
    slopes = alibi_slopes(A_HEADS)
    scale = A_QK_DIM ** -0.5
    k1, k2 = k[:, :, 0], k[:, :, 1]
    k_pos = jnp.arange(seq, dtype=jnp.int32)

    def block(start, q1b, q2b):
        q_pos = start + jnp.arange(Q_BLOCK, dtype=jnp.int32)
        dist = q_pos[:, None] - k_pos[None, :]
        causal = dist >= 0
        bias = -slopes[:, None, None] * dist.astype(jnp.float32)
        s1 = jnp.einsum('bhqd,bhkd->bhqk', q1b, k1).astype(jnp.float32) * scale + bias
        s2 = jnp.einsum('bhqd,bhkd->bhqk', q2b, k2).astype(jnp.float32) * scale + bias
        p1 = jax.nn.softmax(jnp.where(causal, s1, -jnp.inf), axis=-1)
        p2 = jax.nn.softmax(jnp.where(causal, s2, -jnp.inf), axis=-1)
        attn = (p1 - lam * p2).astype(v.dtype)
        return jnp.einsum('bhqk,bhkd->bhqd', attn, v)

    o = sweep_query_blocks(block, q[:, :, 0], q[:, :, 1])
    o = rms_norm(o, out_g) * (1.0 - lam_init)
    return o.transpose(0, 2, 1, 3).reshape(bsz, seq, A_WIDTH)

def causal_depthwise_conv(u, w, b):
    c = u.shape[-1]
    y = lax.conv_general_dilated(u, w[:, None, :].astype(u.dtype), window_strides=(1,),
                                 padding=[(CONV_W - 1, 0)],
                                 dimension_numbers=('NWC', 'WIO', 'NWC'),
                                 feature_group_count=c)
    return y + b.astype(u.dtype)

def short_gated_conv(h, c_gate, b_gate, w, b):
    return b_gate * causal_depthwise_conv(c_gate * h, w, b)

def forgetting_attention(q, k, v, f_logit, f_bias, q_g, k_g):
    bsz, seq, _ = q.shape
    q = rms_norm(q.reshape(bsz, seq, C_HEADS, C_DIM), q_g).transpose(0, 2, 1, 3)
    k = rms_norm(k.reshape(bsz, seq, C_HEADS, C_DIM), k_g).transpose(0, 2, 1, 3)
    v = v.reshape(bsz, seq, C_HEADS, C_DIM).transpose(0, 2, 1, 3)
    log_f = jax.nn.log_sigmoid(f_logit.astype(jnp.float32) + f_bias.astype(jnp.float32))
    cum = jnp.cumsum(log_f, axis=1).transpose(0, 2, 1)
    scale = C_DIM ** -0.5
    k_pos = jnp.arange(seq, dtype=jnp.int32)

    def block(start, qb, cqb):
        q_pos = start + jnp.arange(Q_BLOCK, dtype=jnp.int32)
        causal = q_pos[:, None] >= k_pos[None, :]
        s = jnp.einsum('bhqd,bhkd->bhqk', qb, k).astype(jnp.float32) * scale
        s = s + (cqb[..., :, None] - cum[:, :, None, :])
        p = jax.nn.softmax(jnp.where(causal, s, -jnp.inf), axis=-1).astype(v.dtype)
        return jnp.einsum('bhqk,bhkd->bhqd', p, v)

    o = sweep_query_blocks(block, q, cum)
    return o.transpose(0, 2, 1, 3).reshape(bsz, seq, C_WIDTH)

def memory_cross_attention(q, mem, mem_g, w_mem_kv, q_g, k_g):
    bsz, seq, _ = q.shape
    m = mem.shape[1]
    mk, mv = jnp.split(rms_norm(mem, mem_g) @ w_mem_kv, 2, axis=-1)
    q = rms_norm(q.reshape(bsz, seq, X_HEADS, X_DIM), q_g)
    mk = rms_norm(mk.reshape(bsz, m, X_HEADS, X_DIM), k_g)
    mv = mv.reshape(bsz, m, X_HEADS, X_DIM)
    s = jnp.einsum('bshd,bmhd->bhsm', q, mk).astype(jnp.float32) * (X_DIM ** -0.5)
    p = jax.nn.softmax(s, axis=-1).astype(mv.dtype)
    o = jnp.einsum('bhsm,bmhd->bshd', p, mv)
    return o.reshape(bsz, seq, X_WIDTH)

def even_layer(h, mem, layer, norm_g, w_in, w_out, a_qn, a_kn, a_lam, a_on,
               b_cw, b_cb, x_qn, x_kn, mem_g, w_mem_kv):
    u = rms_norm(h, norm_g)
    proj = u @ w_in
    cuts = np.cumsum([A_WIDTH] * 4 + [B_WIDTH] * 4 + [X_WIDTH] * 2)[:-1].tolist()
    aq, ak, av, az, bh, bc, bb, bz, xq, xz = jnp.split(proj, cuts, axis=-1)
    lam_init = 0.8 - 0.6 * math.exp(-0.3 * layer)
    ya = differential_attention(aq, ak, av, a_qn, a_kn, a_lam, a_on, lam_init)
    yb = short_gated_conv(bh, bc, bb, b_cw, b_cb)
    yx = memory_cross_attention(xq, mem, mem_g, w_mem_kv, x_qn, x_kn)
    y = jnp.concatenate([ya * jax.nn.silu(az), yb * jax.nn.silu(bz), yx * jax.nn.silu(xz)], axis=-1)
    return h + y @ w_out

def odd_layer(h, mem, norm_g, w_in, w_out, c_qn, c_kn, c_fb, x_qn, x_kn, mem_g, w_mem_kv):
    u = rms_norm(h, norm_g)
    proj = u @ w_in
    cuts = np.cumsum([C_WIDTH] * 4 + [C_HEADS] + [X_WIDTH] * 2)[:-1].tolist()
    cq, ck, cv, cz, cf, xq, xz = jnp.split(proj, cuts, axis=-1)
    yc = forgetting_attention(cq, ck, cv, cf, c_fb, c_qn, c_kn)
    yx = memory_cross_attention(xq, mem, mem_g, w_mem_kv, x_qn, x_kn)
    y = jnp.concatenate([yc * jax.nn.silu(cz), yx * jax.nn.silu(xz)], axis=-1)
    return h + y @ w_out

def first_inputs(seed: int = 0) -> dict:
    key = jax.random.key(seed)
    ks = jax.random.split(key, 32)
    it = iter(range(32))
    ne = (DEPTH + 1) // 2
    no = DEPTH // 2

    def nrm(shape, scale):
        return scale * jax.random.normal(ks[next(it)], shape, jnp.float32)

    def gain(shape):
        return 1.0 + 0.02 * jax.random.normal(ks[next(it)], shape, jnp.float32)

    return {
        "x": nrm((BATCH, SEQ, D_MODEL), 1.0),
        "mem": nrm((BATCH, MEM_LEN, D_MODEL), 1.0),
        "e_norm_g": gain((ne, D_MODEL)),
        "e_w_in": nrm((ne, D_MODEL, EVEN_IN), D_MODEL ** -0.5),
        "e_w_out": nrm((ne, EVEN_MIX, D_MODEL), EVEN_MIX ** -0.5),
        "e_a_q_norm_g": gain((ne, A_QK_DIM)),
        "e_a_k_norm_g": gain((ne, A_QK_DIM)),
        "e_a_lambda": nrm((ne, 4, A_QK_DIM), 0.1),
        "e_a_out_norm_g": gain((ne, A_V_DIM)),
        "e_b_conv_w": nrm((ne, CONV_W, B_WIDTH), CONV_W ** -0.5),
        "e_b_conv_b": nrm((ne, B_WIDTH), 0.02),
        "e_x_q_norm_g": gain((ne, X_DIM)),
        "e_x_k_norm_g": gain((ne, X_DIM)),
        "e_mem_norm_g": gain((ne, D_MODEL)),
        "e_w_mem_kv": nrm((ne, D_MODEL, 2 * X_WIDTH), D_MODEL ** -0.5),
        "o_norm_g": gain((no, D_MODEL)),
        "o_w_in": nrm((no, D_MODEL, ODD_IN), D_MODEL ** -0.5),
        "o_w_out": nrm((no, ODD_MIX, D_MODEL), ODD_MIX ** -0.5),
        "o_c_q_norm_g": gain((no, C_DIM)),
        "o_c_k_norm_g": gain((no, C_DIM)),
        "o_c_forget_b": 3.0 + nrm((no, C_HEADS), 0.5),
        "o_x_q_norm_g": gain((no, X_DIM)),
        "o_x_k_norm_g": gain((no, X_DIM)),
        "o_mem_norm_g": gain((no, D_MODEL)),
        "o_w_mem_kv": nrm((no, D_MODEL, 2 * X_WIDTH), D_MODEL ** -0.5),
    }

def first_block(x, mem, e_norm_g, e_w_in, e_w_out, e_a_q_norm_g, e_a_k_norm_g, e_a_lambda,
              e_a_out_norm_g, e_b_conv_w, e_b_conv_b, e_x_q_norm_g, e_x_k_norm_g,
              e_mem_norm_g, e_w_mem_kv, o_norm_g, o_w_in, o_w_out, o_c_q_norm_g,
              o_c_k_norm_g, o_c_forget_b, o_x_q_norm_g, o_x_k_norm_g, o_mem_norm_g,
              o_w_mem_kv):
    h = x
    for layer in range(DEPTH):
        i = layer // 2
        if layer % 2 == 0:
            h = even_layer(h, mem, layer, e_norm_g[i], e_w_in[i], e_w_out[i],
                           e_a_q_norm_g[i], e_a_k_norm_g[i], e_a_lambda[i], e_a_out_norm_g[i],
                           e_b_conv_w[i], e_b_conv_b[i], e_x_q_norm_g[i], e_x_k_norm_g[i],
                           e_mem_norm_g[i], e_w_mem_kv[i])
        else:
            h = odd_layer(h, mem, o_norm_g[i], o_w_in[i], o_w_out[i],
                          o_c_q_norm_g[i], o_c_k_norm_g[i], o_c_forget_b[i],
                          o_x_q_norm_g[i], o_x_k_norm_g[i], o_mem_norm_g[i], o_w_mem_kv[i])
    return h


DEPTH_2 = 1

GRID_W = 64
CTX_LEN = 256
HEAD_DIM = 64
ATTN_HEADS = 8
ATTN_KV_HEADS = 2
GQA_GROUP = ATTN_HEADS // ATTN_KV_HEADS
RET_HEADS = 8
ATTN_WIDTH = ATTN_HEADS * HEAD_DIM
KV_WIDTH = ATTN_KV_HEADS * HEAD_DIM
RET_WIDTH = RET_HEADS * HEAD_DIM
MIX_WIDTH = ATTN_WIDTH + RET_WIDTH
IN_PROJ_WIDTH = ATTN_WIDTH + 2 * KV_WIDTH + 4 * RET_WIDTH
SPLITS = (ATTN_WIDTH, ATTN_WIDTH + KV_WIDTH, ATTN_WIDTH + 2 * KV_WIDTH,
          ATTN_WIDTH + 2 * KV_WIDTH + RET_WIDTH, ATTN_WIDTH + 2 * KV_WIDTH + 2 * RET_WIDTH,
          ATTN_WIDTH + 2 * KV_WIDTH + 3 * RET_WIDTH)
FFN_HIDDEN = -(-8 * D_MODEL // (3 * 256)) * 256
N_MOD = 6
QBLOCK = 128
RET_CHUNK = 128
ROPE_BASE = 10000.0
ATTN_SCALE = HEAD_DIM ** -0.5


def rms_norm_2(x, g):
    xf = x.astype(jnp.float32)
    y = xf * lax.rsqrt(jnp.mean(xf * xf, axis=-1, keepdims=True) + EPS)
    return (y * g.astype(jnp.float32)).astype(x.dtype)

def head_group_norm(o):
    mu = jnp.mean(o, axis=-1, keepdims=True)
    var = jnp.mean(jnp.square(o - mu), axis=-1, keepdims=True)
    return (o - mu) * lax.rsqrt(var + EPS)

def modulate(h, shift, scale):
    return h * (1 + scale) + shift

def axial_rope(rows):
    row = jnp.broadcast_to(jnp.arange(rows)[:, None], (rows, GRID_W)).reshape(-1).astype(jnp.float32)
    col = jnp.broadcast_to(jnp.arange(GRID_W)[None, :], (rows, GRID_W)).reshape(-1).astype(jnp.float32)
    n_freq = HEAD_DIM // 4
    inv = ROPE_BASE ** (-jnp.arange(n_freq, dtype=jnp.float32) / n_freq)
    ang = jnp.concatenate([row[:, None] * inv, col[:, None] * inv], axis=-1)
    return jnp.cos(ang), jnp.sin(ang)

def apply_rope(x, cos, sin):
    half = HEAD_DIM // 2
    x1, x2 = x[..., :half], x[..., half:]
    c, s = cos[None, :, None, :], sin[None, :, None, :]
    return jnp.concatenate([x1 * c - x2 * s, x1 * s + x2 * c], axis=-1).astype(x.dtype)

def project(h, w_in, q_norm_g, k_norm_g):
    B, N, _ = h.shape
    qa, ka, va, qr, kr, vr, gr = jnp.split(h @ w_in, SPLITS, axis=-1)
    heads = lambda a: a.reshape(B, N, -1, HEAD_DIM)
    qa = rms_norm_2(heads(qa), q_norm_g)
    ka = rms_norm_2(heads(ka), k_norm_g)
    return qa, ka, heads(va), heads(qr), heads(kr) * ATTN_SCALE, heads(vr), gr

def gqa_block(q, k, v):
    B, Q = q.shape[:2]
    qg = q.reshape(B, Q, ATTN_KV_HEADS, GQA_GROUP, HEAD_DIM)
    s = jnp.einsum('bqkgd,btkd->bkgqt', qg, k, preferred_element_type=jnp.float32) * ATTN_SCALE
    p = jax.nn.softmax(s, axis=-1).astype(v.dtype)
    o = jnp.einsum('bkgqt,btkd->bqkgd', p, v)
    return o.reshape(B, Q, ATTN_WIDTH)

def latent_attention(q, k_lat, v_lat, k_ctx, v_ctx):
    B, N = q.shape[:2]
    k_all = jnp.concatenate([k_ctx, k_lat], axis=1)
    v_all = jnp.concatenate([v_ctx, v_lat], axis=1)
    qb = q.reshape(B, N // QBLOCK, QBLOCK, ATTN_HEADS, HEAD_DIM).swapaxes(0, 1)
    o = lax.map(lambda qi: gqa_block(qi, k_all, v_all), qb)
    return o.swapaxes(0, 1).reshape(B, N, ATTN_WIDTH)

def retention_chunkwise(q, k, v, log_gamma, state0):
    B, N, H, d = q.shape
    C = RET_CHUNK
    nc = N // C
    lg = log_gamma.astype(jnp.float32)
    chunks = lambda a: a.astype(jnp.float32).reshape(B, nc, C, H, d).transpose(1, 0, 3, 2, 4)
    pos = jnp.arange(C, dtype=jnp.float32)
    diff = pos[:, None] - pos[None, :]
    decay_mat = jnp.where(diff >= 0, jnp.exp(lg[:, None, None] * jnp.maximum(diff, 0.0)), 0.0)
    q_decay = jnp.exp(lg[:, None] * (pos + 1.0))[..., None]
    k_decay = jnp.exp(lg[:, None] * (C - 1.0 - pos))[..., None]
    chunk_decay = jnp.exp(lg * C)[:, None, None]

    def step(state, qkv):
        qc, kc, vc = qkv
        inner = jnp.einsum('bhid,bhjd->bhij', qc, kc) * decay_mat
        o = jnp.einsum('bhij,bhjd->bhid', inner, vc) + jnp.einsum('bhid,bhde->bhie', qc, state) * q_decay
        state = state * chunk_decay + jnp.einsum('bhjd,bhje->bhde', kc * k_decay, vc)
        return state, o

    state, o = lax.scan(step, state0.astype(jnp.float32), (chunks(q), chunks(k), chunks(v)))
    return o.transpose(1, 0, 3, 2, 4).reshape(B, N, H, d), state

def bidir_retention(q, k, v, lg_f, lg_b, state_f, state_b):
    o_f, s_f = retention_chunkwise(q, k, v, lg_f, state_f)
    o_b, s_b = retention_chunkwise(q[:, ::-1], k[:, ::-1], v[:, ::-1], lg_b, state_b)
    return o_f + o_b[:, ::-1], s_f, s_b

def merge_heads(att, ret, g_r, w_out):
    B, N = att.shape[:2]
    ret = head_group_norm(ret).reshape(B, N, RET_WIDTH).astype(g_r.dtype) * jax.nn.silu(g_r)
    return jnp.concatenate([att, ret], axis=-1) @ w_out

def swiglu(h, w_ffn_in, w_ffn_out):
    a, b = jnp.split(h @ w_ffn_in, 2, axis=-1)
    return (jax.nn.silu(a) * b) @ w_ffn_out

def second_inputs(seed: int = 0) -> dict:
    key = jax.random.key(seed)
    ks = jax.random.split(key, 18)
    D = D_MODEL
    nrm = lambda k, shape: jax.random.normal(k, shape, jnp.float32)
    w = lambda k, shape, fan_in, g=1.0: nrm(k, shape) * (g * fan_in ** -0.5)
    gain = lambda k, shape: 1.0 + 0.05 * nrm(k, shape)
    gammas = 1.0 - 2.0 ** (-5.0 - jnp.arange(RET_HEADS, dtype=jnp.float32))
    base = jnp.log(-jnp.log(gammas))
    return {
        'x': nrm(ks[0], (BATCH, SEQ, D)),
        'c': nrm(ks[1], (BATCH, D)),
        'ctx': nrm(ks[2], (BATCH, CTX_LEN, D)),
        'c_ctx': nrm(ks[3], (D,)),
        'w_mod': w(ks[4], (DEPTH_2, D, N_MOD * D), D, 0.5),
        'b_mod': 0.02 * nrm(ks[5], (DEPTH_2, N_MOD * D)),
        'g_pre_mix': gain(ks[6], (DEPTH_2, D)),
        'g_post_mix': gain(ks[7], (DEPTH_2, D)),
        'g_pre_ffn': gain(ks[8], (DEPTH_2, D)),
        'g_post_ffn': gain(ks[9], (DEPTH_2, D)),
        'w_in': w(ks[10], (DEPTH_2, D, IN_PROJ_WIDTH), D),
        'q_norm_g': gain(ks[11], (DEPTH_2, HEAD_DIM)),
        'k_norm_g': gain(ks[12], (DEPTH_2, HEAD_DIM)),
        'ret_decay_fwd': base + 0.1 * nrm(ks[13], (DEPTH_2, RET_HEADS)),
        'ret_decay_bwd': base + 0.1 * nrm(ks[14], (DEPTH_2, RET_HEADS)),
        'w_out': w(ks[15], (DEPTH_2, MIX_WIDTH, D), MIX_WIDTH),
        'w_ffn_in': w(ks[16], (DEPTH_2, D, 2 * FFN_HIDDEN), D),
        'w_ffn_out': w(ks[17], (DEPTH_2, FFN_HIDDEN, D), FFN_HIDDEN),
    }

def second_block(x, c, ctx, c_ctx, w_mod, b_mod, g_pre_mix, g_post_mix, g_pre_ffn, g_post_ffn,
              w_in, q_norm_g, k_norm_g, ret_decay_fwd, ret_decay_bwd, w_out, w_ffn_in, w_ffn_out):
    B, n_lat, _ = x.shape
    rows = n_lat // GRID_W
    cos, sin = axial_rope(rows)
    for layer in range(DEPTH_2):
        mod_x = (jax.nn.silu(c) @ w_mod[layer] + b_mod[layer])[:, None, :]
        mod_c = jax.nn.silu(c_ctx) @ w_mod[layer] + b_mod[layer]
        sh_m, sc_m, gt_m, sh_f, sc_f, gt_f = jnp.split(mod_x, N_MOD, axis=-1)
        csh_m, csc_m, cgt_m, csh_f, csc_f, cgt_f = jnp.split(mod_c, N_MOD, axis=-1)
        lg_f = -jnp.exp(ret_decay_fwd[layer].astype(jnp.float32))
        lg_b = -jnp.exp(ret_decay_bwd[layer].astype(jnp.float32))

        hx = modulate(rms_norm_2(x, g_pre_mix[layer]), sh_m, sc_m)
        hc = modulate(rms_norm_2(ctx, g_pre_mix[layer]), csh_m, csc_m)
        qa_x, ka_x, va_x, qr_x, kr_x, vr_x, gr_x = project(hx, w_in[layer], q_norm_g[layer], k_norm_g[layer])
        qa_c, ka_c, va_c, qr_c, kr_c, vr_c, gr_c = project(hc, w_in[layer], q_norm_g[layer], k_norm_g[layer])

        zero_state = jnp.zeros((B, RET_HEADS, HEAD_DIM, HEAD_DIM), jnp.float32)
        ret_c, st_f, st_b = bidir_retention(qr_c, kr_c, vr_c, lg_f, lg_b, zero_state, zero_state)

        att_x = latent_attention(apply_rope(qa_x, cos, sin), apply_rope(ka_x, cos, sin), va_x, ka_c, va_c)
        ret_x, _, _ = bidir_retention(apply_rope(qr_x, cos, sin), apply_rope(kr_x, cos, sin), vr_x,
                                      lg_f, lg_b, st_f, st_b)
        mix_x = merge_heads(att_x, ret_x, gr_x, w_out[layer])
        x_new = x + gt_m * rms_norm_2(mix_x, g_post_mix[layer])
        hf = modulate(rms_norm_2(x_new, g_pre_ffn[layer]), sh_f, sc_f)
        x_new = x_new + gt_f * rms_norm_2(swiglu(hf, w_ffn_in[layer], w_ffn_out[layer]), g_post_ffn[layer])

        if layer < DEPTH_2 - 1:
            att_c = gqa_block(qa_c, ka_c, va_c)
            mix_c = merge_heads(att_c, ret_c, gr_c, w_out[layer])
            ctx = ctx + cgt_m * rms_norm_2(mix_c, g_post_mix[layer])
            hfc = modulate(rms_norm_2(ctx, g_pre_ffn[layer]), csh_f, csc_f)
            ctx = ctx + cgt_f * rms_norm_2(swiglu(hfc, w_ffn_in[layer], w_ffn_out[layer]), g_post_ffn[layer])
        x = x_new
    return x


def setup_inputs(seed=0):
    out = dict(first_inputs(seed))
    for name, value in second_inputs(seed + 1).items():
        if name != "x":
            out[name + "_2"] = value
    return out


def reference(
    x, mem, e_norm_g, e_w_in, e_w_out, e_a_q_norm_g, e_a_k_norm_g, e_a_lambda, e_a_out_norm_g,
    e_b_conv_w, e_b_conv_b, e_x_q_norm_g, e_x_k_norm_g, e_mem_norm_g, e_w_mem_kv, o_norm_g,
    o_w_in, o_w_out, o_c_q_norm_g, o_c_k_norm_g, o_c_forget_b, o_x_q_norm_g, o_x_k_norm_g,
    o_mem_norm_g, o_w_mem_kv, c_2, ctx_2, c_ctx_2, w_mod_2, b_mod_2, g_pre_mix_2, g_post_mix_2,
    g_pre_ffn_2, g_post_ffn_2, w_in_2, q_norm_g_2, k_norm_g_2, ret_decay_fwd_2, ret_decay_bwd_2,
    w_out_2, w_ffn_in_2, w_ffn_out_2,
):
    x = first_block(
        x, mem, e_norm_g, e_w_in, e_w_out, e_a_q_norm_g, e_a_k_norm_g, e_a_lambda,
        e_a_out_norm_g, e_b_conv_w, e_b_conv_b, e_x_q_norm_g, e_x_k_norm_g, e_mem_norm_g,
        e_w_mem_kv, o_norm_g, o_w_in, o_w_out, o_c_q_norm_g, o_c_k_norm_g, o_c_forget_b,
        o_x_q_norm_g, o_x_k_norm_g, o_mem_norm_g, o_w_mem_kv,
    )
    return second_block(
        x, c_2, ctx_2, c_ctx_2, w_mod_2, b_mod_2, g_pre_mix_2, g_post_mix_2, g_pre_ffn_2,
        g_post_ffn_2, w_in_2, q_norm_g_2, k_norm_g_2, ret_decay_fwd_2, ret_decay_bwd_2, w_out_2,
        w_ffn_in_2, w_ffn_out_2,
    )


_drawn_inputs = setup_inputs


def setup_inputs(seed=0):
    import zlib

    import numpy as np

    out = dict(_drawn_inputs(seed))
    spreads = {}
    factors = {'e_norm_g': 3.112,
     'e_a_q_norm_g': 8.0,
     'e_a_k_norm_g': 8.0,
     'e_a_out_norm_g': 7.789,
     'e_b_conv_b': 8.0,
     'e_x_q_norm_g': 8.0,
     'e_x_k_norm_g': 8.0,
     'e_mem_norm_g': 8.0,
     'o_norm_g': 8.0,
     'o_c_q_norm_g': 8.0,
     'o_c_k_norm_g': 8.0,
     'o_x_q_norm_g': 8.0,
     'o_x_k_norm_g': 8.0,
     'o_mem_norm_g': 8.0,
     'g_post_mix_2': 200.0,
     'g_pre_ffn_2': 86.31,
     'g_post_ffn_2': 190.879,
     'q_norm_g_2': 64.0,
     'k_norm_g_2': 64.0,
     'ctx_2': 3.382,
     'c_ctx_2': 3.86,
     'b_mod_2': 8.0,
     'g_pre_mix_2': 8.0,
     'ret_decay_fwd_2': 8.0,
     'ret_decay_bwd_2': 8.0}
    for name, (base, spread) in spreads.items():
        noise = np.random.default_rng([zlib.crc32(name.encode()), seed]).standard_normal(out[name].shape)
        drawn = base * np.exp(spread * noise) if base else spread * noise
        out[name] = __import__('jax').numpy.asarray(drawn.astype(out[name].dtype))
    for name, factor in factors.items():
        out[name] = (out[name] * factor).astype(out[name].dtype)
    return out
```

```python
import math
from contextlib import ExitStack

import numpy as np

import concourse.bass as bass
from concourse import mybir

F32 = mybir.dt.float32
F32R = mybir.dt.float32r
ACT = mybir.ActivationFunctionType
ALU = mybir.AluOpType
AX = mybir.AxisListType

P = 128
D = 1024
T = 256
NT = T // P
KT = D // P
CW = 512
SUBK = 2
RAWK = 4
RAW_SLOTS, SPLIT_SLOTS, LEAD = 3, 4, 3
EPS = 1e-6
LAM_INIT = 0.8 - 0.6 * math.exp(-0.3 * 0)
FFN = 2816
EVEN_Y, ODD_Y, MIX_Y = 2048, 2048, 1024
BIG = -1e30

ROW = dict(e_norm=0, e_mem=8, o_norm=16, o_mem=24, pre_mix=32, pre_ffn=40, b_mod=48, c=96, c_ctx=104,
           conv_w=112, conv_b=124)
ROW2 = dict(aq=0, ak=1, aon=2, exq=3, exk=4, cq=5, ck=6, oxq=7, oxk=8)

CONST = {}


def constants():
    p = np.arange(P)[:, None]
    t = np.arange(T)[None, :]
    parts = {
        "ident": np.eye(P, dtype=np.float32),
        "tri": (p <= t).astype(np.float32),
        "dist": np.concatenate([np.where(p >= t[:, :P], p - t[:, :P], 1e34),
                                np.where(p + P >= t, p + P - t, 1e34)], axis=1).astype(np.float32),
    }
    pos = np.arange(T).reshape(NT, P).T.astype(np.float32)
    parts["expo"] = np.concatenate([pos + 1, T - pos, T - 1 - pos, pos], axis=1)
    at, out = 0, []
    for name, a in parts.items():
        CONST[name] = (at, a.shape[1])
        at += a.shape[1]
        out.append(a.astype(np.float32))
    first = np.concatenate(out, axis=1)
    j = np.arange(T).reshape(NT, P).T[:, :, None]
    i = np.arange(T)[None, None, :]
    ret = np.concatenate([np.maximum(i - j, 0).reshape(P, -1), np.maximum(j - i, 0).reshape(P, -1),
                          (0.125 * (1 + (i == j))).reshape(P, -1)], axis=1).astype(np.float32)
    tok = np.arange(T)
    inv = (10000.0 ** (-np.arange(16, dtype=np.float32) / 16)).astype(np.float32)
    ang = np.concatenate([(tok // 64).astype(np.float32)[:, None] * inv,
                          (tok % 64).astype(np.float32)[:, None] * inv], axis=1).astype(np.float32)
    c, s = np.cos(ang).astype(np.float32), np.sin(ang).astype(np.float32)
    cc = np.concatenate([c, c], axis=1).reshape(NT, P, 64).transpose(1, 0, 2).reshape(P, -1)
    ss = np.concatenate([-s, s], axis=1).reshape(NT, P, 64).transpose(1, 0, 2).reshape(P, -1)
    return first, ret, np.ascontiguousarray(np.concatenate([cc, ss], axis=1))




class Step:

    def __init__(self, kind, panel=None, sub=None, h=None, src=None, dst=None, waits=(), xn=None, ready=None,
                 key=None, scale=None, bias=None, half=None, tile=None, gs=None, c=None, h_evac=None, gate=None,
                 gate_tile=None, tiles=None, prev_s=None, part=None, what=None, after=0, rows=0, chunk=None,
                 u=None, ctx=None, prev=None, mod_read=None, bias_done=None, which=None, mod_sb=None,
                 v_evac=None, g=None, rope_done=None, qfb=None, prev_o=None, qkT_sb=None, m_ready=None,
                 am_ready=None, ret_sb=None, gate_ready=None):
        self.kind, self.on, self.free = kind, {}, {}
        self.panel, self.sub, self.h, self.src, self.dst, self.waits = panel, sub, h, src, dst, waits
        self.xn, self.ready, self.key, self.scale, self.bias, self.half = xn, ready, key, scale, bias, half
        self.tile, self.gs, self.c, self.h_evac, self.gate = tile, gs, c, h_evac, gate
        self.gate_tile, self.tiles, self.prev_s, self.part = gate_tile, tiles, prev_s, part
        self.what, self.after, self.rows, self.chunk, self.u, self.ctx = what, after, rows, chunk, u, ctx
        self.prev, self.mod_read, self.bias_done, self.which, self.mod_sb = prev, mod_read, bias_done, which, mod_sb
        self.v_evac, self.g, self.rope_done, self.qfb, self.prev_o = v_evac, g, rope_done, qfb, prev_o
        self.qkT_sb, self.m_ready, self.am_ready, self.ret_sb = qkT_sb, m_ready, am_ready, ret_sb
        self.gate_ready = gate_ready


class Panel:

    def __init__(self, w, col, ncols, src, orient, kts):
        self.w, self.col, self.ncols, self.src, self.orient, self.kts = w, col, ncols, src, orient, kts


class Sub:

    def __init__(self, i, panel, k0, nk, first, last, waits):
        self.i, self.panel, self.k0, self.nk, self.waits = i, panel, k0, nk, waits
        self.first, self.last = first, last


class Load:

    def __init__(self, i, w, row, nk, col, ncols, read):
        self.i, self.w, self.row, self.nk, self.col, self.ncols, self.read = i, w, row, nk, col, ncols, read


class Head:

    def __init__(self, type, g, j, tile, ready, gain=None, rows=None, part=0, base=0, kT_sb=None):
        self.type, self.g, self.j, self.tile, self.ready = type, g, j, tile, ready
        self.gain, self.rows, self.part, self.base, self.kT_sb = gain, rows, part, base, kT_sb


class Plan:

    def __init__(self):
        self.steps = []
        self.count = {}
        self.subs = []
        self.busy = {}
        self.acc_uses = 0
        self.src = {}
        self.tile_ready = {}
        self.later = {}
        self.pos = 0
        self.heads = 0
        self.gated = {}
        self.chunks = []
        self.pending = {}

    def tick(self, st, *names):
        for n in names:
            self.count[n] = self.count.get(n, 0) + 1
            st.on[n] = self.count[n]

    def step(self, kind, **kw):
        st = Step(kind, **kw)
        self.steps.append(st)
        return st

    def uses(self, st, bank, by):
        st.free[bank] = self.busy.get(bank)
        self.busy[bank] = (by, st.on[by])

    def next_acc(self, st, by):
        st.acc = self.acc_uses % 2
        st.free["acc"] = self.busy.get(("acc", st.acc))
        self.busy[("acc", st.acc)] = (by, st.on[by])
        self.acc_uses += 1

    def panel(self, w, col, ncols, src, evac, orient="tok", kts=KT, opened=False, order=None, **kw):
        pan = Panel(w, col, ncols, src, orient, kts)
        ev = Step("evac_" + evac, panel=pan, **kw)
        ticks = {"norm": ("sq_ready", "ms_ready", "rstd_ready", "qk_evac"), "copy": ("v_evac",),
                 "gate": ("tanh_ready", "gate_ready"), "conv_h": ("v_evac",), "conv_c": ("conv_u",),
                 "conv_b": ("v_evac",), "conv_z": ("tanh_ready", "gate_ready"),
                 "resid": ("resid_done",), "forget": ("forget_in",),
                 "rope": ("rope_done",), "normrope": ("sq_ready", "ms_ready", "rstd_ready", "norm_mid", "rope_done"),
                 "ctxkv": ("sq_ready", "ms_ready", "rstd_ready", "norm_mid", "v_evac", "rope_done"),
                 "latkv": ("sq_ready", "ms_ready", "rstd_ready", "norm_mid", "v_evac", "rope_done"),
                 "mix": ("v_evac",), "ffa": ("tanh_ready", "gate_ready"), "ffb": ("ytmp_ready", "yhi_ready", "y_ready")}
        frees = {"norm": "qk_evac", "copy": "v_evac", "gate": "gate_ready", "conv_h": "v_evac", "conv_c": "conv_u",
                 "conv_b": "v_evac", "conv_z": "gate_ready", "resid": "resid_done", "forget": "forget_in",
                 "rope": "rope_done", "normrope": "norm_mid", "ctxkv": "v_evac", "latkv": "v_evac",
                 "mix": "v_evac", "ffa": "gate_ready", "ffb": "ytmp_ready"}
        pan.ev, pan.ticks, pan.frees = ev, ticks[evac], frees[evac]
        pan.acc = self.acc_uses % 2
        pan.free_acc = self.busy.get(("acc", pan.acc))
        self.acc_uses += 1
        pan.done = 0
        if not opened:
            for a, b in order or [(0, kts)]:
                self.parts(pan, a, b)
        return ev

    def parts(self, pan, first, end):
        for k0 in range(first, end, SUBK):
            nk = min(SUBK, end - k0)
            first = pan.done == 0
            pan.done += nk
            waits = []
            if first:
                waits += [pan.free_acc] if pan.free_acc else []
                waits += [self.src[pan.src]] if pan.src in self.src else []
            if pan.src == "y":
                waits.append(("y_ready", max(self.tile_ready[k] for k in range(k0, k0 + nk))))
            sub = Sub(len(self.subs), pan, k0, nk, first, pan.done == pan.kts, waits)
            self.subs.append(sub)
            self.steps.append(Step("sub", sub=sub))
            if sub.last:
                ev = pan.ev
                ev.done, ev.acc = len(self.subs), pan.acc
                self.tick(ev, *pan.ticks)
                self.busy[("acc", pan.acc)] = (pan.frees, ev.on[pan.frees])
                scr_by = {"evac_norm": "ms_ready", "evac_rope": "rope_done", "evac_normrope": "rope_done",
                          "evac_ctxkv": "rope_done", "evac_latkv": "rope_done", "evac_ffb": "y_ready"}.get(ev.kind)
                if scr_by:
                    self.uses(ev, "scr", scr_by)
                self.steps.append(ev)
                if ev.kind in ("evac_gate", "evac_conv_z"):
                    for k in range(ev.tile, ev.tile + pan.ncols // P):
                        self.gated[k] = ev.on["gate_ready"]
                if ev.dst:
                    assert not self.pending.get(ev.dst[0]), ev.dst
                if ev.kind == "evac_ffb":
                    for k in ev.tiles:
                        self.tile_ready[k] = ev.on["y_ready"]
            for make in self.later.pop(self.pos, []):
                make()
            self.pos += 1

    def at(self, pos, make):
        self.later.setdefault(max(pos, self.pos), []).append(make)

    def flush(self):
        while self.later:
            p = min(self.later)
            for make in self.later.pop(p):
                make()

    def norm_rows(self, src, dst, *waits):
        st = self.step("rows_norm", src=src, dst=dst, waits=waits)
        self.tick(st, "sq_ready", "ms_ready", "rstd_ready", "rows_ready")
        self.uses(st, "scr", "sq_ready")
        return st

    def transposed(self, xn, ready, key, scale, bias=None):
        for half in range(2):
            st = self.step("rows_T", xn=xn, ready=ready, key=key, scale=scale, bias=bias, half=half)
            self.tick(st, "rt_ps", "rt_hi", "rt_lo")
            if bias is not None:
                self.tick(st, "rt_tmp")
                self.uses(st, "scr", "rt_lo")
            self.next_acc(st, "rt_tmp" if bias is not None else "rt_lo")
        self.src[key] = ("rt_lo", st.on["rt_lo"])

    def head(self, h, pos):
        h.n = self.heads
        self.heads += 1
        self.pending[h.g] = self.pending.get(h.g, 0) + 1
        kind = h.type

        def f1():
            h.f1 = self.step("qkT", h=h, prev_s=self.count.get("s_ps", 0))
            self.tick(h.f1, "qkT_ps", "qkT_sb")
            self.uses(h.f1, "tp", "qkT_sb")

        def f2(transposes_due=0):
            h.f2 = self.step("scores", h=h)
            h.f2.qkT_sb = self.count["qkT_sb"]
            h.f2.prev_pt = self.count.get("PT_ps", 0) + transposes_due
            self.tick(h.f2, "s_ps", "mx_ready", "exp_ready", "p_ready")
            if kind in "AC":
                self.tick(h.f2, "s_rd")
            by = "s_rd" if kind in "AC" else "exp_ready"
            banks = {"A": ("s0", "s1"), "G": ("s0", "s1")}.get(kind, (f"s{h.n % 2}",))
            h.banks = banks
            for b in banks:
                self.uses(h.f2, b, by)

        def f3(part=0):
            st = self.step("PT", h=h, part=part)
            st.p_ready = h.f2.on["p_ready"]
            st.prev_o = self.count.get("o_ps", 0)
            self.tick(st, "PT_ps", "PT_sb")
            self.uses(st, "tp", "PT_sb")
            h.f3 = st

        def f4():
            self.pending[h.g] -= 1
            h.f4 = self.step("pv", h=h)
            h.f4.PT_sb = h.f3.on["PT_sb"]
            self.tick(h.f4, "o_ps")
            if kind == "A":
                self.tick(h.f4, "sq_ready", "ms_ready", "rstd_ready", "on_ready")
                self.uses(h.f4, "o", "on_ready")
                self.uses(h.f4, "scr", "sq_ready")
            elif kind == "G":
                self.tick(h.f4, "yhi_ready", "y_ready")
                self.uses(h.f4, "o", "y_ready")
                self.tile_ready[h.tile] = h.f4.on["y_ready"]
            else:
                self.tick(h.f4, "ytmp_ready", "yhi_ready", "y_ready")
                h.f4.gate_ready = self.gated[h.tile]
                self.uses(h.f4, "o", "ytmp_ready")
                self.tile_ready[h.tile] = h.f4.on["y_ready"]

        def f5():
            h.f5 = self.step("oT", h=h)
            h.f5.on_ready = h.f4.on["on_ready"]
            h.f5.gate_ready = self.gated[h.tile]
            self.tick(h.f5, "oT_ps", "ytmp_ready", "yhi_ready", "y_ready")
            self.uses(h.f5, "tp", "ytmp_ready")
            self.tile_ready[h.tile] = h.f5.on["y_ready"]

        def due(at, make):
            if pos is not None:
                self.at(pos + at, make)
        due(1, f1)
        due(2, f2)
        due(5 if kind == "A" else 4, f3)
        due(6 if kind == "A" else 5, f4)
        if kind == "A":
            due(8, f5)
        return f1, f2, f3, f4

    def grouped(self, heads, pos):
        fs = [self.head(h, None) for h in heads]

        def beside(i):
            if i > 0:
                fs[i - 1][2](0)
            if i < len(heads):
                fs[i][1](i > 0)
            if i > 0:
                fs[i - 1][2](1)
            if i + 1 < len(heads) and heads[i + 1].part == 0:
                fs[i + 1][0]()
            if i > 0:
                fs[i - 1][3]()
        self.at(pos, fs[0][0])
        for i in range(len(heads) + 1):
            self.at(pos + 1 + i, lambda i=i: beside(i))
        return pos + 1 + len(heads)

    def residual(self):
        return [(n, self.count[n]) for n in ("resid_done", "post_done") if n in self.count]

    def load(self, what, after=0, rows=0):
        st = self.step("load", what=what, after=after, rows=rows)
        self.tick(st, "loaded_" + what)
        return st

    def mod(self, pos, chunk, ctx=False, gate=False):
        pos = max(pos, self.pos) + max(pos, self.pos) % 2

        def read(u):
            if u == 0 and gate:
                st = self.step("mod_bias_in", chunk=chunk, prev=self.count.get("mod_ps", 0))
                self.tick(st, "bias_in")
            st = self.step("mod", chunk=chunk, u=u, ctx=ctx)
            self.tick(st, "mod_read")

        def out():
            if gate:
                st = self.step("mod_bias", chunk=chunk)
                st.on["bias_in"] = self.count["bias_in"]
                self.tick(st, "bias_done")
            st = self.step("mod_out", chunk=chunk, ctx=ctx, gate=gate, mod_read=self.count["mod_read"],
                           bias_done=self.count.get("bias_done", 0))
            self.tick(st, "mod_ps", "mod_sb")
            self.uses(st, "tp", "mod_sb")
            self.chunks.append(chunk)
        self.at(pos, lambda: read(0))
        self.at(pos + 2, lambda: read(1))
        self.at(pos + 4, out)
        return pos + 6


def make_plan(stop=None):
    pl = Plan()

    def heads(kind, g, evs, base, n, tile0, gap=4, **kw):
        ready = [(s, e.on[s]) for e in evs for s in ("qk_evac", "v_evac") if s in e.on]
        for j in range(n):
            pl.head(Head(kind, g, j, tile0 + j, ready, **kw), base)
            base += gap
        return base

    pl.step("setup")
    st = pl.norm_rows("g0", "g0", ("loaded_g0", 16))
    pl.transposed("g0", st.on["rows_ready"], "x", ROW["e_norm"])
    stm = pl.norm_rows("h", "h", ("loaded_h", 16))
    pl.transposed("h", stm.on["rows_ready"], "side", ROW["e_mem"])
    W = "e_w_in"
    evs = [pl.panel(W, 0, CW, "x", "norm", gs=64, dst=("g0", 0)),
           pl.panel(W, 1024, CW, "x", "norm", gs=64, dst=("g0", 1)),
           pl.panel(W, 2048, CW, "x", "copy", dst=("g0", 2))]
    b = heads("A", "g0", evs, pl.pos, 4, 0)
    pl.panel(W, 3072, CW, "x", "gate", "col", tile=0)
    evs = [pl.panel(W, 512, CW, "x", "norm", gs=64, dst=("g1", 0)),
           pl.panel(W, 1536, CW, "x", "norm", gs=64, dst=("g1", 1)),
           pl.panel(W, 2560, CW, "x", "copy", dst=("g1", 2))]
    b = heads("A", "g1", evs, max(b, pl.pos), 4, 4)
    pl.panel(W, 3584, CW, "x", "gate", "col", tile=4)
    evs = [pl.panel(W, 6144, CW, "x", "norm", gs=128, dst=("g0", 0)),
           pl.panel("e_w_mem_kv", 0, CW, "side", "norm", gs=128, dst=("g0", 1)),
           pl.panel("e_w_mem_kv", CW, CW, "side", "copy", dst=("g0", 2))]
    b = heads("X", "g0", evs, max(b, pl.pos), 4, 12, gain="ex")
    pl.panel(W, 6656, CW, "x", "gate", "col", tile=12)
    ch = pl.panel(W, 4096, CW, "x", "conv_h", "col")
    pl.panel(W, 4608, CW, "x", "conv_c", "col", h_evac=ch.on["v_evac"])
    pl.panel(W, 5120, CW, "x", "conv_b", "col")
    ev = pl.panel(W, 5632, CW, "x", "conv_z", "col", tile=8)
    st = pl.step("conv", gate=ev.on["gate_ready"], v_evac=pl.count["v_evac"])
    pl.tick(st, "ytmp_ready", "yhi_ready", "y_ready")
    for k in range(8, 12):
        pl.tile_ready[k] = st.on["y_ready"]
    pl.transposed("h", stm.on["rows_ready"], "side", ROW["o_mem"])
    pl.load("x", rows=pl.count["rt_ps"])
    for c in range(2):
        pl.panel("e_w_out", c * CW, CW, "y", "resid", kts=EVEN_Y // P, c=c)
    assert not pl.later
    if stop == 1:
        pl.step("store")
        return finish(pl)

    st = pl.norm_rows("h", "gates", *pl.residual())
    evs = [pl.panel("o_w_mem_kv", CW, CW, "side", "copy", dst=("g1", 2))]
    pl.transposed("gates", st.on["rows_ready"], "x", ROW["o_norm"])
    evs.append(pl.panel("o_w_mem_kv", 0, CW, "side", "norm", gs=128, dst=("g1", 1)))
    pl.tile_ready = {}
    W = "o_w_in"
    pl.panel(W, 6144, 12, "x", "forget")
    st = pl.step("forget_sum")
    pl.tick(st, "logf_ready", "cum_ps", "cum_sb", "cum_sb2", "cum_out")
    pl.uses(st, "o", "cum_sb2")
    evs.append(pl.panel(W, 6156, CW, "x", "norm", gs=128, dst=("g1", 0)))
    b = heads("X", "g1", evs, pl.pos, 4, 12, gain="ox")
    pl.panel(W, 6668, CW, "x", "gate", "col", tile=12)
    m = pl.pos
    for chunk in range(4):
        m = pl.mod(m, chunk, ctx=True) + 2
    for g in range(3):
        buf = ("g2", "g0", "g1")[g]
        evs = [pl.panel(W, CW * g, CW, "x", "norm", gs=128, dst=(buf, 0)),
               pl.panel(W, 1536 + CW * g, CW, "x", "norm", gs=128, dst=(buf, 1))]
        if g == 2:
            assert not pl.pending["g2"]
            pl.load("ctx", after=pl.count["o_ps"])
            pl.load("rope", after=pl.count["o_ps"])
        evs.append(pl.panel(W, 3072 + CW * g, CW, "x", "copy", dst=(buf, 2)))
        masked = {}

        def make_rows(g=g, masked=masked):
            s = pl.step("forget_rows", g=g, prev=pl.count.get("s_rd", 0))
            pl.tick(s, "rows_in", "mask0", "mask1")
            masked["mask1"] = s.on["mask1"]
        b = max(b, pl.pos)
        pl.at(b - 1, make_rows)
        b = heads("C", buf, evs, b, 4, 4 * g, rows=masked)
        if g == 2:
            st = pl.norm_rows("g2", "g2", ("loaded_ctx", 16))
            pl.step("rope_tables")
        pl.panel(W, 4608 + CW * g, CW, "x", "gate", "col", tile=4 * g)
    assert pl.chunks == [0, 1, 2, 3] and not pl.pending["g0"]
    pl.step("mod_cols", which="mix", mod_sb=pl.count["mod_sb"])
    pl.transposed("g2", st.on["rows_ready"], "side", "ctx_A", "ctx_B")
    pl.load("post_mix", after=pl.count["o_ps"])
    m = pl.pos
    for chunk in range(4, 10):
        m = pl.mod(m, chunk, gate=chunk < 6)
    V = "w_in_2"
    pl.panel(V, 512, 256, "side", "ctxkv")
    pl.panel(V, 1280, CW, "side", "copy", dst=("g2", 0))
    for c in range(2):
        pl.panel("o_w_out", c * CW, CW, "y", "resid", kts=ODD_Y // P, c=c, order=[(12, 16), (0, 12)])
    assert not any(pl.pending.values())
    if stop == 2:
        pl.flush()
        pl.step("store")
        return finish(pl)

    pl.load("ret", after=pl.count["o_ps"])
    st = pl.norm_rows("h", "gates", *pl.residual())
    pl.step("decays")
    pl.panel(V, 1792, CW, "side", "copy", dst=("g2", 1))
    v_evac = pl.count["v_evac"]
    pl.transposed("gates", st.on["rows_ready"], "x", "mix_A", "mix_B")

    def ctx_state():
        st = pl.step("ctx_state", v_evac=v_evac)
        pl.tick(st, "kfb_ready", "state_ps", "state_sb")
        pl.uses(st, "o", "state_sb")
    pl.at(pl.pos + 1, ctx_state)
    pl.tile_ready = {}
    lat = pl.panel(V, 512, 256, "x", "latkv")
    q = pl.panel(V, 0, CW, "x", "normrope")
    st = pl.step("gqa_kT", ready=[("rope_done", lat.on["rope_done"])])
    pl.tick(st, "kT_ps", "kT_sb")
    pl.uses(st, "tp", "kT_sb")
    ready = [("rope_done", q.on["rope_done"]), ("v_evac", lat.on["v_evac"])]
    gqa = []
    for j in range(4):
        for part in range(2):
            hd = part * 4 + j
            gqa.append(Head("G", "g0", j, hd // 2, ready, part=part, base=(hd % 2) * 64, kT_sb=st.on["kT_sb"]))
    pl.grouped(gqa, pl.pos + 1)
    rq = [pl.panel(V, 768, CW, "x", "rope", dst=("g1", 0)),
          pl.panel(V, 1280, CW, "x", "rope", dst=("g1", 1)),
          pl.panel(V, 1792, CW, "x", "copy", dst=("g1", 2))]
    assert not pl.pending["g0"]
    retention(pl, rq, pl.pos)
    pl.panel(V, 2304, CW, "x", "gate", "col", tile=4)
    outs = [pl.panel("w_out_2", c * CW, CW, "y", "mix", kts=MIX_Y // P, c=c, opened=True) for c in range(2)]
    for o in outs:
        pl.parts(o.panel, 0, 4)
    pl.flush()
    for o in outs:
        pl.parts(o.panel, 4, 8)
    assert pl.chunks == list(range(10))
    pl.tile_ready = {}
    st = pl.step("post", which=0, mod_sb=pl.count["mod_sb"])
    pl.tick(st, "sq_ready", "ms_ready", "rstd_ready", "post_done")
    pl.uses(st, "scr", "sq_ready")
    st.v_evac = pl.count["v_evac"]
    if stop == 3:
        pl.step("store")
        return finish(pl)
    pl.load("post_ffn", after=pl.count["o_ps"])
    st = pl.norm_rows("h", "gates", *pl.residual())
    pl.step("mod_cols", which="ffn", mod_sb=pl.count["mod_sb"])
    pl.transposed("gates", st.on["rows_ready"], "x", "ffn_A", "ffn_B")
    pl.mod(pl.mod(pl.pos + 8, 10, gate=True), 11, gate=True)
    for j in range(0, FFN, CW):
        n = min(CW, FFN - j)
        slot = (j // CW) % 2
        a = pl.panel("w_ffn_in", j, n, "x", "ffa", "col", tile=4 * slot)
        pl.panel("w_ffn_in", FFN + j, n, "x", "ffb", "col", gate_tile=4 * slot, gate=a.on["gate_ready"],
                 tiles=list(range(j // P, (j + n) // P)))
    for c in range(2):
        pl.panel("w_ffn_out", c * CW, CW, "y", "mix", kts=FFN // P, c=c)
    st = pl.step("post", which=1, mod_sb=pl.count["mod_sb"])
    pl.tick(st, "sq_ready", "ms_ready", "rstd_ready", "post_done")
    pl.uses(st, "scr", "sq_ready")
    st.v_evac = pl.count["v_evac"]
    pl.step("store")
    return finish(pl)


def retention(pl, rq, pos):
    ready = [("rope_done", rq[1].on["rope_done"]), ("v_evac", rq[2].on["v_evac"])]
    qfb = {}
    decay, score, out = {}, {}, {}

    def ret_q():
        st = pl.step("ret_q", rope_done=pl.count["rope_done"])
        pl.tick(st, "qfb_ready")
        qfb["ready"] = st.on["qfb_ready"]

    def ret_decay(h):
        st = decay[h] = pl.step("ret_decay", h=h)
        st.am_read = score[h - 2].on["am_ready"] if h >= 2 else 0
        pl.tick(st, "m_arg", "m_exp", "m_ready")

    def beside(h):
        if h < 8 and h % 2 == 0:
            a = pl.step("ret_T", h=h, prev_s=pl.count["s_ps"], ready=ready)
            pl.tick(a, "qkT_ps", "qkT_sb")
            pl.uses(a, "tp", "qkT_sb")
            qkT_sb = a.on["qkT_sb"]
            qfb["qkT"] = qkT_sb
        if h > 0:
            o = out[h - 1] = pl.step("ret_pv", h=h - 1, am_ready=score[h - 1].on["am_ready"], qkT_sb=qfb["T2"])
            pl.tick(o, "o_ps", "ret_sb")
            pl.uses(o, "o", "ret_sb")
        if h < 8 and h % 2 == 0:
            a = pl.step("ret_T2", h=h, prev_o=pl.count["o_ps"], qfb=qfb["ready"])
            pl.tick(a, "qkT_ps", "qkT_sb")
            qfb["T2"] = a.on["qkT_sb"]
            pl.uses(a, "tp", "qkT_sb")
        if h < 8:
            prev_o = out[h - 2].on["o_ps"] if h >= 2 else pl.count["o_ps"]
            s = score[h] = pl.step("ret_scores", h=h, prev_o=prev_o, qkT_sb=qfb["qkT"], m_ready=decay[h].on["m_ready"])
            pl.tick(s, "s_ps", "am_ready")
            pl.uses(s, f"s{h % 2}", "am_ready")
        if h + 2 < 8:
            ret_decay(h + 2)

    def ret_norm():
        st = pl.step("ret_norm", ret_sb=pl.count["ret_sb"], gate_ready=pl.count["gate_ready"])
        pl.tick(st, "ret_mid", "sq_ready", "ms_ready", "rstd_ready", "rn_ready", "rt_ps", "ytmp_ready", "yhi_ready",
                "y_ready")
        pl.uses(st, "s0", "ytmp_ready")
        pl.uses(st, "s1", "ytmp_ready")
        pl.uses(st, "scr", "y_ready")
        for k in range(4, 8):
            pl.tile_ready[k] = st.on["y_ready"]
    ret_decay(0)
    ret_decay(1)
    ret_q()
    for h in range(9):
        pl.at(pos + h, lambda h=h: beside(h))
    pl.at(pos + 9, ret_norm)


def finish(pl):
    out = []
    n = len(pl.subs)
    made = 0

    def split():
        nonlocal made
        if made < n:
            out.append(Step("split", sub=pl.subs[made]))
            made += 1
    for st in pl.steps:
        if st.kind == "sub":
            while made <= st.sub.i + LEAD and made < n:
                split()
        if st.kind == "mod" and made < n and pl.subs[made].k0 % RAWK:
            split()
        out.append(st)
        if st.kind == "setup":
            for _ in range(LEAD):
                split()
    raws = []
    for st in out:
        if st.kind == "split":
            sub = st.sub
            if sub.k0 % RAWK == 0:
                nk = min(RAWK, sub.panel.kts - sub.k0)
                raws.append(Load(len(raws), sub.panel.w, sub.k0 * P, nk, sub.panel.col, sub.panel.ncols, None))
                current = raws[-1]
            sub.raw = current
            sub.raw.read = ("lo_ready", sub.i + 1)
            sub.koff = sub.k0 % RAWK
        elif st.kind == "mod":
            st.raw = Load(len(raws), "w_mod", st.u * RAWK * P, RAWK, st.chunk * CW, CW,
                          ("mod_read", st.on["mod_read"]))
            raws.append(st.raw)
    pl.steps, pl.raws = out, raws
    return pl



SEMS = """raw_loaded0 raw_loaded1 raw_loaded2 loaded_first loaded_g0 loaded_h loaded_x loaded_ctx loaded_rope
loaded_ret loaded_post_mix loaded_post_ffn hi_ready lo_ready sub_done mod_read mod_ps mod_sb
sq_ready ms_ready rstd_ready rows_ready rt_ps rt_hi rt_lo rt_tmp qk_evac v_evac tanh_ready gate_ready
conv_u resid_done forget_in rope_done norm_mid ytmp_ready yhi_ready y_ready
qkT_ps qkT_sb s_ps s_rd mx_ready exp_ready p_ready PT_ps PT_sb o_ps on_ready oT_ps
logf_ready logf_e cum_ps cum_sb cum_sb2 cum_out rows_in mask0 mask1
kfb_ready state_ps state_sb kT_ps kT_sb qfb_ready m_arg m_exp m_ready am_ready ret_sb ret_mid rn_ready
post_done cols_ps cols_sb gains_ready lam_in lam_exp tanh_c lg_exp dec_arg dec_exp setup_pool bias_in bias_done logf_a
dve_chain act_chain pool_chain stored""".split()


def program(nc, w, out, stop=None):
    first_c, ret_c, rope_c = constants()
    pl = make_plan(stop)
    ctx = ExitStack()
    with ctx:
        place = [(nc.sbuf_base + 31) // 32 * 32]

        def sb(name, shape, dtype=F32, at=None):
            off = place[0] if at is None else at
            t = nc.alloc_sbuf_tensor_at(name, shape, dtype, offset=off)
            if at is None:
                place[0] += (int(np.prod(shape[1:])) * 4 + 31) // 32 * 32
            return t

        raw = sb("raw", [P, RAW_SLOTS, RAWK, CW])
        whi = sb("whi", [P, SPLIT_SLOTS, SUBK, CW], F32R)
        wlo = sb("wlo", [P, SPLIT_SLOTS, SUBK, CW], F32R)
        xhi, xlo = (sb(n, [P, KT, T], F32R) for n in ("xhi", "xlo"))
        shi, slo = (sb(n, [P, KT, T], F32R) for n in ("shi", "slo"))
        yhi, ylo = (sb(n, [P, 16, T], F32R) for n in ("yhi", "ylo"))
        g2_at = place[0]
        g2 = sb("g2", [P, 3072])
        zhi = sb("zhi", [P, 6, T], F32R, at=g2_at)
        zlo = sb("zlo", [P, 6, T], F32R, at=g2_at + 6 * T * 4)
        g0, g1 = sb("g0", [P, 3072]), sb("g1", [P, 3072])
        gates = sb("gates", [P, 16, T])
        h_res = sb("h_res", [P, NT, D])
        pbuf = sb("pbuf", [P, 768])
        ptb = sb("ptb", [P, 512])
        qkT = sb("qkT", [P, 2, T])
        ytmp = sb("ytmp", [P, T])
        scr = sb("scr", [P, 1024])
        macc = sb("macc", [P, 2, CW])
        nc_at = place[0]
        negcum = sb("negcum", [P, 4, T])
        negcum0 = sb("negcum0", [P, 4, P])
        rett = sb("rett", [P, 3, 512], at=nc_at)
        ytok = sb("ytok", [P, T], at=nc_at)
        nfirst = first_c.shape[1]
        cst = sb("cst", [P, nfirst])
        rows1, rows2 = macc[:, 0, 0:P], macc[0:16, 0, P:2 * P]
        cols = sb("cols", [P, P + 16])
        gain = {n: sb("gain_" + n, [P, 1]) for n in ("A", "ex", "C", "ox", "aon")}
        neglam = sb("neglam", [P, 1])
        scol = sb("scol", [P, 16])
        modc = sb("modc", [P, 2, 48])
        mcol = {n: sb("mc_" + n, [P, 8]) for n in ("mix_A", "ctx_A", "ffn_A")}
        small = sb("small", [P, 6, 16])
        half_neg = sb("half_neg", [P, 16])
        nmx, rsum, rinv = sb("nmx", [P, 4]), sb("rsum", [P, 4]), sb("rinv", [P, 4])
        fbb = sb("fbb", [P, 12])
        fx, fe, logf = sb("fx", [P, NT, 12]), sb("fe", [P, NT, 12]), sb("logf", [P, NT, 12])
        cumq = sb("cumq", [P, NT, 12])
        cumT = macc[0:12, 1, 0:T]
        lg = sb("lg", [P, 16])
        dec = sb("dec", [P, 4, NT, 8])
        assert place[0] <= nc.sbuf_usable_end, place[0] - nc.sbuf_usable_end
        scratch = nc.dram_tensor("cum_scratch", (12, T), F32, kind="Internal").ap()

        groups = {"g0": g0, "g1": g1, "g2": g2}

        def grp(name, part):
            return groups[name][:, part * 1024:(part + 1) * 1024]

        def const(name, a=0, b=None):
            at, n = CONST[name]
            return cst[:, at + a:at + (n if b is None else b)]

        ident = const("ident")
        ones = const("tri", P, 2 * P)
        gflat = gates[:, :, :].rearrange("p k t -> p (k t)")
        rows_of = {"g0": g0[:, 0:2048].rearrange("p (t d) -> p t d", t=NT), "h": h_res[:, :, :],
                   "g2": g2[:, 0:2048].rearrange("p (t d) -> p t d", t=NT),
                   "gates": gflat[:, 0:2048].rearrange("p (t d) -> p t d", t=NT)}
        p2 = gflat[:, 2048:3072].rearrange("p (t k) -> p t k", t=NT)
        pt2 = gflat[:, 3072:4096].rearrange("p (k t) -> p k t", t=T)
        kfb = gflat[:, 2048:4096].rearrange("p (t h f d) -> p t h f d", t=NT, h=8, f=2)
        dmat = gflat[:, 0:1024].rearrange("p (s n) -> p s n", s=2)
        qfb = g2[:, 0:2048].rearrange("p (t h f d) -> p t h f d", t=NT, h=8, f=2)
        ropes = {n: g2[:, 2048 + 256 * i:2304 + 256 * i].rearrange("p (c t d) -> p c t d", c=2, t=NT)
                 for i, n in enumerate(("ret", "q", "k"))}
        growb = g2[:, 2816:2944]
        kT2 = ptb
        sfb = pbuf[:, 0:512].rearrange("p (h d) -> p h d", h=8)
        qfbT = gflat[:, 2048:2560].rearrange("p (h t) -> p h t", h=2)
        am = gflat[:, 3072:4096].rearrange("p (s n) -> p s n", s=2)
        ret = g0[:, 0:1024].rearrange("p (t n) -> p t n", t=NT)
        lat_k, lat_v = (g0[:, 1024 + 256 * i:1280 + 256 * i].rearrange("p (t d) -> p t d", t=NT) for i in (0, 1))
        ctx_k, ctx_v = (g0[:, 1536 + 256 * i:1792 + 256 * i].rearrange("p (t d) -> p t d", t=NT) for i in (0, 1))
        mixed = g0[:, 0:2048].rearrange("p (t d) -> p t d", t=NT)
        post_gain = (g0[:, 2048:3072], g1[:, 0:1024])

        acc = ctx.enter_context(nc.psum_tensor("acc", [P, 4, CW], F32))
        spsum = ctx.enter_context(nc.psum_tensor("spsum", [P, 2, CW], F32))
        tp = ctx.enter_context(nc.psum_tensor("tp", [P, CW], F32))
        opsum = ctx.enter_context(nc.psum_tensor("opsum", [P, CW], F32))
        S = {n: ctx.enter_context(nc.semaphore(n)) for n in SEMS}

        spt = spsum[:, :, :].rearrange("p b (c t) -> p (b c) t", t=T)

        def acc2(a, n=CW):
            return acc[:, 2 * a:2 * a + 2, 0:n]

        def acct(a, n=4):
            return acc[:, 2 * a:2 * a + 2, :].rearrange("p b (c t) -> p (b c) t", t=T)[:, 0:n, :]

        def operand(src, k):
            if src == "x":
                return xhi[:, k, :], xlo[:, k, :]
            if src == "side":
                return shi[:, k, :], slo[:, k, :]
            return (yhi[:, k, :], ylo[:, k, :]) if k < 16 else (zhi[:, k - 16, :], zlo[:, k - 16, :])

        def y_part(k0, n, lo, p0=0, p1=P):
            t = ((yhi, zhi), (ylo, zlo))[lo][k0 >= 16]
            return t[p0:p1, k0 % 16:k0 % 16 + n, :]

        def scale_cols(key):
            if isinstance(key, int):
                return cols[:, key:key + 8]
            return {"mix_A": mcol["mix_A"][:, :], "ctx_A": mcol["ctx_A"][:, :], "ffn_A": mcol["ffn_A"][:, :],
                    "mix_B": modc[:, 0, 0:8], "ctx_B": modc[:, 1, 0:8], "ffn_B": modc[:, 0, 24:32]}[key]

        def heads_of(ap, n, d):
            return ap.rearrange("p (h d) -> p h d", h=n)

        def across(ap, shape):
            return ap.unsqueeze(len(shape) - 1).to_broadcast(shape)

        block = ctx.enter_context(nc.Block())

        @block.sync
        def _(sp):
            sp.dma_start(rows_of["g0"], w["x"].rearrange("b (t p) d -> p (b t) d", p=P)).then_inc(S["loaded_g0"], 16)
            sp.dma_start(cst[:, :], w["const_first"]).then_inc(S["loaded_first"], 16)
            for name, r in (("e_norm_g", "e_norm"), ("e_mem_norm_g", "e_mem"), ("o_norm_g", "o_norm"),
                            ("o_mem_norm_g", "o_mem"), ("g_pre_mix_2", "pre_mix"), ("g_pre_ffn_2", "pre_ffn"),
                            ("b_mod_2", "b_mod"), ("c_2", "c"), ("e_b_conv_b", "conv_b")):
                n = w[name].shape[1] // P
                sp.dma_start(macc[ROW[r]:ROW[r] + n, 0, 0:P], w[name].rearrange("a (r c) -> (a r) c", c=P))\
                    .then_inc(S["loaded_first"], 16)
            sp.dma_start(macc[ROW["c_ctx"]:ROW["c_ctx"] + 8, 0, 0:P], w["c_ctx_2"].rearrange("(r c) -> r c", c=P))\
                .then_inc(S["loaded_first"], 16)
            sp.dma_start(macc[ROW["conv_w"]:ROW["conv_w"] + 12, 0, 0:P],
                         w["e_b_conv_w"].rearrange("a k (r c) -> (a k r) c", c=P)).then_inc(S["loaded_first"], 16)
            for name, r, n in (("e_a_q_norm_g", "aq", 64), ("e_a_k_norm_g", "ak", 64), ("e_a_out_norm_g", "aon", P),
                               ("e_x_q_norm_g", "exq", P), ("e_x_k_norm_g", "exk", P), ("o_c_q_norm_g", "cq", P),
                               ("o_c_k_norm_g", "ck", P), ("o_x_q_norm_g", "oxq", P), ("o_x_k_norm_g", "oxk", P)):
                for a in range(0, P, n):
                    sp.dma_start(macc[ROW2[r]:ROW2[r] + 1, 0, P + a:P + a + n], w[name]).then_inc(S["loaded_first"], 16)
            sp.dma_start(macc[9:16, 0, P:2 * P], w["e_norm_g"][:, 0:7 * P].rearrange("a (r c) -> (a r) c", c=P))\
                .then_inc(S["loaded_first"], 16)
            sp.dma_start(scr[:, 0:256], w["e_a_lambda"].rearrange("a r c -> a (r c)").to_broadcast([P, 256]))\
                .then_inc(S["loaded_first"], 16)
            sp.dma_start(fbb[:, :], w["o_c_forget_b"].to_broadcast([P, 12])).then_inc(S["loaded_first"], 16)
            sp.dma_start(lg[:, 0:8], w["ret_decay_fwd_2"].to_broadcast([P, 8])).then_inc(S["loaded_first"], 16)
            sp.dma_start(lg[:, 8:16], w["ret_decay_bwd_2"].to_broadcast([P, 8])).then_inc(S["loaded_first"], 16)
            sp.dma_start(h_res[:, :, :], w["mem"].rearrange("b (t p) d -> p (b t) d", p=P)).then_inc(S["loaded_h"], 16)
            for r in pl.raws:
                if r.i >= RAW_SLOTS:
                    sem, n = pl.raws[r.i - RAW_SLOTS].read
                    sp.wait_ge(S[sem], n)
                src = w[r.w][r.row:r.row + r.nk * P, r.col:r.col + r.ncols].rearrange("(k p) n -> p k n", p=P)
                sp.dma_start(raw[:, r.i % RAW_SLOTS, 0:r.nk, 0:r.ncols], src)\
                    .then_inc(S[f"raw_loaded{r.i % RAW_SLOTS}"], 16)
            sp.wait_ge(S["resid_done" if stop in (1, 2) else "post_done"],
                       pl.count["resid_done" if stop in (1, 2) else "post_done"])
            sp.dma_start(out.rearrange("b (t p) d -> p (b t) d", p=P), h_res[:, :, :]).then_inc(S["stored"], 16)
            sp.wait_ge(S["stored"], 16)

        n_first = 16 * (1 + 9 + 1 + 1 + (2 + 2 + 7) + 1 + 1 + 1 + 2)

        def raw_wait(eng, r):
            eng.wait_ge(S[f"raw_loaded{r.i % RAW_SLOTS}"], 16 * (r.i // RAW_SLOTS + 1))

        @block.tensor
        def _(pe):
            mm, tr = nc.tensor.matmul, nc.tensor.transpose

            def wait(pair):
                if pair:
                    pe.wait_ge(S[pair[0]], pair[1])

            def sub(st):
                s, pan = st.sub, st.sub.panel
                for pair in s.waits:
                    wait(pair)
                pe.wait_ge(S["lo_ready"], s.i + 1)
                slot = s.i % SPLIT_SLOTS
                last = None
                if pan.orient == "tok":
                    for t in range(NT):
                        o = acc[:, 2 * pan.acc + t, 0:pan.ncols]
                        for k in range(s.nk):
                            hi, lo = operand(pan.src, s.k0 + k)
                            a, z = s.first and k == 0, s.last and k == s.nk - 1
                            hi, lo = hi[:, t * P:(t + 1) * P], lo[:, t * P:(t + 1) * P]
                            mm(o, hi, whi[:, slot, k, 0:pan.ncols], start=a, stop=False)
                            mm(o, hi, wlo[:, slot, k, 0:pan.ncols], start=False, stop=False)
                            last = mm(o, lo, whi[:, slot, k, 0:pan.ncols], start=False, stop=z)
                else:
                    for c in range(pan.ncols // P):
                        o = acct(pan.acc)[:, c, :]
                        for k in range(s.nk):
                            hi, lo = operand(pan.src, s.k0 + k)
                            a, z = s.first and k == 0 and c % 2 == 0, s.last and k == s.nk - 1
                            wh, wl = (t[:, slot, k, c * P:(c + 1) * P] for t in (whi, wlo))
                            mm(o, wh, hi, start=a, stop=False, skip_group_check=True)
                            mm(o, wl, hi, start=False, stop=False, skip_group_check=True)
                            last = mm(o, wh, lo, start=False, stop=z, skip_group_check=True)
                last.then_inc(S["sub_done"], 1)

            def setup(st):
                pe.wait_ge(S["loaded_first"], n_first)
                tr(tp[:, 0:P], rows1, ident)
                mm(tp[:, P:P + 16], rows2, ident[0:16, 0:16], is_transpose=True).then_inc(S["cols_ps"], 1)

            def rows_T(st):
                wait(st.free["acc"])
                pe.wait_ge(S["rows_ready"], st.ready)
                for k in range(4):
                    for t in range(NT):
                        kk = 4 * st.half + k
                        last = tr(acct(st.acc)[:, k, t * P:(t + 1) * P],
                                  rows_of[st.xn][:, t, kk * P:(kk + 1) * P], ident)
                last.then_inc(S["rt_ps"], 1)

            def qkT_(st):
                h = st.h
                wait(st.free["tp"])
                for pair in h.ready:
                    wait(pair)
                q, k = (grp(h.g, i).rearrange("p (t n) -> p t n", t=NT) for i in (0, 1))
                for t in range(NT):
                    last = tr(tp[:, t * P:(t + 1) * P], q[:, t, h.j * P:(h.j + 1) * P], ident)
                if h.type != "G":
                    for t in range(NT):
                        last = tr(tp[:, T + t * P:T + (t + 1) * P], k[:, t, h.j * P:(h.j + 1) * P], ident)
                last.then_inc(S["qkT_ps"], 1)

            def scores(st):
                h = st.h
                pe.wait_ge(S["qkT_sb"], st.qkT_sb)
                for b in h.banks:
                    wait(st.free[b])
                if h.type in "AC":
                    for half in range(2 if h.type == "A" else 1):
                        p0, p1 = (half * 64, half * 64 + 64) if h.type == "A" else (0, P)
                        bank = spsum[:, half if h.type == "A" else h.n % 2, :]
                        q, k = qkT[p0:p1, 0, :], qkT[p0:p1, 1, :]
                        mm(bank[:, 0:P], q[:, 0:P], k[:, 0:P], start=True, stop=True)
                        last = mm(bank[:, P:P + T], q[:, P:T], k, start=True, stop=True)
                elif h.type == "X":
                    for t in range(NT):
                        last = mm(spsum[:, h.n % 2, t * T:(t + 1) * T], qkT[:, 0, t * P:(t + 1) * P], qkT[:, 1, :],
                                  start=True, stop=True)
                else:
                    p0 = h.part * 64
                    pe.wait_ge(S["kT_sb"], h.kT_sb)
                    for t in range(NT):
                        last = mm(spsum[:, t, :], qkT[p0:p0 + 64, 0, t * P:(t + 1) * P], kT2[p0:p0 + 64, :],
                                  start=True, stop=True)
                last.then_inc(S["s_ps"], 1)

            def PT(st):
                h = st.h
                pe.wait_ge(S["p_ready"], st.p_ready)
                wait(st.free["tp"])
                if h.type in "AC":
                    blocks = [pbuf[:, 0:P], pbuf[:, P:2 * P], pbuf[:, 2 * P:3 * P]]
                elif h.type == "X":
                    blocks = [pbuf[:, t * T + k * P:t * T + (k + 1) * P] for k in range(2) for t in range(NT)]
                else:
                    blocks = [p2[:, t, k * P:(k + 1) * P] for k in (2 * st.part, 2 * st.part + 1) for t in range(NT)]
                for i, b in enumerate(blocks):
                    last = tr(tp[:, i * P:(i + 1) * P], b, ident)
                last.then_inc(S["PT_ps"], 1)

            def pv(st):
                h = st.h
                pe.wait_ge(S["PT_sb"], st.PT_sb)
                wait(st.free["o"])
                for pair in h.ready:
                    wait(pair)
                if h.type == "G":
                    for k in range(4):
                        v = (ctx_v, lat_v)[k // 2][:, k % 2, h.part * 64:h.part * 64 + 64]
                        last = mm(opsum[h.base:h.base + 64, 0:T], v, pt2[:, k, :], start=k == 0, stop=k == 3)
                else:
                    v = grp(h.g, 2).rearrange("p (t n) -> p t n", t=NT)[:, :, h.j * P:(h.j + 1) * P]
                    if h.type == "A":
                        mm(opsum[:, 0:P], ptb[:, 0:P], v[:, 0, :], start=True, stop=True)
                        mm(opsum[:, P:T], ptb[:, P:T], v[:, 0, :], start=True, stop=False)
                        last = mm(opsum[:, P:T], ptb[:, T:T + P], v[:, 1, :], start=False, stop=True)
                    elif h.type == "C":
                        mm(opsum[:, 0:P], v[:, 0, :], ptb[:, 0:P], start=True, stop=True)
                        mm(opsum[:, P:T], v[:, 0, :], ptb[:, P:T], start=True, stop=False)
                        last = mm(opsum[:, P:T], v[:, 1, :], ptb[:, T:T + P], start=False, stop=True)
                    else:
                        mm(opsum[:, 0:T], v[:, 0, :], ptb[:, 0:T], start=True, stop=False)
                        last = mm(opsum[:, 0:T], v[:, 1, :], ptb[:, T:2 * T], start=False, stop=True)
                last.then_inc(S["o_ps"], 1)

            def oT(st):
                pe.wait_ge(S["on_ready"], st.on_ready)
                wait(st.free["tp"])
                tr(tp[:, 0:P], ytok[:, 0:P], ident)
                tr(tp[:, P:T], ytok[:, P:T], ident).then_inc(S["oT_ps"], 1)

            def mod_out(st):
                pe.wait_ge(S["mod_read"], st.mod_read)
                wait(st.free["tp"])
                if st.gate:
                    pe.wait_ge(S["bias_done"], st.bias_done)
                    mm(tp[:, :], ones, macc[:, 0, :], start=True, stop=True).then_inc(S["mod_ps"], 1)
                    return
                for v in range(2 if st.ctx else 1):
                    for i in range(4):
                        last = mm(tp[:, v * 4 + i:v * 4 + i + 1], macc[:, v, i * P:(i + 1) * P], ones[:, 0:1],
                                  start=True, stop=True)
                last.then_inc(S["mod_ps"], 1)

            def forget_sum(st):
                pe.wait_ge(S["logf_ready"], st.on["logf_ready"])
                wait(st.free["o"])
                tri, f0, f1 = const("tri"), logf[:, 0, :], logf[:, 1, :]
                mm(opsum[:, 0:12], tri[:, 0:P], f0, start=True, stop=True)
                mm(opsum[:, 12:24], ones, f0, start=True, stop=False)
                mm(opsum[:, 12:24], tri[:, 0:P], f1, start=False, stop=True)
                mm(opsum[0:12, 64:64 + T], f0, tri, start=True, stop=False, skip_group_check=True)
                mm(opsum[0:12, 64 + P:64 + T], f1, tri[:, 0:P], start=False, stop=True, skip_group_check=True)\
                    .then_inc(S["cum_ps"], 1)

            def ctx_state(st):
                pe.wait_ge(S["kfb_ready"], st.on["kfb_ready"])
                wait(st.free["o"])
                v = grp("g2", 1).rearrange("p (t n) -> p t n", t=NT)
                for h in range(8):
                    for t in range(NT):
                        last = mm(opsum[:, h * 64:(h + 1) * 64], kfb[:, t, h, :, :], v[:, t, h * 64:(h + 1) * 64],
                                  start=t == 0, stop=t == NT - 1)
                last.then_inc(S["state_ps"], 1)

            def gqa_kT(st):
                for pair in st.ready:
                    wait(pair)
                wait(st.free["tp"])
                for i, k in enumerate((ctx_k[:, 0, :], ctx_k[:, 1, :], lat_k[:, 0, :], lat_k[:, 1, :])):
                    last = tr(tp[:, i * P:(i + 1) * P], k, ident)
                last.then_inc(S["kT_ps"], 1)

            def ret_T(st):
                wait(st.free["tp"])
                for pair in st.ready:
                    wait(pair)
                for i in (0, 1):
                    src = grp("g1", i).rearrange("p (t n) -> p t n", t=NT)
                    for t in range(NT):
                        last = tr(tp[:, i * T + t * P:i * T + (t + 1) * P], src[:, t, st.h * 64:st.h * 64 + P], ident)
                last.then_inc(S["qkT_ps"], 1)

            def ret_T2(st):
                wait(st.free["tp"])
                pe.wait_ge(S["qfb_ready"], st.qfb)
                for i in (0, 1):
                    for t in range(NT):
                        last = tr(tp[:, i * T + t * P:i * T + (t + 1) * P], qfb[:, t, st.h + i, :, :], ident)
                last.then_inc(S["qkT_ps"], 1)

            def ret_scores(st):
                pe.wait_ge(S["qkT_sb"], st.qkT_sb)
                wait(st.free[f"s{st.h % 2}"])
                p0 = (st.h % 2) * 64
                for j in range(NT):
                    last = mm(spsum[:, st.h % 2, j * T:(j + 1) * T], qkT[p0:p0 + 64, 1, j * P:(j + 1) * P],
                              qkT[p0:p0 + 64, 0, :], start=True, stop=True)
                last.then_inc(S["s_ps"], 1)

            def ret_pv(st):
                pe.wait_ge(S["am_ready"], st.am_ready)
                pe.wait_ge(S["qkT_sb"], st.qkT_sb)
                wait(st.free["o"])
                v = grp("g1", 2).rearrange("p (t n) -> p t n", t=NT)[:, :, st.h * 64:(st.h + 1) * 64]
                for i in range(NT):
                    o = opsum[:, i * 64:(i + 1) * 64]
                    for j in range(NT):
                        mm(o, am[:, st.h % 2, j * T + i * P:j * T + (i + 1) * P], v[:, j, :], start=j == 0, stop=False)
                    last = mm(o, qfbT[:, st.h % 2, i * P:(i + 1) * P], sfb[:, st.h, :], start=False, stop=True)
                last.then_inc(S["o_ps"], 1)

            def ret_norm(st):
                pe.wait_ge(S["rn_ready"], st.on["rn_ready"])
                wait(st.free["s0"])
                wait(st.free["s1"])
                for k in range(4):
                    for t in range(NT):
                        last = tr(spt[:, k, t * P:(t + 1) * P], ret[:, t, k * P:(k + 1) * P], ident)
                last.then_inc(S["rt_ps"], 1)

            does = {"sub": sub, "setup": setup, "rows_T": rows_T, "qkT": qkT_, "scores": scores, "PT": PT, "pv": pv,
                    "oT": oT, "mod_out": mod_out, "forget_sum": forget_sum, "ctx_state": ctx_state,
                    "gqa_kT": gqa_kT, "ret_T": ret_T, "ret_T2": ret_T2, "ret_scores": ret_scores, "ret_pv": ret_pv,
                    "ret_norm": ret_norm}
            for st in pl.steps:
                if st.kind in does:
                    does[st.kind](st)

        @block.scalar
        def _(act):
            f = nc.scalar.activation
            chain = [0]

            def wait(pair):
                if pair and pair[1] > 0:
                    act.wait_ge(S[pair[0]], pair[1])

            def link(ins):
                chain[0] += 1
                ins.then_inc(S["act_chain"], 1)
                act.wait_ge(S["act_chain"], chain[0])

            def raises(ins, st, name):
                ins.then_inc(S[name], 1)

            def stat(st, i):
                return small[:, 3 * (st.on["sq_ready"] % 2) + i, :]

            def before_squares(st):
                wait(("ms_ready", st.on["sq_ready"] - 1))
                wait(st.free["scr"])

            def squares(st, parts):
                for t, x in enumerate(parts):
                    ins = f(scr[:, 0:x.shape[1]], x, ACT.Square, accum_out=stat(st, 0)[:, t:t + 1])
                    if t + 1 < len(parts):
                        link(ins)
                ins.then_inc(S["sq_ready"], 1)

            def setup(st):
                act.wait_ge(S["lam_in"], 1)
                f(small[:, 2, 14:16], small[:, 2, 12:14], ACT.Exp).then_inc(S["lam_exp"], 1)
                act.wait_ge(S["cols_sb"], 1)
                f(scol[:, :], cols[:, ROW["c"]:ROW["c"] + 16], ACT.Tanh, scale=0.5).then_inc(S["tanh_c"], 1)
                act.wait_ge(S["gains_ready"], 1)

            def split(st):
                s = st.sub
                raw_wait(act, s.raw)
                if s.i >= SPLIT_SLOTS:
                    act.wait_ge(S["sub_done"], s.i - SPLIT_SLOTS + 1)
                n = s.panel.ncols
                nc.scalar.copy(whi[:, s.i % SPLIT_SLOTS, 0:s.nk, 0:n],
                               raw[:, s.raw.i % RAW_SLOTS, s.koff:s.koff + s.nk, 0:n]).then_inc(S["hi_ready"], 1)

            def rows_norm(st):
                for pair in st.waits:
                    wait(pair)
                before_squares(st)
                squares(st, [rows_of[st.src][:, t, :] for t in range(NT)])

            def rows_T(st):
                hi = (xhi if st.key == "x" else shi)[:, 4 * st.half:4 * st.half + 4, :]
                if st.bias is None:
                    wait(("rt_ps", st.on["rt_ps"]))
                    c = scale_cols(st.scale)
                    for k in range(4):
                        last = f(hi[:, k, :], acct(st.acc)[:, k, :], ACT.Copy,
                                 scale=c[:, 4 * st.half + k:4 * st.half + k + 1])
                else:
                    wait(("rt_tmp", st.on["rt_tmp"]))
                    last = nc.scalar.copy(hi, scr[:, :].rearrange("p (k t) -> p k t", t=T))
                last.then_inc(S["rt_hi"], 1)

            def evac_norm(st):
                act.wait_ge(S["sub_done"], st.done)
                before_squares(st)
                f(scr[:, :].rearrange("p (t n) -> p t n", t=NT), acc2(st.acc), ACT.Square).then_inc(S["sq_ready"], 1)

            def evac_copy(st):
                act.wait_ge(S["sub_done"], st.done)
                nc.scalar.copy(grp(*st.dst).rearrange("p (t n) -> p t n", t=NT), acc2(st.acc)).then_inc(S["v_evac"], 1)

            def evac_gate(st):
                act.wait_ge(S["sub_done"], st.done)
                n = st.panel.ncols // P
                f(gates[:, st.tile:st.tile + n, :], acct(st.acc, n), ACT.Tanh, scale=0.5).then_inc(S["tanh_ready"], 1)

            def evac_conv_h(st):
                act.wait_ge(S["sub_done"], st.done)
                nc.scalar.copy(g2[:, 0:1024].rearrange("p (c t) -> p c t", t=T), acct(st.acc)).then_inc(S["v_evac"], 1)

            def evac_conv_b(st):
                act.wait_ge(S["sub_done"], st.done)
                nc.scalar.copy(g2[:, 1024:2048].rearrange("p (c t) -> p c t", t=T), acct(st.acc))\
                    .then_inc(S["v_evac"], 1)

            def conv(st):
                wait(("ytmp_ready", st.on["ytmp_ready"]))
                nc.scalar.copy(yhi[:, 8:12, :], g2[:, 2048:3072].rearrange("p (c t) -> p c t", t=T))\
                    .then_inc(S["yhi_ready"], 1)

            def forget_sum(st):
                wait(("logf_a", 1))
                link(f(fe[:, :, :], fe[:, :, :], ACT.Exp))
                f(fe[:, :, :], fe[:, :, :], ACT.Ln, bias=1.0).then_inc(S["logf_e"], 1)
                wait(("cum_sb", 1))
                nc.scalar.mul(cumT, opsum[0:12, 64:64 + T], -1.0).then_inc(S["cum_sb2"], 1)

            def qkT_(st):
                h = st.h
                wait(("qkT_ps", st.on["qkT_ps"]))
                wait(("s_ps", st.prev_s))
                if h.type == "G":
                    f(qkT[:, 0, :], tp[:, 0:T], ACT.Copy, scale=0.125).then_inc(S["qkT_sb"], 1)
                    return
                g = gain[h.gain if h.type == "X" else h.type]
                f(qkT[:, 0, :], tp[:, 0:T], ACT.Copy, scale=g[:, :])
                f(qkT[:, 1, :], tp[:, T:2 * T], ACT.Copy).then_inc(S["qkT_sb"], 1)

            def scores(st):
                h = st.h
                wait(("mx_ready", st.on["mx_ready"]))
                if h.type in "AC":
                    for half in range(2 if h.type == "A" else 1):
                        for t in range(NT):
                            i = half * 2 + t
                            a = half * 384 + t * P
                            p = pbuf[:, a:a + P + t * P]
                            last = f(p, p, ACT.Exp, bias=nmx[:, i:i + 1], accum_out=rsum[:, i:i + 1])
                else:
                    wait(("PT_ps", st.prev_pt))
                    for t in range(NT):
                        src, dst = (spsum[:, h.n % 2, t * T:(t + 1) * T], pbuf[:, t * T:(t + 1) * T]) \
                            if h.type == "X" else (spsum[:, t, :], p2[:, t, :])
                        last = f(dst, src, ACT.Exp, bias=nmx[:, t:t + 1], accum_out=rsum[:, t:t + 1])
                last.then_inc(S["exp_ready"], 1)

            def PT(st):
                wait(("PT_ps", st.on["PT_ps"]))
                wait(("o_ps", st.prev_o))
                if st.h.type == "G":
                    dst, n = pt2[:, 2 * st.part:2 * st.part + 2, :], 512
                    nc.scalar.copy(dst, tp[:, :].rearrange("p (k t) -> p k t", t=T)).then_inc(S["PT_sb"], 1)
                    return
                n = 384 if st.h.type in "AC" else 512
                nc.scalar.copy(ptb[:, 0:n], tp[:, 0:n]).then_inc(S["PT_sb"], 1)

            def pv(st):
                h = st.h
                if h.type == "A":
                    before_squares(st)
                    wait(("o_ps", st.on["o_ps"]))
                    squares(st, [opsum[:, t * P:(t + 1) * P] for t in range(NT)])
                elif h.type == "G":
                    wait(("o_ps", st.on["o_ps"]))
                    b = h.base
                    nc.scalar.copy(yhi[b:b + 64, h.tile, :], opsum[b:b + 64, 0:T]).then_inc(S["yhi_ready"], 1)
                else:
                    wait(("ytmp_ready", st.on["ytmp_ready"]))
                    nc.scalar.copy(yhi[:, h.tile, :], ytmp[:, :]).then_inc(S["yhi_ready"], 1)

            def oT(st):
                wait(("ytmp_ready", st.on["ytmp_ready"]))
                nc.scalar.copy(yhi[:, st.h.tile, :], ytmp[:, :]).then_inc(S["yhi_ready"], 1)

            def decays(st):
                link(f(lg[:, :], lg[:, :], ACT.Exp))
                nc.scalar.mul(lg[:, :], lg[:, :], -1.0).then_inc(S["lg_exp"], 1)
                wait(("dec_arg", 1))
                d = dec[:, :, :, :].rearrange("p e t h -> p (e t h)")
                f(d, d, ACT.Exp).then_inc(S["dec_exp"], 1)

            def ctx_state(st):
                wait(("state_ps", 1))
                nc.scalar.mul(sfb, opsum[:, :].rearrange("p (h d) -> p h d", h=8), 0.125).then_inc(S["state_sb"], 1)

            def evac_kv(st):
                act.wait_ge(S["sub_done"], st.done)
                before_squares(st)
                f(scr[:, 0:256].rearrange("p (t n) -> p t n", t=NT), acc2(st.acc, P), ACT.Square)\
                    .then_inc(S["sq_ready"], 1)
                wait(("norm_mid", st.on["norm_mid"]))
                nc.scalar.copy(ctx_v if st.kind == "evac_ctxkv" else lat_v, acc2(st.acc, 2 * P)[:, :, P:2 * P])\
                    .then_inc(S["v_evac"], 1)

            def gqa_kT(st):
                wait(("kT_ps", 1))
                nc.scalar.copy(kT2[:, :], tp[:, :]).then_inc(S["kT_sb"], 1)

            def ret_T(st):
                wait(("qkT_ps", st.on["qkT_ps"]))
                wait(("s_ps", st.prev_s))
                nc.scalar.copy(qkT[:, :, :], tp[:, :].rearrange("p (a t) -> p a t", t=T)).then_inc(S["qkT_sb"], 1)

            def ret_T2(st):
                wait(("qkT_ps", st.on["qkT_ps"]))
                wait(("o_ps", st.prev_o))
                nc.scalar.copy(qfbT, tp[:, :].rearrange("p (a t) -> p a t", t=T)).then_inc(S["qkT_sb"], 1)

            def ret_decay(st):
                wait(("m_arg", st.on["m_arg"]))
                f(dmat[:, st.h % 2, :], dmat[:, st.h % 2, :], ACT.Exp).then_inc(S["m_exp"], 1)

            def ret_pv(st):
                wait(("o_ps", st.on["o_ps"]))
                nc.scalar.copy(ret[:, :, st.h * 64:(st.h + 1) * 64], opsum[:, 0:P].rearrange("p (t d) -> p t d", t=NT))\
                    .then_inc(S["ret_sb"], 1)

            def ret_norm(st):
                wait(("ret_mid", 1))
                before_squares(st)
                f(scr[:, :], g0[:, 0:1024], ACT.Square).then_inc(S["sq_ready"], 1)
                wait(("ytmp_ready", st.on["ytmp_ready"]))
                nc.scalar.copy(yhi[:, 4:8, :], scr[:, :].rearrange("p (k t) -> p k t", t=T))\
                    .then_inc(S["yhi_ready"], 1)

            def evac_mix(st):
                act.wait_ge(S["sub_done"], st.done)
                nc.scalar.copy(mixed[:, :, st.c * CW:(st.c + 1) * CW], acc2(st.acc)).then_inc(S["v_evac"], 1)

            def post(st):
                before_squares(st)
                wait(("v_evac", st.v_evac))
                squares(st, [mixed[:, t, :] for t in range(NT)])

            def evac_ffb(st):
                wait(("ytmp_ready", st.on["ytmp_ready"]))
                n = len(st.tiles)
                nc.scalar.copy(y_part(st.tiles[0], n, 0), scr[:, 0:n * T].rearrange("p (k t) -> p k t", t=T))\
                    .then_inc(S["yhi_ready"], 1)

            does = {"setup": setup, "split": split, "rows_norm": rows_norm, "rows_T": rows_T, "evac_norm": evac_norm,
                    "evac_normrope": evac_norm, "evac_copy": evac_copy, "evac_gate": evac_gate,
                    "evac_conv_z": evac_gate, "evac_ffa": evac_gate, "evac_conv_h": evac_conv_h,
                    "evac_conv_b": evac_conv_b, "conv": conv, "forget_sum": forget_sum, "qkT": qkT_,
                    "scores": scores, "PT": PT, "pv": pv, "oT": oT, "decays": decays, "ctx_state": ctx_state,
                    "evac_ctxkv": evac_kv, "evac_latkv": evac_kv, "gqa_kT": gqa_kT, "ret_T": ret_T,
                    "ret_T2": ret_T2, "ret_decay": ret_decay, "ret_pv": ret_pv, "ret_norm": ret_norm,
                    "evac_mix": evac_mix, "post": post, "evac_ffb": evac_ffb}
            for st in pl.steps:
                if st.kind in does:
                    does[st.kind](st)

        @block.vector
        def _(dve):
            tt, ts, stt = nc.vector.tensor_tensor, nc.vector.tensor_scalar, nc.vector.scalar_tensor_tensor
            chain = [0]

            def wait(pair):
                if pair and pair[1] > 0:
                    dve.wait_ge(S[pair[0]], pair[1])

            def link(ins):
                chain[0] += 1
                ins.then_inc(S["dve_chain"], 1)
                dve.wait_ge(S["dve_chain"], chain[0])

            def stat(st, i):
                return small[:, 3 * (st.on["sq_ready"] % 2) + i, :]

            def mean_rstd(st, n, size):
                ts(stat(st, 1)[:, 0:n], stat(st, 0)[:, 0:n], 1.0 / size, EPS, ALU.mult, ALU.add)\
                    .then_inc(S["ms_ready"], 1)
                wait(("rstd_ready", st.on["rstd_ready"]))

            def setup(st):
                dve.wait_ge(S["loaded_first"], n_first)
                lam = scr[:, 0:256].rearrange("p (a b d) -> p a b d", a=2, b=2)
                prod = scr[:, 256:384].rearrange("p (a d) -> p a d", a=2)
                link(tt(prod, lam[:, :, 0, :], lam[:, :, 1, :], ALU.mult))
                nc.vector.tensor_reduce(small[:, 2, 12:14], prod, AX.X, ALU.add).then_inc(S["lam_in"], 1)
                dve.wait_ge(S["cols_ps"], 1)
                nc.vector.tensor_copy(cols[:, :], tp[:, 0:P + 16]).then_inc(S["cols_sb"], 1)
                dve.wait_ge(S["cols_sb"], 1)

                def col2(n):
                    return cols[:, P + ROW2[n]:P + ROW2[n] + 1]
                for name, a, b, s in (("A", "aq", "ak", 64 ** -0.5), ("ex", "exq", "exk", P ** -0.5),
                                      ("C", "cq", "ck", P ** -0.5), ("ox", "oxq", "oxk", P ** -0.5)):
                    stt(gain[name][:, :], col2(a), s, col2(b), ALU.mult, ALU.mult)
                ts(gain["aon"][:, :], col2("aon"), 0.5 * (1 - LAM_INIT), None, ALU.mult)
                dve.wait_ge(S["lam_exp"], 1)
                stt(neglam[:, :], small[:, 2, 15:16], -LAM_INIT, small[:, 2, 14:15], ALU.add, ALU.subtract)
                dve.wait_ge(S["tanh_c"], 1)
                link(stt(scol[:, :], scol[:, :], 1.0, cols[:, ROW["c"]:ROW["c"] + 16], ALU.add, ALU.mult))
                ts(scol[:, :], scol[:, :], 0.5, None, ALU.mult).then_inc(S["gains_ready"], 1)
                dve.wait_ge(S["gains_ready"], 1)

            def split(st):
                s, n = st.sub, st.sub.panel.ncols
                dve.wait_ge(S["hi_ready"], s.i + 1)
                slot = s.i % SPLIT_SLOTS
                tt(wlo[:, slot, 0:s.nk, 0:n], raw[:, s.raw.i % RAW_SLOTS, s.koff:s.koff + s.nk, 0:n],
                   whi[:, slot, 0:s.nk, 0:n].bitcast(F32), ALU.subtract).then_inc(S["lo_ready"], 1)

            def rows_norm(st):
                wait(("sq_ready", st.on["sq_ready"]))
                mean_rstd(st, NT, D)
                for t in range(NT):
                    last = ts(rows_of[st.dst][:, t, :], rows_of[st.src][:, t, :], stat(st, 2)[:, t:t + 1], None,
                              ALU.mult)
                last.then_inc(S["rows_ready"], 1)

            def rows_T(st):
                k0 = 4 * st.half
                hi, lo = (t[:, k0:k0 + 4, :] for t in ((xhi, xlo) if st.key == "x" else (shi, slo)))
                a = scale_cols(st.scale)
                if st.bias is None:
                    wait(("rt_hi", st.on["rt_hi"]))
                    for k in range(4):
                        last = stt(lo[:, k, :], acct(st.acc)[:, k, :], a[:, k0 + k:k0 + k + 1],
                                   hi[:, k, :].bitcast(F32), ALU.mult, ALU.subtract)
                    last.then_inc(S["rt_lo"], 1)
                    return
                b = scale_cols(st.bias)
                tmp = scr[:, :].rearrange("p (k t) -> p k t", t=T)
                wait(("rt_ps", st.on["rt_ps"]))
                wait(st.free["scr"])
                for k in range(4):
                    last = ts(tmp[:, k, :], acct(st.acc)[:, k, :], a[:, k0 + k:k0 + k + 1],
                              b[:, k0 + k:k0 + k + 1], ALU.mult, ALU.add)
                last.then_inc(S["rt_tmp"], 1)
                wait(("rt_hi", st.on["rt_hi"]))
                tt(lo, tmp, hi.bitcast(F32), ALU.subtract).then_inc(S["rt_lo"], 1)

            def evac_norm(st):
                n, gs = 1024 // st.gs, st.gs
                wait(("sq_ready", st.on["sq_ready"]))
                link(nc.vector.tensor_reduce(stat(st, 0)[:, 0:n], heads_of(scr[:, :], n, gs), AX.X, ALU.add))
                mean_rstd(st, n, gs)
                tt(heads_of(grp(*st.dst), n, gs), acc2(st.acc).rearrange("p t (h d) -> p (t h) d", d=gs),
                   across(stat(st, 2)[:, 0:n], [P, n, gs]), ALU.mult).then_inc(S["qk_evac"], 1)

            def evac_gate(st):
                wait(("tanh_ready", st.on["tanh_ready"]))
                n = st.panel.ncols // P
                g = gates[:, st.tile:st.tile + n, :]
                stt(g, g, 1.0, acct(st.acc, n), ALU.add, ALU.mult).then_inc(S["gate_ready"], 1)

            def evac_conv_c(st):
                wait(("v_evac", st.h_evac))
                dve.wait_ge(S["sub_done"], st.done)
                u = g2[:, 0:1024].rearrange("p (c t) -> p c t", t=T)
                tt(u, u, acct(st.acc), ALU.mult).then_inc(S["conv_u"], 1)

            def conv(st):
                u, bb, y = (g2[:, a:a + 1024].rearrange("p (c t) -> p c t", t=T) for a in (0, 1024, 2048))
                wait(("conv_u", 1))
                for c in range(4):
                    wk = [cols[:, ROW["conv_w"] + 4 * k + c:ROW["conv_w"] + 4 * k + c + 1] for k in range(3)]
                    bias = cols[:, ROW["conv_b"] + c:ROW["conv_b"] + c + 1]
                    link(ts(y[:, c, :], u[:, c, :], wk[2], bias, ALU.mult, ALU.add))
                    link(stt(y[:, c, 1:T], u[:, c, 0:T - 1], wk[1], y[:, c, 1:T], ALU.mult, ALU.add))
                    link(stt(y[:, c, 2:T], u[:, c, 0:T - 2], wk[0], y[:, c, 2:T], ALU.mult, ALU.add))
                wait(("v_evac", st.v_evac))
                link(tt(y, y, bb, ALU.mult))
                wait(("gate_ready", st.gate))
                stt(y, y, 0.5, gates[:, 8:12, :], ALU.mult, ALU.mult).then_inc(S["ytmp_ready"], 1)
                wait(("yhi_ready", st.on["yhi_ready"]))
                tt(ylo[:, 8:12, :], y, yhi[:, 8:12, :].bitcast(F32), ALU.subtract).then_inc(S["y_ready"], 1)

            def evac_resid(st):
                dve.wait_ge(S["sub_done"], st.done)
                if st.on["resid_done"] == 1:
                    dve.wait_ge(S["loaded_x"], 16)
                r = h_res[:, :, st.c * CW:(st.c + 1) * CW]
                tt(r, acc2(st.acc), r, ALU.add).then_inc(S["resid_done"], 1)

            def evac_forget(st):
                dve.wait_ge(S["sub_done"], st.done)
                tt(fx[:, :, :], acc2(st.acc, 12), fbb[:, :].unsqueeze(1).to_broadcast([P, NT, 12]), ALU.add)\
                    .then_inc(S["forget_in"], 1)

            def forget_sum(st):
                wait(("forget_in", 1))
                link(ts(fe[:, :, :], fx[:, :, :], -1.0, None, ALU.mult))
                tt(fe[:, :, :], fe[:, :, :], fx[:, :, :], ALU.min).then_inc(S["logf_a"], 1)
                wait(("logf_e", 1))
                stt(logf[:, :, :], fx[:, :, :], 0.0, fe[:, :, :], ALU.min, ALU.subtract).then_inc(S["logf_ready"], 1)
                wait(("cum_ps", 1))
                nc.vector.tensor_copy(cumq[:, :, :], opsum[:, 0:24].rearrange("p (t h) -> p t h", t=NT))\
                    .then_inc(S["cum_sb"], 1)

            def scores(st):
                h = st.h
                wait(("s_ps", st.on["s_ps"]))
                bank = spsum[:, h.n % 2, :]
                if h.type == "A":
                    wait(("PT_ps", st.prev_pt))
                    p = pbuf[:, :].rearrange("p (a k) -> p a k", a=2)
                    stt(p, const("dist").unsqueeze(1).to_broadcast([P, 2, 384]), -(2.0 ** -(h.tile + 1)),
                        spsum[:, :, 0:384], ALU.mult, ALU.add).then_inc(S["s_rd"], 1)
                    wait(("s_rd", st.on["s_rd"]))
                    m = nmx[:, 0:4].rearrange("p (a t) -> p a t", t=2)
                    nc.vector.tensor_reduce(m[:, :, 0], p[:, :, 0:P], AX.X, ALU.max, negate=True)
                    nc.vector.tensor_reduce(m[:, :, 1], p[:, :, P:384], AX.X, ALU.max, negate=True)\
                        .then_inc(S["mx_ready"], 1)
                    wait(("exp_ready", st.on["exp_ready"]))
                    link(nc.vector.reciprocal(rinv[:, :], rsum[:, :]))
                    link(ts(rinv[:, 2:4], rinv[:, 2:4], neglam[:, :], None, ALU.mult))
                    link(ts(p[:, 1, 0:P], p[:, 1, 0:P], rinv[:, 2:3], None, ALU.mult))
                    link(ts(p[:, 1, P:384], p[:, 1, P:384], rinv[:, 3:4], None, ALU.mult))
                    stt(p[:, 0, 0:P], p[:, 0, 0:P], rinv[:, 0:1], p[:, 1, 0:P], ALU.mult, ALU.add)
                    stt(p[:, 0, P:384], p[:, 0, P:384], rinv[:, 1:2], p[:, 1, P:384], ALU.mult, ALU.add)\
                        .then_inc(S["p_ready"], 1)
                    return
                if h.type == "C":
                    wait(("PT_ps", st.prev_pt))
                    wait(("mask1", h.rows["mask1"]))
                    n = h.tile
                    stt(pbuf[:, 0:P], bank[:, 0:P], cumq[:, 0, n:n + 1], negcum0[:, h.j, :], ALU.add, ALU.add)
                    stt(pbuf[:, P:384], bank[:, P:384], cumq[:, 1, n:n + 1], negcum[:, h.j, :], ALU.add, ALU.add)\
                        .then_inc(S["s_rd"], 1)
                    wait(("s_rd", st.on["s_rd"]))
                    parts = [pbuf[:, 0:P], pbuf[:, P:384]]
                    for t in range(NT):
                        last = nc.vector.tensor_reduce(nmx[:, t:t + 1], parts[t], AX.X, ALU.max, negate=True)
                elif h.type == "X":
                    parts = [pbuf[:, 0:T], pbuf[:, T:2 * T]]
                    last = nc.vector.tensor_reduce(nmx[:, 0:2], bank.rearrange("p (t k) -> p t k", t=NT), AX.X,
                                                   ALU.max, negate=True)
                else:
                    parts = [p2[:, 0, :], p2[:, 1, :]]
                    last = nc.vector.tensor_reduce(nmx[:, 0:2], spsum[:, :, :], AX.X, ALU.max, negate=True)
                last.then_inc(S["mx_ready"], 1)
                wait(("exp_ready", st.on["exp_ready"]))
                link(nc.vector.reciprocal(rinv[:, 0:2], rsum[:, 0:2]))
                for t in range(NT):
                    last = ts(parts[t], parts[t], rinv[:, t:t + 1], None, ALU.mult)
                last.then_inc(S["p_ready"], 1)

            def to_lo(st, tile):
                wait(("yhi_ready", st.on["yhi_ready"]))
                tt(ylo[:, tile, :], ytmp[:, :], yhi[:, tile, :].bitcast(F32), ALU.subtract).then_inc(S["y_ready"], 1)

            def pv(st):
                h = st.h
                if h.type == "A":
                    wait(("sq_ready", st.on["sq_ready"]))
                    mean_rstd(st, NT, P)
                    for t in range(NT):
                        last = ts(ytok[:, t * P:(t + 1) * P], opsum[:, t * P:(t + 1) * P], stat(st, 2)[:, t:t + 1],
                                  None, ALU.mult)
                    last.then_inc(S["on_ready"], 1)
                elif h.type == "G":
                    wait(("yhi_ready", st.on["yhi_ready"]))
                    b = h.base
                    tt(ylo[b:b + 64, h.tile, :], opsum[b:b + 64, 0:T], yhi[b:b + 64, h.tile, :].bitcast(F32),
                       ALU.subtract).then_inc(S["y_ready"], 1)
                else:
                    wait(("o_ps", st.on["o_ps"]))
                    wait(("y_ready", st.on["y_ready"] - 1))
                    wait(("gate_ready", st.gate_ready))
                    stt(ytmp[:, :], opsum[:, 0:T], 0.5, gates[:, h.tile, :], ALU.mult, ALU.mult)\
                        .then_inc(S["ytmp_ready"], 1)
                    to_lo(st, h.tile)

            def oT(st):
                wait(("oT_ps", st.on["oT_ps"]))
                wait(("y_ready", st.on["y_ready"] - 1))
                wait(("gate_ready", st.gate_ready))
                stt(ytmp[:, :], tp[:, 0:T], gain["aon"][:, :], gates[:, st.h.tile, :], ALU.mult, ALU.mult)\
                    .then_inc(S["ytmp_ready"], 1)
                to_lo(st, st.h.tile)

            def mod(st):
                raw_wait(dve, st.raw)
                if st.u == 0:
                    wait(("cum_out", 16))
                for k in range(RAWK):
                    for v in range(2 if st.ctx else 1):
                        c = scol[:, 8 * v + RAWK * st.u + k:8 * v + RAWK * st.u + k + 1]
                        src = raw[:, st.raw.i % RAW_SLOTS, k, :]
                        if st.u == 0 and k == 0:
                            ins = ts(macc[:, v, :], src, c, None, ALU.mult)
                        else:
                            ins = stt(macc[:, v, :], src, c, macc[:, v, :], ALU.mult, ALU.add)
                        if k == RAWK - 1 and v == (1 if st.ctx else 0):
                            ins.then_inc(S["mod_read"], 1)
                            wait(("mod_read", st.on["mod_read"]))
                        elif v == (1 if st.ctx else 0):
                            link(ins)

            def mod_bias(st):
                wait(("bias_in", 16 * st.on["bias_in"]))
                tt(macc[0:1, 0, :], macc[0:1, 0, :], macc[0:1, 1, :], ALU.add).then_inc(S["bias_done"], 1)

            def mod_out(st):
                wait(("mod_ps", st.on["mod_ps"]))
                c = st.chunk
                if st.gate:
                    which = c >= 6
                    dve.wait_ge(S["loaded_post_ffn" if which else "loaded_post_mix"], 16)
                    g = post_gain[which][:, (c % 2) * CW:(c % 2 + 1) * CW]
                    tt(g, tp[:, :], g, ALU.mult).then_inc(S["mod_sb"], 1)
                    return
                for v in range(2 if st.ctx else 1):
                    last = tt(modc[:, v, 4 * c:4 * c + 4], tp[:, 4 * v:4 * v + 4],
                              cols[:, ROW["b_mod"] + 4 * c:ROW["b_mod"] + 4 * c + 4], ALU.add)
                last.then_inc(S["mod_sb"], 1)

            def mod_cols(st):
                wait(("mod_sb", st.mod_sb))
                for name, v, at, g in ((("mix_A", 0, 8, "pre_mix"), ("ctx_A", 1, 8, "pre_mix"))
                                       if st.which == "mix" else (("ffn_A", 0, 32, "pre_ffn"),)):
                    link(stt(mcol[name][:, :], modc[:, v, at:at + 8], 1.0, cols[:, ROW[g]:ROW[g] + 8],
                             ALU.add, ALU.mult))

            def rope_tables(st):
                dve.wait_ge(S["loaded_rope"], 16 * 3)
                base = ropes["ret"]
                for i, n in enumerate(("q", "k")):
                    g = growb[:, 64 * i:64 * i + 64]

                    def rep(a):
                        return a.unsqueeze(1).to_broadcast([P, NT, a.shape[1]])
                    tt(ropes[n][:, 0, :, :], base[:, 0, :, :], rep(g), ALU.mult)
                    tt(ropes[n][:, 1, :, 0:32], base[:, 1, :, 0:32], rep(g[:, 32:64]), ALU.mult)
                    link(tt(ropes[n][:, 1, :, 32:64], base[:, 1, :, 32:64], rep(g[:, 0:32]), ALU.mult))

            def evac_kv(st):
                ctx_side = st.kind == "evac_ctxkv"
                wait(("sq_ready", st.on["sq_ready"]))
                link(nc.vector.tensor_reduce(stat(st, 0)[:, 0:4], heads_of(scr[:, 0:256], 4, 64), AX.X, ALU.add))
                mean_rstd(st, 4, 64)
                tmp = scr[:, 256:512].rearrange("p (t h d) -> p t h d", t=NT, h=2)
                rs = stat(st, 2)[:, 0:4].rearrange("p (t h) -> p t h", t=NT).unsqueeze(3).to_broadcast([P, NT, 2, 64])
                tt(tmp, acc2(st.acc, P).rearrange("p t (h d) -> p t h d", h=2), rs, ALU.mult)\
                    .then_inc(S["norm_mid"], 1)
                wait(("norm_mid", st.on["norm_mid"]))
                dst = (ctx_k if ctx_side else lat_k).rearrange("p t (h d) -> p t h d", h=2)
                if ctx_side:
                    g = growb[:, 64:128].unsqueeze(1).to_broadcast([P, 4, 64])
                    tt(dst.rearrange("p t h d -> p (t h) d"), tmp.rearrange("p t h d -> p (t h) d"), g, ALU.mult)\
                        .then_inc(S["rope_done"], 1)
                    return
                tb = ropes["k"]

                def rep(a):
                    return a.unsqueeze(2).to_broadcast([P, NT, 2, a.shape[2]])
                tt(dst[:, :, :, 0:32], tmp[:, :, :, 32:64], rep(tb[:, 1, :, 0:32]), ALU.mult)
                link(tt(dst[:, :, :, 32:64], tmp[:, :, :, 0:32], rep(tb[:, 1, :, 32:64]), ALU.mult))
                link(tt(tmp, tmp, rep(tb[:, 0, :, :]), ALU.mult))
                tt(dst, dst, tmp, ALU.add).then_inc(S["rope_done"], 1)

            def evac_rope(st):
                dve.wait_ge(S["sub_done"], st.done)
                wait(st.free["scr"])
                tb = ropes["ret"]
                for t in range(NT):
                    x = acc2(st.acc)[:, t, :].rearrange("p (h d) -> p h d", d=64)
                    y = grp(*st.dst)[:, t * CW:(t + 1) * CW].rearrange("p (h d) -> p h d", d=64)
                    z = scr[:, t * CW:(t + 1) * CW].rearrange("p (h d) -> p h d", d=64)

                    def rep(a):
                        return a.unsqueeze(1).to_broadcast([P, 8, a.shape[1]])
                    tt(y[:, :, 0:32], x[:, :, 32:64], rep(tb[:, 1, t, 0:32]), ALU.mult)
                    tt(y[:, :, 32:64], x[:, :, 0:32], rep(tb[:, 1, t, 32:64]), ALU.mult)
                    link(tt(z, x, rep(tb[:, 0, t, :]), ALU.mult))
                    last = tt(y, y, z, ALU.add)
                last.then_inc(S["rope_done"], 1)

            def evac_normrope(st):
                wait(("sq_ready", st.on["sq_ready"]))
                link(nc.vector.tensor_reduce(stat(st, 0)[:, 0:16], heads_of(scr[:, :], 16, 64), AX.X, ALU.add))
                mean_rstd(st, 16, 64)
                tt(heads_of(scr[:, :], 16, 64), acc2(st.acc).rearrange("p t (h d) -> p (t h) d", d=64),
                   across(stat(st, 2)[:, 0:16], [P, 16, 64]), ALU.mult).then_inc(S["norm_mid"], 1)
                wait(("norm_mid", st.on["norm_mid"]))
                tb = ropes["q"]
                for t in range(NT):
                    x = scr[:, t * CW:(t + 1) * CW].rearrange("p (b a d) -> p b a d", b=2, a=4)
                    y = g0[:, t * CW:(t + 1) * CW].rearrange("p (a b d) -> p b a d", b=2, a=4)

                    def rep(a):
                        return a.unsqueeze(1).unsqueeze(1).to_broadcast([P, 2, 4, a.shape[1]])
                    tt(y[:, :, :, 0:32], x[:, :, :, 32:64], rep(tb[:, 1, t, 0:32]), ALU.mult)
                    link(tt(y[:, :, :, 32:64], x[:, :, :, 0:32], rep(tb[:, 1, t, 32:64]), ALU.mult))
                    link(tt(x, x, rep(tb[:, 0, t, :]), ALU.mult))
                    last = tt(y, y, x, ALU.add)
                last.then_inc(S["rope_done"], 1)

            def decays(st):
                wait(("lg_exp", 1))
                for e in range(4):
                    for t in range(NT):
                        last = ts(dec[:, e, t, :], lg[:, 8 * (e % 2):8 * (e % 2) + 8],
                                  const("expo", e * 2 + t, e * 2 + t + 1), None, ALU.mult)
                last.then_inc(S["dec_arg"], 1)

            def decayed(dst, src, e, done):
                for t in range(NT):
                    x = src[:, t * CW:(t + 1) * CW].rearrange("p (h d) -> p h d", d=64)
                    for fb in range(2):
                        last = tt(dst[:, t, :, fb, :], x, across(dec[:, e + fb, t, :], [P, 8, 64]), ALU.mult)
                last.then_inc(S[done], 1)

            def ctx_state(st):
                wait(("dec_exp", 1))
                wait(("v_evac", st.v_evac))
                decayed(kfb, grp("g2", 0), 2, "kfb_ready")

            def ret_q(st):
                wait(("state_ps", 1))
                wait(("rope_done", st.rope_done))
                decayed(qfb, grp("g1", 0), 0, "qfb_ready")

            def ret_decay(st):
                h = st.h
                dve.wait_ge(S["loaded_ret"], 16)
                m = dmat[:, h % 2, :]
                wait(("am_ready", st.am_read))
                link(ts(m, rett[:, 1, :], lg[:, 8 + h:9 + h], None, ALU.mult))
                stt(m, rett[:, 0, :], lg[:, h:h + 1], m, ALU.mult, ALU.add).then_inc(S["m_arg"], 1)

            def ret_scores(st):
                wait(("s_ps", st.on["s_ps"]))
                wait(("m_ready", st.m_ready))
                wait(("o_ps", st.prev_o))
                tt(am[:, st.h % 2, :], spsum[:, st.h % 2, :], dmat[:, st.h % 2, :], ALU.mult)\
                    .then_inc(S["am_ready"], 1)

            def ret_norm(st):
                r = heads_of(g0[:, 0:1024], 16, 64)
                mean = stat(st, 0)[:, 0:16]
                wait(("ret_sb", st.ret_sb))
                link(nc.vector.tensor_reduce(mean, r, AX.X, ALU.add))
                link(ts(mean, mean, 1.0 / 64, None, ALU.mult))
                tt(r, r, across(mean, [P, 16, 64]), ALU.subtract).then_inc(S["ret_mid"], 1)
                wait(("sq_ready", st.on["sq_ready"]))
                link(nc.vector.tensor_reduce(stat(st, 0)[:, 0:16], heads_of(scr[:, :], 16, 64), AX.X, ALU.add))
                mean_rstd(st, 16, 64)
                tt(r, r, across(stat(st, 2)[:, 0:16], [P, 16, 64]), ALU.mult).then_inc(S["rn_ready"], 1)
                wait(("rt_ps", st.on["rt_ps"]))
                z = scr[:, :].rearrange("p (k t) -> p k t", t=T)
                wait(("gate_ready", st.gate_ready))
                stt(z, spt, 0.5, gates[:, 4:8, :], ALU.mult, ALU.mult).then_inc(S["ytmp_ready"], 1)
                wait(("yhi_ready", st.on["yhi_ready"]))
                tt(ylo[:, 4:8, :], z, yhi[:, 4:8, :].bitcast(F32), ALU.subtract).then_inc(S["y_ready"], 1)

            def post(st):
                wait(("sq_ready", st.on["sq_ready"]))
                mean_rstd(st, NT, D)
                wait(("mod_sb", st.mod_sb))
                for t in range(NT):
                    last = stt(mixed[:, t, :], mixed[:, t, :], stat(st, 2)[:, t:t + 1], post_gain[st.which],
                               ALU.mult, ALU.mult)
                link(last)
                tt(h_res[:, :, :], h_res[:, :, :], mixed, ALU.add).then_inc(S["post_done"], 1)

            def evac_ffb(st):
                dve.wait_ge(S["sub_done"], st.done)
                wait(st.free["scr"])
                n = len(st.tiles)
                z = scr[:, 0:n * T].rearrange("p (k t) -> p k t", t=T)
                wait(("gate_ready", st.gate))
                stt(z, gates[:, st.gate_tile:st.gate_tile + n, :], 0.5, acct(st.acc, n), ALU.mult, ALU.mult)\
                    .then_inc(S["ytmp_ready"], 1)
                wait(("yhi_ready", st.on["yhi_ready"]))
                tt(y_part(st.tiles[0], n, 1), z, y_part(st.tiles[0], n, 0).bitcast(F32), ALU.subtract)\
                    .then_inc(S["y_ready"], 1)

            does = {"setup": setup, "split": split, "rows_norm": rows_norm, "rows_T": rows_T, "evac_norm": evac_norm,
                    "evac_gate": evac_gate, "evac_conv_z": evac_gate, "evac_ffa": evac_gate,
                    "evac_conv_c": evac_conv_c, "conv": conv, "evac_resid": evac_resid,
                    "evac_forget": evac_forget, "forget_sum": forget_sum, "scores": scores, "pv": pv, "oT": oT,
                    "mod": mod, "mod_bias": mod_bias, "mod_out": mod_out, "mod_cols": mod_cols,
                    "rope_tables": rope_tables, "evac_ctxkv": evac_kv, "evac_latkv": evac_kv,
                    "evac_rope": evac_rope, "evac_normrope": evac_normrope, "decays": decays,
                    "ctx_state": ctx_state, "ret_q": ret_q, "ret_decay": ret_decay, "ret_scores": ret_scores,
                    "ret_norm": ret_norm, "post": post, "evac_ffb": evac_ffb}
            for st in pl.steps:
                if st.kind in does:
                    does[st.kind](st)

        @block.gpsimd
        def _(pool):
            def wait(pair):
                if pair and pair[1] > 0:
                    pool.wait_ge(S[pair[0]], pair[1])

            groups_of = {"rows_norm": NT, "evac_norm": 16, "evac_normrope": 16, "evac_ctxkv": 4, "evac_latkv": 4,
                         "pv": NT, "ret_norm": 16, "post": NT}

            def rstd(st):
                n = 1024 // st.gs if st.kind == "evac_norm" else groups_of[st.kind]
                i = 3 * (st.on["sq_ready"] % 2)
                wait(("ms_ready", st.on["ms_ready"]))
                nc.gpsimd.tensor_tensor(small[:, i + 2, 0:n], small[:, i + 1, 0:n],
                                        half_neg[:, 0:n], ALU.pow).then_inc(S["rstd_ready"], 1)

            def forget_sum(st):
                wait(("cum_sb2", 1))
                pool.dma_start(scratch, cumT).then_inc(S["cum_out"], 16)

            def forget_rows(st):
                wait(("s_rd", st.prev))
                wait(("cum_out", 16))
                pool.dma_start(negcum[:, :, :], scratch[4 * st.g:4 * st.g + 4, :].unsqueeze(0).to_broadcast([P, 4, T]))\
                    .then_inc(S["rows_in"], 16)
                wait(("rows_in", 16 * st.on["rows_in"]))
                for dst, src, name in ((negcum0[:, :, :], negcum[:, :, 0:P], "mask0"),
                                       (negcum[:, :, P:T], negcum[:, :, P:T], "mask1")):
                    nc.gpsimd.affine_select(out=dst, in_=src, pattern=[[0, 4], [-1, P]], compare_op=ALU.is_ge,
                                            fill=BIG, base=0, channel_multiplier=1).then_inc(S[name], 1)

            def load(st):
                wait(("o_ps", st.after))
                wait(("rt_ps", st.rows))
                s = S["loaded_" + st.what]
                if st.what == "x":
                    pool.dma_start(h_res[:, :, :], w["x"].rearrange("b (t p) d -> p (b t) d", p=P)).then_inc(s, 16)
                elif st.what == "ctx":
                    pool.dma_start(rows_of["g2"], w["ctx_2"].rearrange("b (t p) d -> p (b t) d", p=P)).then_inc(s, 16)
                elif st.what == "rope":
                    pool.dma_start(g2[:, 2048:2304], w["const_rope"]).then_inc(s, 16)
                    pool.dma_start(growb[:, 0:64], w["q_norm_g_2"].to_broadcast([P, 64])).then_inc(s, 16)
                    pool.dma_start(growb[:, 64:128], w["k_norm_g_2"].to_broadcast([P, 64])).then_inc(s, 16)
                elif st.what == "ret":
                    pool.dma_start(rett[:, :, :].rearrange("p a n -> p (a n)"), w["const_ret"]).then_inc(s, 16)
                else:
                    i = st.what == "post_ffn"
                    pool.dma_start(post_gain[i], w["g_post_ffn_2" if i else "g_post_mix_2"].to_broadcast([P, D]))\
                        .then_inc(s, 16)

            def mod_bias_in(st):
                wait(("mod_ps", st.prev))
                pool.dma_start(macc[0:1, 1, :], w["b_mod_2"][:, st.chunk * CW:(st.chunk + 1) * CW])\
                    .then_inc(S["bias_in"], 16)

            def ret_decay(st):
                wait(("m_exp", st.on["m_exp"]))
                m = dmat[:, st.h % 2, :]
                nc.gpsimd.tensor_tensor(m, m, rett[:, 2, :], ALU.mult).then_inc(S["m_ready"], 1)

            nc.gpsimd.memset(half_neg[:, :], -0.5).then_inc(S["setup_pool"], 1)
            pool.wait_ge(S["setup_pool"], 1)
            does = {"forget_sum": forget_sum, "forget_rows": forget_rows, "load": load, "mod_bias_in": mod_bias_in,
                    "ret_decay": ret_decay}
            for st in pl.steps:
                if st.kind in does:
                    does[st.kind](st)
                if st.kind in groups_of and "rstd_ready" in st.on:
                    rstd(st)



_INS = ["x", "mem", "e_norm_g", "e_w_in", "e_w_out", "e_a_q_norm_g", "e_a_k_norm_g", "e_a_lambda",
        "e_a_out_norm_g", "e_b_conv_w", "e_b_conv_b", "e_x_q_norm_g", "e_x_k_norm_g", "e_mem_norm_g",
        "e_w_mem_kv", "o_norm_g", "o_w_in", "o_w_out", "o_c_q_norm_g", "o_c_k_norm_g", "o_c_forget_b",
        "o_x_q_norm_g", "o_x_k_norm_g", "o_mem_norm_g", "o_w_mem_kv", "c_2", "ctx_2", "c_ctx_2", "w_mod_2",
        "b_mod_2", "g_pre_mix_2", "g_post_mix_2", "g_pre_ffn_2", "g_post_ffn_2", "w_in_2", "q_norm_g_2",
        "k_norm_g_2", "ret_decay_fwd_2", "ret_decay_bwd_2", "w_out_2", "w_ffn_in_2", "w_ffn_out_2"]
_MATRICES = {"e_w_in": "e_w_in", "e_w_out": "e_w_out", "e_w_mem_kv": "e_w_mem_kv", "o_w_in": "o_w_in",
             "o_w_out": "o_w_out", "o_w_mem_kv": "o_w_mem_kv", "w_mod": "w_mod_2", "w_in_2": "w_in_2",
             "w_out_2": "w_out_2", "w_ffn_in": "w_ffn_in_2", "w_ffn_out": "w_ffn_out_2"}
STOP = None


def kernel(**inputs):
    import concourse.bacc as bacc
    from concourse.bass_utils import run_bass_kernel_spmd

    nc = bacc.Bacc("TRN2", target_bir_lowering=False, num_devices=1)
    first_c, ret_c, rope_c = constants()
    arrays, w = {}, {}
    named = {name: np.ascontiguousarray(inputs[name]) for name in _INS}
    named.update(const_first=first_c, const_ret=ret_c, const_rope=rope_c)
    for name, a in named.items():
        arrays["in_" + name] = a
        w[name] = nc.dram_tensor("in_" + name, a.shape, mybir.dt.from_np(a.dtype), kind="ExternalInput").ap()
    for short, name in _MATRICES.items():
        w[short] = w[name].rearrange("a k n -> (a k) n")
    out = nc.dram_tensor("out_0", (1, T, D), F32, kind="ExternalOutput").ap()
    program(nc, w, out, STOP)
    r = run_bass_kernel_spmd(nc, [arrays], core_ids=[0])
    return r.results[0]["out_0"]
```

```python
import math
from contextlib import ExitStack

import numpy as np

import concourse.bass as bass
from concourse import mybir

F32 = mybir.dt.float32
F32R = mybir.dt.float32r
ACT = mybir.ActivationFunctionType
ALU = mybir.AluOpType
AX = mybir.AxisListType

P = 128
D = 1024
T = 256
NT = T // P
KT = D // P
CW = 512
SUBK = 2
RAWK = 4
RAW_SLOTS, SPLIT_SLOTS, LEAD = 3, 4, 3
EPS = 1e-6
LAM_INIT = 0.8 - 0.6 * math.exp(-0.3 * 0)
FFN = 2816
EVEN_Y, ODD_Y, MIX_Y = 2048, 2048, 1024
BIG = -1e30

ROW = dict(e_norm=0, e_mem=8, o_norm=16, o_mem=24, pre_mix=32, pre_ffn=40, b_mod=48, c=96, c_ctx=104,
           conv_w=112, conv_b=124)
ROW2 = dict(aq=0, ak=1, aon=2, exq=3, exk=4, cq=5, ck=6, oxq=7, oxk=8)

CONST = {}


def constants():
    p = np.arange(P)[:, None]
    t = np.arange(T)[None, :]
    parts = {
        "ident": np.eye(P, dtype=np.float32),
        "tri": (p <= t).astype(np.float32),
        "dist": np.concatenate([np.where(p >= t[:, :P], p - t[:, :P], 1e34),
                                np.where(p + P >= t, p + P - t, 1e34)], axis=1).astype(np.float32),
    }
    pos = np.arange(T).reshape(NT, P).T.astype(np.float32)
    parts["expo"] = np.concatenate([pos + 1, T - pos, T - 1 - pos, pos], axis=1)
    at, out = 0, []
    for name, a in parts.items():
        CONST[name] = (at, a.shape[1])
        at += a.shape[1]
        out.append(a.astype(np.float32))
    first = np.concatenate(out, axis=1)
    j = np.arange(T).reshape(NT, P).T[:, :, None]
    i = np.arange(T)[None, None, :]
    ret = np.concatenate([np.maximum(i - j, 0).reshape(P, -1), np.maximum(j - i, 0).reshape(P, -1),
                          (0.125 * (1 + (i == j))).reshape(P, -1)], axis=1).astype(np.float32)
    tok = np.arange(T)
    inv = (10000.0 ** (-np.arange(16, dtype=np.float32) / 16)).astype(np.float32)
    ang = np.concatenate([(tok // 64).astype(np.float32)[:, None] * inv,
                          (tok % 64).astype(np.float32)[:, None] * inv], axis=1).astype(np.float32)
    c, s = np.cos(ang).astype(np.float32), np.sin(ang).astype(np.float32)
    cc = np.concatenate([c, c], axis=1).reshape(NT, P, 64).transpose(1, 0, 2).reshape(P, -1)
    ss = np.concatenate([-s, s], axis=1).reshape(NT, P, 64).transpose(1, 0, 2).reshape(P, -1)
    return first, ret, np.ascontiguousarray(np.concatenate([cc, ss], axis=1))




class Step:

    def __init__(self, kind, panel=None, sub=None, h=None, src=None, dst=None, waits=(), xn=None, ready=None,
                 key=None, scale=None, bias=None, half=None, tile=None, gs=None, c=None, h_evac=None, gate=None,
                 gate_tile=None, tiles=None, prev_s=None, part=None, what=None, after=0, rows=0, chunk=None,
                 u=None, ctx=None, prev=None, mod_read=None, bias_done=None, which=None, mod_sb=None,
                 v_evac=None, g=None, rope_done=None, qfb=None, prev_o=None, qkT_sb=None, m_ready=None,
                 am_ready=None, ret_sb=None, gate_ready=None, first=None, sq_ready=None):
        self.kind, self.on, self.free = kind, {}, {}
        self.panel, self.sub, self.h, self.src, self.dst, self.waits = panel, sub, h, src, dst, waits
        self.xn, self.ready, self.key, self.scale, self.bias, self.half = xn, ready, key, scale, bias, half
        self.tile, self.gs, self.c, self.h_evac, self.gate = tile, gs, c, h_evac, gate
        self.gate_tile, self.tiles, self.prev_s, self.part = gate_tile, tiles, prev_s, part
        self.what, self.after, self.rows, self.chunk, self.u, self.ctx = what, after, rows, chunk, u, ctx
        self.prev, self.mod_read, self.bias_done, self.which, self.mod_sb = prev, mod_read, bias_done, which, mod_sb
        self.v_evac, self.g, self.rope_done, self.qfb, self.prev_o = v_evac, g, rope_done, qfb, prev_o
        self.qkT_sb, self.m_ready, self.am_ready, self.ret_sb = qkT_sb, m_ready, am_ready, ret_sb
        self.gate_ready, self.first, self.sq_ready = gate_ready, first, sq_ready


class Panel:

    def __init__(self, w, col, ncols, src, orient, kts):
        self.w, self.col, self.ncols, self.src, self.orient, self.kts = w, col, ncols, src, orient, kts


class Sub:

    def __init__(self, i, panel, k0, nk, first, last, waits):
        self.i, self.panel, self.k0, self.nk, self.waits = i, panel, k0, nk, waits
        self.first, self.last = first, last


class Load:

    def __init__(self, i, w, row, nk, col, ncols, read):
        self.i, self.w, self.row, self.nk, self.col, self.ncols, self.read = i, w, row, nk, col, ncols, read


class Head:

    def __init__(self, type, g, j, tile, ready, gain=None, rows=None, part=0, base=0, kT_sb=None):
        self.type, self.g, self.j, self.tile, self.ready = type, g, j, tile, ready
        self.gain, self.rows, self.part, self.base, self.kT_sb = gain, rows, part, base, kT_sb


class Plan:

    def __init__(self):
        self.steps = []
        self.count = {}
        self.subs = []
        self.busy = {}
        self.acc_uses = 0
        self.src = {}
        self.tile_ready = {}
        self.later = {}
        self.pos = 0
        self.heads = 0
        self.gated = {}
        self.chunks = []
        self.pending = {}

    def tick(self, st, *names):
        for n in names:
            self.count[n] = self.count.get(n, 0) + 1
            st.on[n] = self.count[n]

    def step(self, kind, **kw):
        st = Step(kind, **kw)
        self.steps.append(st)
        return st

    def uses(self, st, bank, by):
        st.free[bank] = self.busy.get(bank)
        self.busy[bank] = (by, st.on[by])

    def next_acc(self, st, by):
        st.acc = self.acc_uses % 2
        st.free["acc"] = self.busy.get(("acc", st.acc))
        self.busy[("acc", st.acc)] = (by, st.on[by])
        self.acc_uses += 1

    def panel(self, w, col, ncols, src, evac, orient="tok", kts=KT, opened=False, order=None, **kw):
        pan = Panel(w, col, ncols, src, orient, kts)
        ev = Step("evac_" + evac, panel=pan, **kw)
        ticks = {"norm": ("sq_ready", "ms_ready", "rstd_ready", "qk_evac"), "copy": ("v_evac",),
                 "gate": ("tanh_ready", "gate_ready"), "conv_h": ("v_evac",), "conv_c": ("conv_u",),
                 "conv_b": ("v_evac",), "conv_z": ("tanh_ready", "gate_ready"),
                 "resid": ("resid_done",), "forget": ("forget_in",),
                 "rope": ("rope_done",), "normrope": ("sq_ready", "ms_ready", "rstd_ready", "norm_mid", "rope_done"),
                 "ctxkv": ("sq_ready", "ms_ready", "rstd_ready", "norm_mid", "v_evac", "rope_done"),
                 "latkv": ("sq_ready", "ms_ready", "rstd_ready", "norm_mid", "v_evac", "rope_done"),
                 "mix": ("sq_ready", "sq_ready", "v_evac", "v_evac"), "ffa": ("tanh_ready", "gate_ready"), "ffb": ("ytmp_ready", "yhi_ready", "y_ready")}
        frees = {"norm": "qk_evac", "copy": "v_evac", "gate": "gate_ready", "conv_h": "v_evac", "conv_c": "conv_u",
                 "conv_b": "v_evac", "conv_z": "gate_ready", "resid": "resid_done", "forget": "forget_in",
                 "rope": "rope_done", "normrope": "norm_mid", "ctxkv": "v_evac", "latkv": "v_evac",
                 "mix": "v_evac", "ffa": "gate_ready", "ffb": "ytmp_ready"}
        pan.ev, pan.ticks, pan.frees = ev, ticks[evac], frees[evac]
        pan.acc = self.acc_uses % 2
        pan.free_acc = self.busy.get(("acc", pan.acc))
        self.acc_uses += 1
        pan.done = 0
        if not opened:
            for a, b in order or [(0, kts)]:
                self.parts(pan, a, b)
        return ev

    def parts(self, pan, first, end):
        for k0 in range(first, end, SUBK):
            nk = min(SUBK, end - k0)
            first = pan.done == 0
            pan.done += nk
            waits = []
            if first:
                waits += [pan.free_acc] if pan.free_acc else []
            if pan.src in self.src:
                waits.append(("rt_lo", self.src[pan.src] - (k0 < 4)))
            if pan.src == "y":
                waits.append(("y_ready", max(self.tile_ready[k] for k in range(k0, k0 + nk))))
            sub = Sub(len(self.subs), pan, k0, nk, first, pan.done == pan.kts, waits)
            self.subs.append(sub)
            self.steps.append(Step("sub", sub=sub))
            if sub.last:
                ev = pan.ev
                ev.done, ev.acc = len(self.subs), pan.acc
                self.tick(ev, *pan.ticks)
                self.busy[("acc", pan.acc)] = (pan.frees, ev.on[pan.frees])
                scr_by = {"evac_norm": "ms_ready", "evac_rope": "rope_done", "evac_normrope": "rope_done",
                          "evac_ctxkv": "rope_done", "evac_latkv": "rope_done", "evac_ffb": "y_ready",
                          "evac_mix": "sq_ready"}.get(ev.kind)
                if scr_by:
                    self.uses(ev, "scr", scr_by)
                self.steps.append(ev)
                if ev.kind in ("evac_gate", "evac_conv_z"):
                    for k in range(ev.tile, ev.tile + pan.ncols // P):
                        self.gated[k] = ev.on["gate_ready"]
                if ev.dst:
                    assert not self.pending.get(ev.dst[0]), ev.dst
                if ev.kind == "evac_ffb":
                    for k in ev.tiles:
                        self.tile_ready[k] = ev.on["y_ready"]
            self.run_due(self.pos)
            self.pos += 1

    def at(self, pos, make, rank=0):
        self.later.setdefault(max(pos, self.pos), []).append((rank, len(self.steps), make))

    def run_due(self, pos):
        for _, _, make in sorted(self.later.pop(pos, []), key=lambda x: x[0]):
            make()

    def flush(self):
        while self.later:
            self.run_due(min(self.later))

    def norm_rows(self, src, dst, *waits):
        st = self.step("rows_norm", src=src, dst=dst, waits=waits)
        self.tick(st, "sq_ready", "ms_ready", "rstd_ready", "rows_ready")
        self.uses(st, "scr", "sq_ready")
        return st

    def transposed(self, xn, ready, key, scale, bias=None):
        for half in range(2):
            st = self.step("rows_T", xn=xn, ready=ready, key=key, scale=scale, bias=bias, half=half)
            self.tick(st, "rt_ps", "rt_hi", "rt_lo")
            if bias is not None:
                self.tick(st, "rt_tmp")
                self.uses(st, "scr", "rt_lo")
            self.next_acc(st, "rt_tmp" if bias is not None else "rt_lo")
        self.src[key] = st.on["rt_lo"]

    def head(self, h, pos, gap=4):
        h.n = self.heads
        self.heads += 1
        self.pending[h.g] = self.pending.get(h.g, 0) + 1
        kind = h.type

        def f1():
            h.f1 = self.step("qkT", h=h, prev_s=self.count.get("s_ps", 0))
            self.tick(h.f1, "qkT_ps", "qkT_sb")
            self.uses(h.f1, "tp", "qkT_sb")

        def f2(transposes_due=0):
            h.f2 = self.step("scores", h=h)
            h.f2.qkT_sb = self.count["qkT_sb"]
            h.f2.prev_pt = self.count.get("PT_ps", 0) + transposes_due
            self.tick(h.f2, "s_ps", "mx_ready", "exp_ready", "p_ready")
            if kind in "AC":
                self.tick(h.f2, "s_rd")
            by = "s_rd" if kind in "AC" else "exp_ready"
            banks = {"A": ("s0", "s1"), "G": ("s0", "s1")}.get(kind, (f"s{h.n % 2}",))
            h.banks = banks
            for b in banks:
                self.uses(h.f2, b, by)

        def f3(part=0):
            st = self.step("PT", h=h, part=part)
            st.p_ready = h.f2.on["p_ready"]
            st.prev_o = self.count.get("o_ps", 0)
            self.tick(st, "PT_ps", "PT_sb")
            self.uses(st, "tp", "PT_sb")
            h.f3 = st

        def f4():
            self.pending[h.g] -= 1
            h.f4 = self.step("pv", h=h)
            h.f4.PT_sb = h.f3.on["PT_sb"]
            self.tick(h.f4, "o_ps")
            if kind == "A":
                self.tick(h.f4, "sq_ready", "ms_ready", "rstd_ready", "on_ready")
                self.uses(h.f4, "o", "on_ready")
                self.uses(h.f4, "scr", "sq_ready")
            elif kind == "G":
                self.tick(h.f4, "yhi_ready", "y_ready")
                self.uses(h.f4, "o", "y_ready")
                self.tile_ready[h.tile] = h.f4.on["y_ready"]
            else:
                self.tick(h.f4, "ytmp_ready", "yhi_ready", "y_ready")
                h.f4.gate_ready = self.gated[h.tile]
                self.uses(h.f4, "o", "ytmp_ready")
                self.tile_ready[h.tile] = h.f4.on["y_ready"]

        def f5():
            h.f5 = self.step("oT", h=h)
            h.f5.on_ready = h.f4.on["on_ready"]
            h.f5.gate_ready = self.gated[h.tile]
            self.tick(h.f5, "oT_ps", "ytmp_ready", "yhi_ready", "y_ready")
            self.uses(h.f5, "tp", "ytmp_ready")
            self.tile_ready[h.tile] = h.f5.on["y_ready"]

        def due(at, make, rank=0):
            if pos is not None:
                self.at(pos + at, make, rank)
        due(0 if h.j else 1, f1, -1)
        due(2, f2)
        due(gap + 2, f3, -1)
        due(gap + 3, f4)
        if kind == "A":
            due(gap + 6, f5, 1)
        return f1, f2, f3, f4

    def grouped(self, heads, pos):
        fs = [self.head(h, None) for h in heads]

        def beside(i):
            if i > 0:
                fs[i - 1][2](0)
            if i < len(heads):
                fs[i][1](i > 0)
            if i > 0:
                fs[i - 1][2](1)
            if i < len(heads):
                self.step("exps", first=heads[i].f2)
            if i + 1 < len(heads) and heads[i + 1].part == 0:
                fs[i + 1][0]()
            if i > 0:
                fs[i - 1][3]()
        self.at(pos, fs[0][0])
        for i in range(len(heads) + 1):
            self.at(pos + 1 + i, lambda i=i: beside(i))
        return pos + 1 + len(heads)

    def residual(self):
        return [(n, self.count[n]) for n in ("resid_done", "post_done") if n in self.count]

    def load(self, what, after=0, rows=0):
        st = self.step("load", what=what, after=after, rows=rows)
        self.tick(st, "loaded_" + what)
        return st

    def mod(self, pos, chunk, ctx=False, gate=False):
        pos = max(pos, self.pos) + max(pos, self.pos) % 2

        def read(u, part):
            if u == 0 and part == 0 and gate:
                st = self.step("mod_bias_in", chunk=chunk, prev=self.count.get("mod_ps", 0))
                self.tick(st, "bias_in")
            st = self.step("mod", chunk=chunk, u=u, part=part, ctx=ctx)
            self.tick(st, "mod_read")

        def out():
            if gate:
                st = self.step("mod_bias", chunk=chunk)
                st.on["bias_in"] = self.count["bias_in"]
                self.tick(st, "bias_done")
            st = self.step("mod_out", chunk=chunk, ctx=ctx, gate=gate, mod_read=self.count["mod_read"],
                           bias_done=self.count.get("bias_done", 0))
            self.tick(st, "mod_ps", "mod_sb")
            self.uses(st, "tp" if gate else "o", "mod_sb")
            self.chunks.append(chunk)
        for i in range(4):
            self.at(pos + (i if ctx else i // 2 * 2), lambda i=i: read(i // 2, i % 2))
        self.at(pos + 6, out, 2)
        return pos + 8


def make_plan():
    pl = Plan()

    def heads(kind, g, evs, base, n, tile0, gap=4, **kw):
        ready = [(s, e.on[s]) for e in evs for s in ("qk_evac", "v_evac") if s in e.on]
        for j in range(n):
            pl.head(Head(kind, g, j, tile0 + j, ready, **kw), base, gap)
            base += gap
        return base

    pl.step("setup")
    st = pl.norm_rows("g0", "g0", ("loaded_x0", 16), ("loaded_x1", 16))
    pl.transposed("g0", st.on["rows_ready"], "x", ROW["e_norm"])
    pl.step("setup_gains")
    W = "e_w_in"
    evs = [pl.panel(W, 0, CW, "x", "norm", gs=64, dst=("g0", 0))]
    stm = pl.norm_rows("h", "h", ("loaded_h", 16))
    evs += [pl.panel(W, 1024, CW, "x", "norm", gs=64, dst=("g0", 1)),
            pl.panel(W, 2048, CW, "x", "copy", dst=("g0", 2))]
    pl.transposed("h", stm.on["rows_ready"], "side", ROW["e_mem"])
    b = heads("A", "g0", evs, pl.pos, 4, 0)
    pl.panel(W, 3072, CW, "x", "gate", "col", tile=0)
    evs = [pl.panel(W, 512, CW, "x", "norm", gs=64, dst=("g1", 0)),
           pl.panel(W, 1536, CW, "x", "norm", gs=64, dst=("g1", 1)),
           pl.panel(W, 2560, CW, "x", "copy", dst=("g1", 2))]
    b = heads("A", "g1", evs, max(b, pl.pos), 4, 4)
    m = pl.pos
    for chunk in (6, 7, 8, 9, 0, 1, 2, 3):
        m = pl.mod(m, chunk, ctx=chunk < 4)
    pl.panel(W, 3584, CW, "x", "gate", "col", tile=4)
    evs = [pl.panel(W, 6144, CW, "x", "norm", gs=128, dst=("g0", 0)),
           pl.panel("e_w_mem_kv", 0, CW, "side", "norm", gs=128, dst=("g0", 1)),
           pl.panel("e_w_mem_kv", CW, CW, "side", "copy", dst=("g0", 2))]
    b = heads("X", "g0", evs, max(b, pl.pos), 4, 12, gain="ex")
    pl.panel(W, 6656, CW, "x", "gate", "col", tile=12)
    ch = pl.panel(W, 4096, CW, "x", "conv_h", "col")
    pl.transposed("h", stm.on["rows_ready"], "side", ROW["o_mem"])
    pl.load("x", rows=pl.count["rt_ps"])
    pl.panel(W, 4608, CW, "x", "conv_c", "col", h_evac=ch.on["v_evac"])
    pl.step("conv_taps")
    pl.panel(W, 5120, CW, "x", "conv_b", "col")
    ev = pl.panel(W, 5632, CW, "x", "conv_z", "col", tile=8)
    st = pl.step("conv", gate=ev.on["gate_ready"], v_evac=pl.count["v_evac"])
    pl.tick(st, "ytmp_ready", "yhi_ready", "y_ready")
    for k in range(8, 12):
        pl.tile_ready[k] = st.on["y_ready"]
    for c in range(2):
        pl.panel("e_w_out", c * CW, CW, "y", "resid", kts=EVEN_Y // P, c=c, order=[(0, 8), (12, 16), (8, 12)])
    assert not any(pl.pending.values())

    st = pl.norm_rows("h", "gates", *pl.residual())
    evs = [pl.panel("o_w_mem_kv", CW, CW, "side", "copy", dst=("g1", 2))]
    pl.transposed("gates", st.on["rows_ready"], "x", ROW["o_norm"])
    evs.append(pl.panel("o_w_mem_kv", 0, CW, "side", "norm", gs=128, dst=("g1", 1)))
    pl.tile_ready = {}
    W = "o_w_in"
    pl.panel(W, 6144, 12, "x", "forget")
    pl.step("forget_log")

    def forget_sum():
        st = pl.step("forget_sum")
        pl.tick(st, "logf_ready", "cum_ps", "cum_sb", "cum_sb2", "cum_out")
        pl.uses(st, "o", "cum_sb2")
    pl.at(pl.pos, forget_sum)
    evs.append(pl.panel(W, 6156, CW, "x", "norm", gs=128, dst=("g1", 0)))
    b = heads("X", "g1", evs, pl.pos, 4, 12, gain="ox")
    pl.panel(W, 6668, CW, "x", "gate", "col", tile=12)
    for g in range(3):
        buf = ("g2", "g0", "g1")[g]
        evs = [pl.panel(W, CW * g, CW, "x", "norm", gs=128, dst=(buf, 0))]
        if g == 2:
            assert not pl.pending["g2"]
            pl.load("ctx", after=pl.count["o_ps"])
            pl.load("rope", after=pl.count["o_ps"])
        evs.append(pl.panel(W, 1536 + CW * g, CW, "x", "norm", gs=128, dst=(buf, 1)))
        if g == 2:
            st = pl.norm_rows("g2", "g2", ("loaded_ctx", 16))
            pl.step("rope_tables")
        evs.append(pl.panel(W, 3072 + CW * g, CW, "x", "copy", dst=(buf, 2)))
        if g == 2:
            assert set(range(4)) <= set(pl.chunks)
            pl.step("mod_cols", which="mix", mod_sb=pl.count["mod_sb"])
            pl.transposed("g2", st.on["rows_ready"], "side", "ctx_A", "ctx_B")
        masked = {}

        def make_rows(g=g, masked=masked):
            s = pl.step("forget_rows", g=g, prev=pl.count.get("s_rd", 0))
            pl.tick(s, "rows_in", "mask0", "mask1")
            masked["mask1"] = s.on["mask1"]
        b = max(b, pl.pos)
        pl.at(b - 1, make_rows)
        b = heads("C", buf, evs, b, 4, 4 * g, gap=3 if g == 2 else 4, rows=masked)
        pl.panel(W, 4608 + CW * g, CW, "x", "gate", "col", tile=4 * g)
    assert not pl.pending["g0"]
    pl.load("post_mix", after=pl.count["o_ps"])
    pl.mod(pl.mod(pl.pos + 4, 4, gate=True), 5, gate=True)
    V = "w_in_2"
    pl.panel(V, 512, 256, "side", "ctxkv")
    outs = [pl.panel("o_w_out", c * CW, CW, "y", "resid", kts=ODD_Y // P, c=c, opened=True) for c in range(2)]
    for c, a, e in ((0, 12, 16), (0, 0, 8), (1, 12, 16), (0, 8, 12), (1, 0, 12)):
        pl.parts(outs[c].panel, a, e)
    assert not any(pl.pending.values())

    pl.load("ret", after=pl.count["o_ps"])
    st = pl.norm_rows("h", "gates", *pl.residual())
    pl.step("decays")
    pl.panel(V, 1280, CW, "side", "copy", dst=("g2", 0))
    pl.transposed("gates", st.on["rows_ready"], "x", "mix_A", "mix_B")
    pl.tile_ready = {}
    q = pl.panel(V, 0, CW, "x", "normrope")
    pl.panel(V, 1792, CW, "side", "copy", dst=("g2", 1))
    v_evac = pl.count["v_evac"]

    def ctx_state():
        st = pl.step("ctx_state", v_evac=v_evac)
        pl.tick(st, "kfb_ready", "state_ps", "state_sb")
        pl.uses(st, "o", "state_sb")
    pl.at(pl.pos + 2, ctx_state)
    lat = pl.panel(V, 512, 256, "x", "latkv")

    def gqa_kT():
        st = pl.step("gqa_kT", ready=[("rope_done", lat.on["rope_done"])])
        pl.tick(st, "kT_ps", "kT_sb")
        pl.uses(st, "tp", "kT_sb")
    pl.at(pl.pos + 1, gqa_kT)
    ready = [("rope_done", q.on["rope_done"]), ("v_evac", lat.on["v_evac"])]
    gqa = []
    for j in range(4):
        for part in range(2):
            hd = part * 4 + j
            gqa.append(Head("G", "g0", j, hd // 2, ready, part=part, base=(hd % 2) * 64, kT_sb=1))
    pl.grouped(gqa, pl.pos + 2)
    rq = [pl.panel(V, 768, CW, "x", "rope", dst=("g1", 0)),
          pl.panel(V, 1280, CW, "x", "rope", dst=("g1", 1)),
          pl.panel(V, 1792, CW, "x", "copy", dst=("g1", 2))]
    ret_out = retention(pl, rq, pl.pos)
    pl.panel(V, 2304, CW, "x", "gate", "col", tile=4)
    outs = [pl.panel("w_out_2", c * CW, CW, "y", "mix", kts=MIX_Y // P, c=c, which=0, mod_sb=pl.count["mod_sb"],
                     opened=True) for c in range(2)]
    for o in outs:
        pl.parts(o.panel, 0, 4)
    pl.flush()
    for o in outs:
        pl.parts(o.panel, 4, 6)
    ret_out()
    for o in outs:
        pl.parts(o.panel, 6, 8)
    assert set(pl.chunks) == set(range(10))
    pl.tile_ready = {}
    st = pl.step("post", sq_ready=pl.count["sq_ready"], v_evac=pl.count["v_evac"])
    pl.tick(st, "ms_ready", "rstd_ready", "post_done", "post_done")
    pl.load("post_ffn", after=pl.count["o_ps"])
    st = pl.norm_rows("h", "gates", *pl.residual())
    pl.step("mod_cols", which="ffn", mod_sb=pl.count["mod_sb"])
    pl.transposed("gates", st.on["rows_ready"], "x", "ffn_A", "ffn_B")
    pl.mod(pl.mod(pl.pos + 8, 10, gate=True), 11, gate=True)
    for j in range(0, FFN, CW):
        n = min(CW, FFN - j)
        slot = (j // CW) % 2
        a = pl.panel("w_ffn_in", j, n, "x", "ffa", "col", tile=4 * slot)
        pl.panel("w_ffn_in", FFN + j, n, "x", "ffb", "col", gate_tile=4 * slot, gate=a.on["gate_ready"],
                 tiles=list(range(j // P, (j + n) // P)))
    for c in range(2):
        pl.panel("w_ffn_out", c * CW, CW, "y", "mix", kts=FFN // P, c=c, which=1, mod_sb=pl.count["mod_sb"])
    st = pl.step("post", sq_ready=pl.count["sq_ready"], v_evac=pl.count["v_evac"])
    pl.tick(st, "ms_ready", "rstd_ready", "post_done", "post_done")
    return finish(pl)


def retention(pl, rq, pos):
    ready = [("rope_done", rq[1].on["rope_done"]), ("v_evac", rq[2].on["v_evac"])]
    qfb = {}
    decay, score, out = {}, {}, {}

    def ret_q():
        st = pl.step("ret_q", rope_done=pl.count["rope_done"])
        pl.tick(st, "qfb_ready")
        qfb["ready"] = st.on["qfb_ready"]

    def ret_decay(h):
        st = decay[h] = pl.step("ret_decay", h=h)
        st.am_read = score[h - 2].on["am_ready"] if h >= 2 else 0
        pl.tick(st, "m_arg", "m_exp", "m_ready")

    def beside(h):
        if h < 8 and h % 2 == 0:
            a = pl.step("ret_T", h=h, prev_s=pl.count["s_ps"], ready=ready)
            pl.tick(a, "qkT_ps", "qkT_sb")
            pl.uses(a, "tp", "qkT_sb")
            qkT_sb = a.on["qkT_sb"]
            qfb["qkT"] = qkT_sb
        if h > 0:
            o = out[h - 1] = pl.step("ret_pv", h=h - 1, am_ready=score[h - 1].on["am_ready"], qkT_sb=qfb["T2"])
            pl.tick(o, "o_ps", "ret_sb")
            pl.uses(o, "o", "ret_sb")
        if h < 8 and h % 2 == 0:
            a = pl.step("ret_T2", h=h, prev_o=pl.count["o_ps"], qfb=qfb["ready"])
            pl.tick(a, "qkT_ps", "qkT_sb")
            qfb["T2"] = a.on["qkT_sb"]
            pl.uses(a, "tp", "qkT_sb")
        if h < 8:
            prev_o = out[h - 2].on["o_ps"] if h >= 2 else pl.count["o_ps"]
            s = score[h] = pl.step("ret_scores", h=h, prev_o=prev_o, qkT_sb=qfb["qkT"], m_ready=decay[h].on["m_ready"])
            pl.tick(s, "s_ps", "am_ready")
            pl.uses(s, f"s{h % 2}", "am_ready")
        if h + 2 < 8:
            ret_decay(h + 2)

    def ret_norm(half):
        st = pl.step("ret_norm", half=half, ret_sb=pl.count["ret_sb"])
        pl.tick(st, "ret_mid", "sq_ready", "ms_ready", "rstd_ready", "rn_ready")
        pl.uses(st, "scr", "sq_ready")

    def ret_out(half):
        st = pl.step("ret_out", half=half, gate_ready=pl.gated[4])
        st.on["rn_ready"] = half + 1
        pl.tick(st, "rt_ps", "ytmp_ready", "yhi_ready", "y_ready")
        pl.uses(st, "tp", "ytmp_ready")
        pl.uses(st, "scr", "y_ready")
        for k in (4 + 2 * half, 5 + 2 * half):
            pl.tile_ready[k] = st.on["y_ready"]
    ret_decay(0)
    ret_decay(1)
    ret_q()
    for h in range(9):
        pl.at(pos + h, lambda h=h: beside(h))
        if h % 4 == 0 and h > 0:
            pl.at(pos + h, lambda h=h: ret_norm(h // 4 - 1), 2)
    pl.at(pos + 6, lambda: ret_out(0), 2)
    return lambda: ret_out(1)


PASSABLE = ("sub", "split", "evac_norm", "evac_copy", "evac_gate", "evac_conv_h", "evac_conv_c", "evac_conv_b",
            "evac_conv_z", "qkT", "scores", "PT", "pv", "oT", "forget_rows", "mod", "mod_out", "load", "exps")


def late_halves(steps):
    out, held = [], []
    for st in steps:
        if st.kind == "split":
            out.append(st)
            held = [(n - 1, kind, x) for n, kind, x in held]
        rest = []
        for n, kind, x in held:
            needed = st.kind not in PASSABLE or (st.kind in ("PT", "oT") and x.h and x.h is st.h)
            if n == 0 or needed:
                out.append(Step(kind, first=x))
            else:
                rest.append((n, kind, x))
        held = rest
        if st.kind != "split":
            out.append(st)
        if st.kind == "evac_norm":
            held.append((2, "late_half", st))
        elif st.kind == "scores" and st.h.type != "G":
            held += [(1, "late_exp", st), (1, "late_half", st)]
        elif st.kind in ("scores", "evac_rope", "evac_normrope") or (st.kind == "pv" and st.h.type == "A"):
            held.append((1, "late_half", st))
    return out + [Step(kind, first=x) for _, kind, x in held]


def finish(pl):
    out = []
    n = len(pl.subs)
    made = 0

    def split():
        nonlocal made
        if made < n:
            out.append(Step("split", sub=pl.subs[made]))
            made += 1
    for st in pl.steps:
        if st.kind == "sub":
            while made <= st.sub.i + LEAD and made < n:
                split()
        if st.kind == "mod" and st.part == 0 and made < n and pl.subs[made].k0 % RAWK:
            split()
        out.append(st)
        if st.kind == "setup_gains" and made == 0 or (st.kind == "rows_norm" and made == 0):
            split()
            split()
    out = late_halves(out)
    raws = []
    for st in out:
        if st.kind == "split":
            sub = st.sub
            if sub.k0 % RAWK == 0:
                nk = min(RAWK, sub.panel.kts - sub.k0)
                raws.append(Load(len(raws), sub.panel.w, sub.k0 * P, nk, sub.panel.col, sub.panel.ncols, None))
                sub.panel.load = raws[-1]
            sub.raw = sub.panel.load
            sub.raw.read = ("lo_ready", sub.i + 1)
            sub.koff = sub.k0 % RAWK
        elif st.kind == "mod":
            if st.part == 0:
                mod_load = Load(len(raws), "w_mod", st.u * RAWK * P, RAWK, st.chunk * CW, CW, None)
                raws.append(mod_load)
            st.raw = mod_load
            st.raw.read = ("mod_read", st.on["mod_read"])
    pl.steps, pl.raws = out, raws
    return pl



SEMS = """raw_loaded0 raw_loaded1 raw_loaded2 loaded_rows loaded_first loaded_x0 loaded_x1 loaded_h loaded_x
loaded_ctx loaded_rope loaded_ret loaded_post_mix loaded_post_ffn hi_ready lo_ready sub_done mod_read
mod_ps mod_sb sq_ready ms_ready rstd_ready rows_ready rt_ps rt_hi rt_lo rt_tmp qk_evac v_evac tanh_ready
gate_ready conv_u resid_done forget_in rope_done norm_mid ytmp_ready yhi_ready y_ready qkT_ps qkT_sb
s_ps s_rd mx_ready exp_ready p_ready PT_ps PT_sb o_ps on_ready oT_ps logf_ready logf_e cum_ps cum_sb
cum_sb2 cum_out rows_in mask0 mask1 kfb_ready state_ps state_sb kT_ps kT_sb qfb_ready m_arg m_exp
m_ready am_ready ret_sb ret_mid rn_ready post_done cols_ps cols_sb gains_ready lam_in lam_exp tanh_c
lg_exp dec_arg dec_exp setup_pool bias_in bias_done logf_a taps_done dve_chain act_chain stored""".split()


def program(nc, w, out):
    first_c, ret_c, rope_c = constants()
    pl = make_plan()
    ctx = ExitStack()
    with ctx:
        place = [(nc.sbuf_base + 31) // 32 * 32]

        def sb(name, shape, dtype=F32, at=None):
            off = place[0] if at is None else at
            t = nc.alloc_sbuf_tensor_at(name, shape, dtype, offset=off)
            if at is None:
                place[0] += (int(np.prod(shape[1:])) * 4 + 31) // 32 * 32
            return t

        raw = sb("raw", [P, RAW_SLOTS, RAWK, CW])
        whi = sb("whi", [P, SPLIT_SLOTS, SUBK, CW], F32R)
        wlo = sb("wlo", [P, SPLIT_SLOTS, SUBK, CW], F32R)
        xhi, xlo = (sb(n, [P, KT, T], F32R) for n in ("xhi", "xlo"))
        shi, slo = (sb(n, [P, KT, T], F32R) for n in ("shi", "slo"))
        yhi, ylo = (sb(n, [P, 16, T], F32R) for n in ("yhi", "ylo"))
        g2_at = place[0]
        g2 = sb("g2", [P, 3072])
        zhi = sb("zhi", [P, 6, T], F32R, at=g2_at)
        zlo = sb("zlo", [P, 6, T], F32R, at=g2_at + 6 * T * 4)
        g0, g1 = sb("g0", [P, 3072]), sb("g1", [P, 3072])
        gates = sb("gates", [P, 16, T])
        h_res = sb("h_res", [P, NT, D])
        pbuf = sb("pbuf", [P, 768])
        ptb = sb("ptb", [P, 512])
        qkT = sb("qkT", [P, 2, T])
        ytmp = sb("ytmp", [P, T])
        scr = sb("scr", [P, 1024])
        macc = sb("macc", [P, 2, CW])
        nc_at = place[0]
        negcum = sb("negcum", [P, 4, T])
        negcum0 = sb("negcum0", [P, 4, P])
        rett = sb("rett", [P, 3, 512], at=nc_at)
        ytok = sb("ytok", [P, T], at=nc_at)
        nfirst = first_c.shape[1]
        cst = sb("cst", [P, nfirst])
        rows1, rows2 = macc[:, 0, 0:P], macc[0:9, 0, P:2 * P]
        cols = sb("cols", [P, P + 9])
        gain = {n: sb("gain_" + n, [P, 1]) for n in ("A", "ex", "C", "ox", "aon")}
        neglam = sb("neglam", [P, 1])
        lam_rows = ptb[:, 0:256]
        scol = sb("scol", [P, 16])
        modc = sb("modc", [P, 2, 48])
        mcol = {n: sb("mc_" + n, [P, 8]) for n in ("mix_A", "ctx_A", "ffn_A")}
        small = sb("small", [P, 9, 16])
        half_neg = sb("half_neg", [P, 16])
        mixsq = sb("mixsq", [P, 2, NT])
        nmx, rsum, rinv = sb("nmx", [P, 4]), sb("rsum", [P, 4]), sb("rinv", [P, 4])
        vecs = sb("vecs", [P, 28])
        fbb, lg = vecs[:, 0:12], vecs[:, 12:28]
        fx, fe, logf = sb("fx", [P, NT, 12]), sb("fe", [P, NT, 12]), sb("logf", [P, NT, 12])
        cumq = sb("cumq", [P, NT, 12])
        cumT = g2[0:12, 2048:2048 + T]
        dec = sb("dec", [P, 4, NT, 8])
        assert place[0] <= nc.sbuf_usable_end, place[0] - nc.sbuf_usable_end
        scratch = nc.dram_tensor("cum_scratch", (12, T), F32, kind="Internal").ap()

        groups = {"g0": g0, "g1": g1, "g2": g2}

        def grp(name, part):
            return groups[name][:, part * 1024:(part + 1) * 1024]

        def const(name, a=0, b=None):
            at, n = CONST[name]
            return cst[:, at + a:at + (n if b is None else b)]

        ident = const("ident")
        ones = const("tri", P, 2 * P)
        gflat = gates[:, :, :].rearrange("p k t -> p (k t)")
        rows_of = {"g0": g0[:, 0:2048].rearrange("p (t d) -> p t d", t=NT), "h": h_res[:, :, :],
                   "g2": g2[:, 0:2048].rearrange("p (t d) -> p t d", t=NT),
                   "gates": gflat[:, 0:2048].rearrange("p (t d) -> p t d", t=NT)}
        p2 = gflat[:, 2048:3072].rearrange("p (t k) -> p t k", t=NT)
        pt2 = gflat[:, 3072:4096].rearrange("p (k t) -> p k t", t=T)
        kfb = gflat[:, 2048:4096].rearrange("p (t h f d) -> p t h f d", t=NT, h=8, f=2)
        dmat = gflat[:, 0:1024].rearrange("p (s n) -> p s n", s=2)
        qfb = g2[:, 0:2048].rearrange("p (t h f d) -> p t h f d", t=NT, h=8, f=2)
        ropes = {n: g2[:, 2048 + 256 * i:2304 + 256 * i].rearrange("p (c t d) -> p c t d", c=2, t=NT)
                 for i, n in enumerate(("ret", "q", "k"))}
        growb = g2[:, 2816:2944]
        kT2 = ptb
        sfb = pbuf[:, 0:512].rearrange("p (h d) -> p h d", h=8)
        qfbT = gflat[:, 2048:2560].rearrange("p (h t) -> p h t", h=2)
        am = gflat[:, 3072:4096].rearrange("p (s n) -> p s n", s=2)
        ret = g0[:, 0:1024].rearrange("p (t n) -> p t n", t=NT)
        lat_k, lat_v = (g0[:, 1024 + 256 * i:1280 + 256 * i].rearrange("p (t d) -> p t d", t=NT) for i in (0, 1))
        ctx_k, ctx_v = (g0[:, 1536 + 256 * i:1792 + 256 * i].rearrange("p (t d) -> p t d", t=NT) for i in (0, 1))
        mixed = g0[:, 0:2048].rearrange("p (t d) -> p t d", t=NT)
        post_gain = (g0[:, 2048:3072], g1[:, 0:1024])

        acc = ctx.enter_context(nc.psum_tensor("acc", [P, 4, CW], F32))
        spsum = ctx.enter_context(nc.psum_tensor("spsum", [P, 2, CW], F32))
        tp = ctx.enter_context(nc.psum_tensor("tp", [P, CW], F32))
        opsum = ctx.enter_context(nc.psum_tensor("opsum", [P, CW], F32))
        S = {n: ctx.enter_context(nc.semaphore(n)) for n in SEMS}

        def acc2(a, n=CW):
            return acc[:, 2 * a:2 * a + 2, 0:n]

        def acct(a, n=4):
            return acc[:, 2 * a:2 * a + 2, :].rearrange("p b (c t) -> p (b c) t", t=T)[:, 0:n, :]

        def operand(src, k):
            if src == "x":
                return xhi[:, k, :], xlo[:, k, :]
            if src == "side":
                return shi[:, k, :], slo[:, k, :]
            return (yhi[:, k, :], ylo[:, k, :]) if k < 16 else (zhi[:, k - 16, :], zlo[:, k - 16, :])

        def y_part(k0, n, lo, p0=0, p1=P):
            t = ((yhi, zhi), (ylo, zlo))[lo][k0 >= 16]
            return t[p0:p1, k0 % 16:k0 % 16 + n, :]

        def scale_cols(key):
            if isinstance(key, int):
                return cols[:, key:key + 8]
            return {"mix_A": mcol["mix_A"][:, :], "ctx_A": mcol["ctx_A"][:, :], "ffn_A": mcol["ffn_A"][:, :],
                    "mix_B": modc[:, 0, 0:8], "ctx_B": modc[:, 1, 0:8], "ffn_B": modc[:, 0, 24:32]}[key]

        def heads_of(ap, n, d):
            return ap.rearrange("p (h d) -> p h d", h=n)

        def across(ap, shape):
            return ap.unsqueeze(len(shape) - 1).to_broadcast(shape)

        block = ctx.enter_context(nc.Block())

        @block.sync
        def _(sp):
            for t in range(NT):
                sp.dma_start(rows_of["g0"][:, t, :], w["x"][0, t * P:(t + 1) * P, :]).then_inc(S[f"loaded_x{t}"], 16)
            for r in pl.raws:
                if r.i >= RAW_SLOTS:
                    sem, n = pl.raws[r.i - RAW_SLOTS].read
                    sp.wait_ge(S[sem], n)
                src = w[r.w][r.row:r.row + r.nk * P, r.col:r.col + r.ncols].rearrange("(k p) n -> p k n", p=P)
                sp.dma_start(raw[:, r.i % RAW_SLOTS, 0:r.nk, 0:r.ncols], src)\
                    .then_inc(S[f"raw_loaded{r.i % RAW_SLOTS}"], 16)
            for t in range(NT):
                sp.wait_ge(S["post_done"], pl.count["post_done"] - (NT - 1 - t))
                sp.dma_start(out[0, t * P:(t + 1) * P, :], h_res[:, t, :]).then_inc(S["stored"], 16)
            sp.wait_ge(S["stored"], 16 * NT)

        def raw_wait(eng, r):
            eng.wait_ge(S[f"raw_loaded{r.i % RAW_SLOTS}"], 16 * (r.i // RAW_SLOTS + 1))

        @block.tensor
        def _(pe):
            mm, tr = nc.tensor.matmul, nc.tensor.transpose

            def wait(pair):
                if pair:
                    pe.wait_ge(S[pair[0]], pair[1])

            def sub(st):
                s, pan = st.sub, st.sub.panel
                for pair in s.waits:
                    wait(pair)
                pe.wait_ge(S["lo_ready"], s.i + 1)
                slot = s.i % SPLIT_SLOTS
                last = None
                if pan.orient == "tok":
                    for t in range(NT):
                        o = acc[:, 2 * pan.acc + t, 0:pan.ncols]
                        for k in range(s.nk):
                            hi, lo = operand(pan.src, s.k0 + k)
                            a, z = s.first and k == 0, s.last and k == s.nk - 1
                            hi, lo = hi[:, t * P:(t + 1) * P], lo[:, t * P:(t + 1) * P]
                            mm(o, hi, whi[:, slot, k, 0:pan.ncols], start=a, stop=False)
                            mm(o, hi, wlo[:, slot, k, 0:pan.ncols], start=False, stop=False)
                            last = mm(o, lo, whi[:, slot, k, 0:pan.ncols], start=False, stop=z)
                else:
                    for c in range(pan.ncols // P):
                        o = acct(pan.acc)[:, c, :]
                        for k in range(s.nk):
                            hi, lo = operand(pan.src, s.k0 + k)
                            a, z = s.first and k == 0 and c % 2 == 0, s.last and k == s.nk - 1
                            wh, wl = (t[:, slot, k, c * P:(c + 1) * P] for t in (whi, wlo))
                            mm(o, wh, hi, start=a, stop=False, skip_group_check=True)
                            mm(o, wl, hi, start=False, stop=False, skip_group_check=True)
                            last = mm(o, wh, lo, start=False, stop=z, skip_group_check=True)
                last.then_inc(S["sub_done"], 1)

            def setup(st):
                pe.wait_ge(S["loaded_rows"], 16 * 3)
                tr(tp[:, 0:P], rows1, ident)
                mm(tp[:, P:P + 9], rows2, ident[0:9, 0:9], is_transpose=True).then_inc(S["cols_ps"], 1)

            def rows_T(st):
                wait(st.free["acc"])
                pe.wait_ge(S["rows_ready"], st.ready)
                for k in range(4):
                    for t in range(NT):
                        kk = 4 * st.half + k
                        last = tr(acct(st.acc)[:, k, t * P:(t + 1) * P],
                                  rows_of[st.xn][:, t, kk * P:(kk + 1) * P], ident)
                last.then_inc(S["rt_ps"], 1)

            def qkT_(st):
                h = st.h
                wait(st.free["tp"])
                for pair in h.ready:
                    wait(pair)
                q, k = (grp(h.g, i).rearrange("p (t n) -> p t n", t=NT) for i in (0, 1))
                for t in range(NT):
                    last = tr(tp[:, t * P:(t + 1) * P], q[:, t, h.j * P:(h.j + 1) * P], ident)
                if h.type != "G":
                    for t in range(NT):
                        last = tr(tp[:, T + t * P:T + (t + 1) * P], k[:, t, h.j * P:(h.j + 1) * P], ident)
                last.then_inc(S["qkT_ps"], 1)

            def scores(st):
                h = st.h
                pe.wait_ge(S["qkT_sb"], st.qkT_sb)
                for b in h.banks:
                    wait(st.free[b])
                if h.type in "AC":
                    for half in range(2 if h.type == "A" else 1):
                        p0, p1 = (half * 64, half * 64 + 64) if h.type == "A" else (0, P)
                        bank = spsum[:, half if h.type == "A" else h.n % 2, :]
                        q, k = qkT[p0:p1, 0, :], qkT[p0:p1, 1, :]
                        mm(bank[:, 0:P], q[:, 0:P], k[:, 0:P], start=True, stop=True)
                        last = mm(bank[:, P:P + T], q[:, P:T], k, start=True, stop=True)
                elif h.type == "X":
                    for t in range(NT):
                        last = mm(spsum[:, h.n % 2, t * T:(t + 1) * T], qkT[:, 0, t * P:(t + 1) * P], qkT[:, 1, :],
                                  start=True, stop=True)
                else:
                    p0 = h.part * 64
                    pe.wait_ge(S["kT_sb"], h.kT_sb)
                    for t in range(NT):
                        last = mm(spsum[:, t, :], qkT[p0:p0 + 64, 0, t * P:(t + 1) * P], kT2[p0:p0 + 64, :],
                                  start=True, stop=True)
                last.then_inc(S["s_ps"], 1)

            def PT(st):
                h = st.h
                pe.wait_ge(S["p_ready"], st.p_ready)
                wait(st.free["tp"])
                if h.type in "AC":
                    blocks = [pbuf[:, 0:P], pbuf[:, P:2 * P], pbuf[:, 2 * P:3 * P]]
                elif h.type == "X":
                    blocks = [pbuf[:, t * T + k * P:t * T + (k + 1) * P] for k in range(2) for t in range(NT)]
                else:
                    blocks = [p2[:, t, k * P:(k + 1) * P] for k in (2 * st.part, 2 * st.part + 1) for t in range(NT)]
                for i, b in enumerate(blocks):
                    last = tr(tp[:, i * P:(i + 1) * P], b, ident)
                last.then_inc(S["PT_ps"], 1)

            def pv(st):
                h = st.h
                pe.wait_ge(S["PT_sb"], st.PT_sb)
                wait(st.free["o"])
                for pair in h.ready:
                    wait(pair)
                if h.type == "G":
                    for k in range(4):
                        v = (ctx_v, lat_v)[k // 2][:, k % 2, h.part * 64:h.part * 64 + 64]
                        last = mm(opsum[h.base:h.base + 64, 0:T], v, pt2[:, k, :], start=k == 0, stop=k == 3)
                else:
                    v = grp(h.g, 2).rearrange("p (t n) -> p t n", t=NT)[:, :, h.j * P:(h.j + 1) * P]
                    if h.type == "A":
                        mm(opsum[:, 0:P], ptb[:, 0:P], v[:, 0, :], start=True, stop=True)
                        mm(opsum[:, P:T], ptb[:, P:T], v[:, 0, :], start=True, stop=False)
                        last = mm(opsum[:, P:T], ptb[:, T:T + P], v[:, 1, :], start=False, stop=True)
                    elif h.type == "C":
                        mm(opsum[:, 0:P], v[:, 0, :], ptb[:, 0:P], start=True, stop=True)
                        mm(opsum[:, P:T], v[:, 0, :], ptb[:, P:T], start=True, stop=False)
                        last = mm(opsum[:, P:T], v[:, 1, :], ptb[:, T:T + P], start=False, stop=True)
                    else:
                        mm(opsum[:, 0:T], v[:, 0, :], ptb[:, 0:T], start=True, stop=False)
                        last = mm(opsum[:, 0:T], v[:, 1, :], ptb[:, T:2 * T], start=False, stop=True)
                last.then_inc(S["o_ps"], 1)

            def oT(st):
                pe.wait_ge(S["on_ready"], st.on_ready)
                wait(st.free["tp"])
                tr(tp[:, 0:P], ytok[:, 0:P], ident)
                tr(tp[:, P:T], ytok[:, P:T], ident).then_inc(S["oT_ps"], 1)

            def mod_out(st):
                pe.wait_ge(S["mod_read"], st.mod_read)
                wait(st.free["tp" if st.gate else "o"])
                if st.gate:
                    pe.wait_ge(S["bias_done"], st.bias_done)
                    mm(tp[:, :], ones, macc[:, 0, :], start=True, stop=True).then_inc(S["mod_ps"], 1)
                    return
                for v in range(2 if st.ctx else 1):
                    for i in range(4):
                        last = mm(opsum[:, v * 4 + i:v * 4 + i + 1], macc[:, v, i * P:(i + 1) * P], ones[:, 0:1],
                                  start=True, stop=True)
                last.then_inc(S["mod_ps"], 1)

            def forget_sum(st):
                pe.wait_ge(S["logf_ready"], st.on["logf_ready"])
                wait(st.free["o"])
                tri, f0, f1 = const("tri"), logf[:, 0, :], logf[:, 1, :]
                mm(opsum[:, 0:12], tri[:, 0:P], f0, start=True, stop=True)
                mm(opsum[:, 12:24], ones, f0, start=True, stop=False)
                mm(opsum[:, 12:24], tri[:, 0:P], f1, start=False, stop=True)
                mm(opsum[0:12, 64:64 + T], f0, tri, start=True, stop=False, skip_group_check=True)
                mm(opsum[0:12, 64 + P:64 + T], f1, tri[:, 0:P], start=False, stop=True, skip_group_check=True)\
                    .then_inc(S["cum_ps"], 1)

            def ctx_state(st):
                pe.wait_ge(S["kfb_ready"], st.on["kfb_ready"])
                wait(st.free["o"])
                v = grp("g2", 1).rearrange("p (t n) -> p t n", t=NT)
                for h in range(8):
                    for t in range(NT):
                        last = mm(opsum[:, h * 64:(h + 1) * 64], kfb[:, t, h, :, :], v[:, t, h * 64:(h + 1) * 64],
                                  start=t == 0, stop=t == NT - 1)
                last.then_inc(S["state_ps"], 1)

            def gqa_kT(st):
                for pair in st.ready:
                    wait(pair)
                wait(st.free["tp"])
                for i, k in enumerate((ctx_k[:, 0, :], ctx_k[:, 1, :], lat_k[:, 0, :], lat_k[:, 1, :])):
                    last = tr(tp[:, i * P:(i + 1) * P], k, ident)
                last.then_inc(S["kT_ps"], 1)

            def ret_T(st):
                wait(st.free["tp"])
                for pair in st.ready:
                    wait(pair)
                for i in (0, 1):
                    src = grp("g1", i).rearrange("p (t n) -> p t n", t=NT)
                    for t in range(NT):
                        last = tr(tp[:, i * T + t * P:i * T + (t + 1) * P], src[:, t, st.h * 64:st.h * 64 + P], ident)
                last.then_inc(S["qkT_ps"], 1)

            def ret_T2(st):
                wait(st.free["tp"])
                pe.wait_ge(S["qfb_ready"], st.qfb)
                for i in (0, 1):
                    for t in range(NT):
                        last = tr(tp[:, i * T + t * P:i * T + (t + 1) * P], qfb[:, t, st.h + i, :, :], ident)
                last.then_inc(S["qkT_ps"], 1)

            def ret_scores(st):
                pe.wait_ge(S["qkT_sb"], st.qkT_sb)
                wait(st.free[f"s{st.h % 2}"])
                p0 = (st.h % 2) * 64
                for j in range(NT):
                    last = mm(spsum[:, st.h % 2, j * T:(j + 1) * T], qkT[p0:p0 + 64, 1, j * P:(j + 1) * P],
                              qkT[p0:p0 + 64, 0, :], start=True, stop=True)
                last.then_inc(S["s_ps"], 1)

            def ret_pv(st):
                pe.wait_ge(S["am_ready"], st.am_ready)
                pe.wait_ge(S["qkT_sb"], st.qkT_sb)
                wait(st.free["o"])
                v = grp("g1", 2).rearrange("p (t n) -> p t n", t=NT)[:, :, st.h * 64:(st.h + 1) * 64]
                for i in range(NT):
                    o = opsum[:, i * 64:(i + 1) * 64]
                    for j in range(NT):
                        mm(o, am[:, st.h % 2, j * T + i * P:j * T + (i + 1) * P], v[:, j, :], start=j == 0, stop=False)
                    last = mm(o, qfbT[:, st.h % 2, i * P:(i + 1) * P], sfb[:, st.h, :], start=False, stop=True)
                last.then_inc(S["o_ps"], 1)

            def ret_out(st):
                pe.wait_ge(S["rn_ready"], st.on["rn_ready"])
                wait(st.free["tp"])
                for k in range(2):
                    for t in range(NT):
                        kk = 2 * st.half + k
                        last = tr(tp[:, k * T + t * P:k * T + (t + 1) * P], ret[:, t, kk * P:(kk + 1) * P], ident)
                last.then_inc(S["rt_ps"], 1)

            does = {"sub": sub, "setup": setup, "rows_T": rows_T, "qkT": qkT_, "scores": scores, "PT": PT, "pv": pv,
                    "oT": oT, "mod_out": mod_out, "forget_sum": forget_sum, "ctx_state": ctx_state,
                    "gqa_kT": gqa_kT, "ret_T": ret_T, "ret_T2": ret_T2, "ret_scores": ret_scores, "ret_pv": ret_pv,
                    "ret_out": ret_out}
            for st in pl.steps:
                if st.kind in does:
                    does[st.kind](st)

        @block.scalar
        def _(act):
            f = nc.scalar.activation
            chain = [0]
            n_id = CONST["ident"][1]
            act.dma_start(macc[:, 0, 0:P], w["vec_rows"][0:P, :]).then_inc(S["loaded_rows"], 16)
            act.dma_start(cst[:, 0:n_id], w["const_first"][:, 0:n_id]).then_inc(S["loaded_rows"], 16)
            act.dma_start(macc[0:9, 0, P:2 * P], w["vec_rows"][P:P + 9, :]).then_inc(S["loaded_rows"], 16)
            act.dma_start(lam_rows, w["vec_all"][:, 0:256].to_broadcast([P, 256])).then_inc(S["loaded_first"], 16)
            act.dma_start(vecs[:, :], w["vec_all"][:, 256:284].to_broadcast([P, 28])).then_inc(S["loaded_first"], 16)
            act.dma_start(cst[:, n_id:nfirst], w["const_first"][:, n_id:nfirst]).then_inc(S["loaded_first"], 16)

            def wait(pair):
                if pair and pair[1] > 0:
                    act.wait_ge(S[pair[0]], pair[1])

            def link(ins):
                chain[0] += 1
                ins.then_inc(S["act_chain"], 1)
                act.wait_ge(S["act_chain"], chain[0])

            def raises(ins, st, name):
                ins.then_inc(S[name], 1)

            def stat(st, i):
                return small[:, 3 * (st.on["rstd_ready"] % 3) + i, :]

            def before_squares(st):
                wait(("ms_ready", st.on["ms_ready"] - 1))
                wait(st.free["scr"])

            def squares(st, parts):
                for t, x in enumerate(parts):
                    ins = f(scr[:, 0:x.shape[1]], x, ACT.Square, accum_out=stat(st, 0)[:, t:t + 1])
                    if t + 1 < len(parts):
                        link(ins)
                ins.then_inc(S["sq_ready"], 1)

            def setup_gains(st):
                act.wait_ge(S["lam_in"], 1)
                f(small[:, 2, 14:16], small[:, 2, 12:14], ACT.Exp).then_inc(S["lam_exp"], 1)
                act.wait_ge(S["cols_sb"], 1)
                f(scol[:, :], cols[:, ROW["c"]:ROW["c"] + 16], ACT.Tanh, scale=0.5).then_inc(S["tanh_c"], 1)
                act.wait_ge(S["gains_ready"], 1)

            def split(st):
                s = st.sub
                raw_wait(act, s.raw)
                if s.i >= SPLIT_SLOTS:
                    act.wait_ge(S["sub_done"], s.i - SPLIT_SLOTS + 1)
                n = s.panel.ncols
                nc.scalar.copy(whi[:, s.i % SPLIT_SLOTS, 0:s.nk, 0:n],
                               raw[:, s.raw.i % RAW_SLOTS, s.koff:s.koff + s.nk, 0:n]).then_inc(S["hi_ready"], 1)

            def rows_norm(st):
                before_squares(st)
                for t in range(NT):
                    for name, value in st.waits:
                        if name != f"loaded_x{1 - t}":
                            wait((name, value - (name == "post_done" and t == 0)))
                    ins = f(scr[:, :], rows_of[st.src][:, t, :], ACT.Square, accum_out=stat(st, 0)[:, t:t + 1])
                    if t == 0:
                        link(ins)
                ins.then_inc(S["sq_ready"], 1)

            def rows_T(st):
                hi = (xhi if st.key == "x" else shi)[:, 4 * st.half:4 * st.half + 4, :]
                if st.bias is None:
                    wait(("rt_ps", st.on["rt_ps"]))
                    c = scale_cols(st.scale)
                    for k in range(4):
                        last = f(hi[:, k, :], acct(st.acc)[:, k, :], ACT.Copy,
                                 scale=c[:, 4 * st.half + k:4 * st.half + k + 1])
                else:
                    wait(("rt_tmp", st.on["rt_tmp"]))
                    last = nc.scalar.copy(hi, scr[:, :].rearrange("p (k t) -> p k t", t=T))
                last.then_inc(S["rt_hi"], 1)

            def evac_norm(st):
                act.wait_ge(S["sub_done"], st.done)
                before_squares(st)
                f(scr[:, :].rearrange("p (t n) -> p t n", t=NT), acc2(st.acc), ACT.Square).then_inc(S["sq_ready"], 1)

            def evac_copy(st):
                act.wait_ge(S["sub_done"], st.done)
                if st.dst == ("g2", 2):
                    wait(("cum_out", 16))
                nc.scalar.copy(grp(*st.dst).rearrange("p (t n) -> p t n", t=NT), acc2(st.acc)).then_inc(S["v_evac"], 1)

            def evac_gate(st):
                act.wait_ge(S["sub_done"], st.done)
                n = st.panel.ncols // P
                f(gates[:, st.tile:st.tile + n, :], acct(st.acc, n), ACT.Tanh, scale=0.5).then_inc(S["tanh_ready"], 1)

            def evac_conv_h(st):
                act.wait_ge(S["sub_done"], st.done)
                nc.scalar.copy(g2[:, 0:1024].rearrange("p (c t) -> p c t", t=T), acct(st.acc)).then_inc(S["v_evac"], 1)

            def evac_conv_b(st):
                act.wait_ge(S["sub_done"], st.done)
                nc.scalar.copy(g2[:, 1024:2048].rearrange("p (c t) -> p c t", t=T), acct(st.acc))\
                    .then_inc(S["v_evac"], 1)

            def conv(st):
                wait(("ytmp_ready", st.on["ytmp_ready"]))
                nc.scalar.copy(yhi[:, 8:12, :], g2[:, 2048:3072].rearrange("p (c t) -> p c t", t=T))\
                    .then_inc(S["yhi_ready"], 1)

            def forget_log(st):
                wait(("logf_a", 1))
                link(f(fe[:, :, :], fe[:, :, :], ACT.Exp))
                f(fe[:, :, :], fe[:, :, :], ACT.Ln, bias=1.0).then_inc(S["logf_e"], 1)

            def forget_sum(st):
                wait(("cum_sb", 1))
                nc.scalar.mul(cumT, opsum[0:12, 64:64 + T], -1.0).then_inc(S["cum_sb2"], 1)

            def qkT_(st):
                h = st.h
                wait(("qkT_ps", st.on["qkT_ps"]))
                wait(("s_ps", st.prev_s))
                if h.type == "G":
                    f(qkT[:, 0, :], tp[:, 0:T], ACT.Copy, scale=0.125).then_inc(S["qkT_sb"], 1)
                    return
                g = gain[h.gain if h.type == "X" else h.type]
                f(qkT[:, 0, :], tp[:, 0:T], ACT.Copy, scale=g[:, :])
                f(qkT[:, 1, :], tp[:, T:2 * T], ACT.Copy).then_inc(S["qkT_sb"], 1)

            def late_exp(st):
                exps(st.first)

            def exps(st):
                h = st.h
                wait(("mx_ready", st.on["mx_ready"]))
                if h.type in "AC":
                    for half in range(2 if h.type == "A" else 1):
                        for t in range(NT):
                            i = half * 2 + t
                            a = half * 384 + t * P
                            p = pbuf[:, a:a + P + t * P]
                            last = f(p, p, ACT.Exp, bias=nmx[:, i:i + 1], accum_out=rsum[:, i:i + 1])
                else:
                    wait(("PT_ps", st.prev_pt))
                    for t in range(NT):
                        src, dst = (spsum[:, h.n % 2, t * T:(t + 1) * T], pbuf[:, t * T:(t + 1) * T]) \
                            if h.type == "X" else (spsum[:, t, :], p2[:, t, :])
                        last = f(dst, src, ACT.Exp, bias=nmx[:, t:t + 1], accum_out=rsum[:, t:t + 1])
                last.then_inc(S["exp_ready"], 1)

            def PT(st):
                wait(("PT_ps", st.on["PT_ps"]))
                wait(("o_ps", st.prev_o))
                if st.h.type == "G":
                    dst, n = pt2[:, 2 * st.part:2 * st.part + 2, :], 512
                    nc.scalar.copy(dst, tp[:, :].rearrange("p (k t) -> p k t", t=T)).then_inc(S["PT_sb"], 1)
                    return
                n = 384 if st.h.type in "AC" else 512
                nc.scalar.copy(ptb[:, 0:n], tp[:, 0:n]).then_inc(S["PT_sb"], 1)

            def pv(st):
                h = st.h
                if h.type == "A":
                    before_squares(st)
                    wait(("o_ps", st.on["o_ps"]))
                    squares(st, [opsum[:, t * P:(t + 1) * P] for t in range(NT)])
                elif h.type == "G":
                    wait(("o_ps", st.on["o_ps"]))
                    b = h.base
                    nc.scalar.copy(yhi[b:b + 64, h.tile, :], opsum[b:b + 64, 0:T]).then_inc(S["yhi_ready"], 1)
                else:
                    wait(("ytmp_ready", st.on["ytmp_ready"]))
                    nc.scalar.copy(yhi[:, h.tile, :], ytmp[:, :]).then_inc(S["yhi_ready"], 1)

            def oT(st):
                wait(("ytmp_ready", st.on["ytmp_ready"]))
                nc.scalar.copy(yhi[:, st.h.tile, :], ytmp[:, :]).then_inc(S["yhi_ready"], 1)

            def decays(st):
                link(f(lg[:, :], lg[:, :], ACT.Exp))
                nc.scalar.mul(lg[:, :], lg[:, :], -1.0).then_inc(S["lg_exp"], 1)
                wait(("dec_arg", 1))
                d = dec[:, :, :, :].rearrange("p e t h -> p (e t h)")
                f(d, d, ACT.Exp).then_inc(S["dec_exp"], 1)

            def ctx_state(st):
                wait(("state_ps", 1))
                nc.scalar.mul(sfb, opsum[:, :].rearrange("p (h d) -> p h d", h=8), 0.125).then_inc(S["state_sb"], 1)

            def evac_kv(st):
                act.wait_ge(S["sub_done"], st.done)
                before_squares(st)
                f(scr[:, 0:256].rearrange("p (t n) -> p t n", t=NT), acc2(st.acc, P), ACT.Square)\
                    .then_inc(S["sq_ready"], 1)
                wait(("norm_mid", st.on["norm_mid"]))
                nc.scalar.copy(ctx_v if st.kind == "evac_ctxkv" else lat_v, acc2(st.acc, 2 * P)[:, :, P:2 * P])\
                    .then_inc(S["v_evac"], 1)

            def gqa_kT(st):
                wait(("kT_ps", 1))
                nc.scalar.copy(kT2[:, :], tp[:, :]).then_inc(S["kT_sb"], 1)

            def ret_T(st):
                wait(("qkT_ps", st.on["qkT_ps"]))
                wait(("s_ps", st.prev_s))
                nc.scalar.copy(qkT[:, :, :], tp[:, :].rearrange("p (a t) -> p a t", t=T)).then_inc(S["qkT_sb"], 1)

            def ret_T2(st):
                wait(("qkT_ps", st.on["qkT_ps"]))
                wait(("o_ps", st.prev_o))
                nc.scalar.copy(qfbT, tp[:, :].rearrange("p (a t) -> p a t", t=T)).then_inc(S["qkT_sb"], 1)

            def ret_decay(st):
                wait(("m_arg", st.on["m_arg"]))
                f(dmat[:, st.h % 2, :], dmat[:, st.h % 2, :], ACT.Exp).then_inc(S["m_exp"], 1)

            def ret_pv(st):
                wait(("o_ps", st.on["o_ps"]))
                nc.scalar.copy(ret[:, :, st.h * 64:(st.h + 1) * 64], opsum[:, 0:P].rearrange("p (t d) -> p t d", t=NT))\
                    .then_inc(S["ret_sb"], 1)

            def ret_norm(st):
                wait(("ret_mid", st.on["ret_mid"]))
                before_squares(st)
                f(scr[:, 0:512].rearrange("p (t n) -> p t n", t=NT), ret[:, :, st.half * T:(st.half + 1) * T],
                  ACT.Square).then_inc(S["sq_ready"], 1)

            def ret_out(st):
                wait(("ytmp_ready", st.on["ytmp_ready"]))
                k = 4 + 2 * st.half
                nc.scalar.copy(yhi[:, k:k + 2, :], scr[:, 0:512].rearrange("p (k t) -> p k t", t=T))\
                    .then_inc(S["yhi_ready"], 1)

            def evac_mix(st):
                act.wait_ge(S["sub_done"], st.done)
                wait(st.free["scr"])
                f(scr[:, 0:CW], acc2(st.acc)[:, 0, :], ACT.Square, accum_out=mixsq[:, st.c, 0:1])\
                    .then_inc(S["sq_ready"], 1)
                wait(("v_evac", st.on["v_evac"] - 1))
                wait(("sq_ready", st.on["sq_ready"] - 1))
                f(scr[:, 0:CW], acc2(st.acc)[:, 1, :], ACT.Square, accum_out=mixsq[:, st.c, 1:2])\
                    .then_inc(S["sq_ready"], 1)

            def evac_ffb(st):
                wait(("ytmp_ready", st.on["ytmp_ready"]))
                n = len(st.tiles)
                nc.scalar.copy(y_part(st.tiles[0], n, 0), scr[:, 0:n * T].rearrange("p (k t) -> p k t", t=T))\
                    .then_inc(S["yhi_ready"], 1)

            does = {"setup_gains": setup_gains, "split": split, "rows_norm": rows_norm, "rows_T": rows_T,
                    "evac_norm": evac_norm, "evac_normrope": evac_norm, "evac_copy": evac_copy, "evac_gate": evac_gate,
                    "evac_conv_z": evac_gate, "evac_ffa": evac_gate, "evac_conv_h": evac_conv_h,
                    "evac_conv_b": evac_conv_b, "conv": conv, "forget_log": forget_log, "forget_sum": forget_sum, "qkT": qkT_,
                    "exps": late_exp, "late_exp": late_exp, "PT": PT, "pv": pv, "oT": oT, "decays": decays, "ctx_state": ctx_state,
                    "evac_ctxkv": evac_kv, "evac_latkv": evac_kv, "gqa_kT": gqa_kT, "ret_T": ret_T,
                    "ret_T2": ret_T2, "ret_decay": ret_decay, "ret_pv": ret_pv, "ret_norm": ret_norm, "ret_out": ret_out,
                    "evac_mix": evac_mix, "evac_ffb": evac_ffb}
            for st in pl.steps:
                if st.kind in does:
                    does[st.kind](st)

        @block.vector
        def _(dve):
            tt, ts, stt = nc.vector.tensor_tensor, nc.vector.tensor_scalar, nc.vector.scalar_tensor_tensor
            chain = [0]

            def wait(pair):
                if pair and pair[1] > 0:
                    dve.wait_ge(S[pair[0]], pair[1])

            def link(ins):
                chain[0] += 1
                ins.then_inc(S["dve_chain"], 1)
                dve.wait_ge(S["dve_chain"], chain[0])

            def stat(st, i):
                return small[:, 3 * (st.on["rstd_ready"] % 3) + i, :]

            def mean(st, n, size):
                ts(stat(st, 1)[:, 0:n], stat(st, 0)[:, 0:n], 1.0 / size, EPS, ALU.mult, ALU.add)\
                    .then_inc(S["ms_ready"], 1)

            def mean_rstd(st, n, size):
                mean(st, n, size)
                wait(("rstd_ready", st.on["rstd_ready"]))

            def late_half(st):
                does_late[st.first.kind](st.first)

            def setup(st):
                dve.wait_ge(S["cols_ps"], 1)
                nc.vector.tensor_copy(cols[:, :], tp[:, 0:P + 9]).then_inc(S["cols_sb"], 1)

            def setup_gains(st):
                dve.wait_ge(S["loaded_first"], 16 * 3)
                lam = lam_rows.rearrange("p (a b d) -> p a b d", a=2, b=2)
                prod = ptb[:, 256:384].rearrange("p (a d) -> p a d", a=2)
                link(tt(prod, lam[:, :, 0, :], lam[:, :, 1, :], ALU.mult))
                nc.vector.tensor_reduce(small[:, 2, 12:14], prod, AX.X, ALU.add).then_inc(S["lam_in"], 1)
                dve.wait_ge(S["cols_sb"], 1)

                def col2(n):
                    return cols[:, P + ROW2[n]:P + ROW2[n] + 1]
                for name, a, b, s in (("A", "aq", "ak", 64 ** -0.5), ("ex", "exq", "exk", P ** -0.5),
                                      ("C", "cq", "ck", P ** -0.5), ("ox", "oxq", "oxk", P ** -0.5)):
                    stt(gain[name][:, :], col2(a), s, col2(b), ALU.mult, ALU.mult)
                ts(gain["aon"][:, :], col2("aon"), 0.5 * (1 - LAM_INIT), None, ALU.mult)
                dve.wait_ge(S["lam_exp"], 1)
                stt(neglam[:, :], small[:, 2, 15:16], -LAM_INIT, small[:, 2, 14:15], ALU.add, ALU.subtract)
                dve.wait_ge(S["tanh_c"], 1)
                link(stt(scol[:, :], scol[:, :], 1.0, cols[:, ROW["c"]:ROW["c"] + 16], ALU.add, ALU.mult))
                ts(scol[:, :], scol[:, :], 0.5, None, ALU.mult).then_inc(S["gains_ready"], 1)
                dve.wait_ge(S["gains_ready"], 1)

            def split(st):
                s, n = st.sub, st.sub.panel.ncols
                dve.wait_ge(S["hi_ready"], s.i + 1)
                slot = s.i % SPLIT_SLOTS
                tt(wlo[:, slot, 0:s.nk, 0:n], raw[:, s.raw.i % RAW_SLOTS, s.koff:s.koff + s.nk, 0:n],
                   whi[:, slot, 0:s.nk, 0:n].bitcast(F32), ALU.subtract).then_inc(S["lo_ready"], 1)

            def rows_norm(st):
                wait(("sq_ready", st.on["sq_ready"]))
                mean_rstd(st, NT, D)
                for t in range(NT):
                    last = ts(rows_of[st.dst][:, t, :], rows_of[st.src][:, t, :], stat(st, 2)[:, t:t + 1], None,
                              ALU.mult)
                last.then_inc(S["rows_ready"], 1)

            def rows_T(st):
                k0 = 4 * st.half
                hi, lo = (t[:, k0:k0 + 4, :] for t in ((xhi, xlo) if st.key == "x" else (shi, slo)))
                a = scale_cols(st.scale)
                if st.bias is None:
                    wait(("rt_hi", st.on["rt_hi"]))
                    for k in range(4):
                        last = stt(lo[:, k, :], acct(st.acc)[:, k, :], a[:, k0 + k:k0 + k + 1],
                                   hi[:, k, :].bitcast(F32), ALU.mult, ALU.subtract)
                    last.then_inc(S["rt_lo"], 1)
                    return
                b = scale_cols(st.bias)
                tmp = scr[:, :].rearrange("p (k t) -> p k t", t=T)
                wait(("rt_ps", st.on["rt_ps"]))
                wait(st.free["scr"])
                for k in range(4):
                    last = ts(tmp[:, k, :], acct(st.acc)[:, k, :], a[:, k0 + k:k0 + k + 1],
                              b[:, k0 + k:k0 + k + 1], ALU.mult, ALU.add)
                last.then_inc(S["rt_tmp"], 1)
                wait(("rt_hi", st.on["rt_hi"]))
                tt(lo, tmp, hi.bitcast(F32), ALU.subtract).then_inc(S["rt_lo"], 1)

            def evac_norm(st):
                n, gs = 1024 // st.gs, st.gs
                wait(("sq_ready", st.on["sq_ready"]))
                link(nc.vector.tensor_reduce(stat(st, 0)[:, 0:n], heads_of(scr[:, :], n, gs), AX.X, ALU.add))
                mean(st, n, gs)

            def evac_norm_late(st):
                n, gs = 1024 // st.gs, st.gs
                wait(("rstd_ready", st.on["rstd_ready"]))
                tt(heads_of(grp(*st.dst), n, gs), acc2(st.acc).rearrange("p t (h d) -> p (t h) d", d=gs),
                   across(stat(st, 2)[:, 0:n], [P, n, gs]), ALU.mult).then_inc(S["qk_evac"], 1)

            def evac_gate(st):
                wait(("tanh_ready", st.on["tanh_ready"]))
                n = st.panel.ncols // P
                g = gates[:, st.tile:st.tile + n, :]
                stt(g, g, 1.0, acct(st.acc, n), ALU.add, ALU.mult).then_inc(S["gate_ready"], 1)

            def evac_conv_c(st):
                wait(("v_evac", st.h_evac))
                dve.wait_ge(S["sub_done"], st.done)
                u = g2[:, 0:1024].rearrange("p (c t) -> p c t", t=T)
                tt(u, u, acct(st.acc), ALU.mult).then_inc(S["conv_u"], 1)

            def conv_taps(st):
                u, y = (g2[:, a:a + 1024].rearrange("p (c t) -> p c t", t=T) for a in (0, 2048))
                wait(("conv_u", 1))

                def tap(k, c):
                    return cols[:, ROW["conv_w"] + 4 * k + c:ROW["conv_w"] + 4 * k + c + 1]
                for c in range(4):
                    last = ts(y[:, c, :], u[:, c, :], tap(2, c), cols[:, ROW["conv_b"] + c:ROW["conv_b"] + c + 1],
                              ALU.mult, ALU.add)
                link(last)
                for c in range(4):
                    last = stt(y[:, c, 1:T], u[:, c, 0:T - 1], tap(1, c), y[:, c, 1:T], ALU.mult, ALU.add)
                link(last)
                for c in range(4):
                    last = stt(y[:, c, 2:T], u[:, c, 0:T - 2], tap(0, c), y[:, c, 2:T], ALU.mult, ALU.add)
                last.then_inc(S["taps_done"], 1)

            def conv(st):
                bb, y = (g2[:, a:a + 1024].rearrange("p (c t) -> p c t", t=T) for a in (1024, 2048))
                wait(("taps_done", 1))
                wait(("v_evac", st.v_evac))
                link(tt(y, y, bb, ALU.mult))
                wait(("gate_ready", st.gate))
                stt(y, y, 0.5, gates[:, 8:12, :], ALU.mult, ALU.mult).then_inc(S["ytmp_ready"], 1)
                wait(("yhi_ready", st.on["yhi_ready"]))
                tt(ylo[:, 8:12, :], y, yhi[:, 8:12, :].bitcast(F32), ALU.subtract).then_inc(S["y_ready"], 1)

            def evac_resid(st):
                dve.wait_ge(S["sub_done"], st.done)
                if st.on["resid_done"] == 1:
                    dve.wait_ge(S["loaded_x"], 16)
                r = h_res[:, :, st.c * CW:(st.c + 1) * CW]
                tt(r, acc2(st.acc), r, ALU.add).then_inc(S["resid_done"], 1)

            def evac_forget(st):
                dve.wait_ge(S["sub_done"], st.done)
                tt(fx[:, :, :], acc2(st.acc, 12), fbb[:, :].unsqueeze(1).to_broadcast([P, NT, 12]), ALU.add)\
                    .then_inc(S["forget_in"], 1)

            def forget_log(st):
                wait(("forget_in", 1))
                link(ts(fe[:, :, :], fx[:, :, :], -1.0, None, ALU.mult))
                tt(fe[:, :, :], fe[:, :, :], fx[:, :, :], ALU.min).then_inc(S["logf_a"], 1)

            def forget_sum(st):
                wait(("logf_e", 1))
                stt(logf[:, :, :], fx[:, :, :], 0.0, fe[:, :, :], ALU.min, ALU.subtract).then_inc(S["logf_ready"], 1)
                wait(("cum_ps", 1))
                nc.vector.tensor_copy(cumq[:, :, :], opsum[:, 0:24].rearrange("p (t h) -> p t h", t=NT))\
                    .then_inc(S["cum_sb"], 1)

            def scores(st):
                h = st.h
                wait(("s_ps", st.on["s_ps"]))
                bank = spsum[:, h.n % 2, :]
                if h.type == "A":
                    wait(("PT_ps", st.prev_pt))
                    p = pbuf[:, :].rearrange("p (a k) -> p a k", a=2)
                    stt(p, const("dist").unsqueeze(1).to_broadcast([P, 2, 384]), -(2.0 ** -(h.tile + 1)),
                        spsum[:, :, 0:384], ALU.mult, ALU.add).then_inc(S["s_rd"], 1)
                    wait(("s_rd", st.on["s_rd"]))
                    m = nmx[:, 0:4].rearrange("p (a t) -> p a t", t=2)
                    nc.vector.tensor_reduce(m[:, :, 0], p[:, :, 0:P], AX.X, ALU.max, negate=True)
                    nc.vector.tensor_reduce(m[:, :, 1], p[:, :, P:384], AX.X, ALU.max, negate=True)\
                        .then_inc(S["mx_ready"], 1)
                    return
                if h.type == "C":
                    wait(("PT_ps", st.prev_pt))
                    wait(("mask1", h.rows["mask1"]))
                    n = h.tile
                    stt(pbuf[:, 0:P], bank[:, 0:P], cumq[:, 0, n:n + 1], negcum0[:, h.j, :], ALU.add, ALU.add)
                    stt(pbuf[:, P:384], bank[:, P:384], cumq[:, 1, n:n + 1], negcum[:, h.j, :], ALU.add, ALU.add)\
                        .then_inc(S["s_rd"], 1)
                    wait(("s_rd", st.on["s_rd"]))
                    for t, part in enumerate(prob_parts(h)):
                        last = nc.vector.tensor_reduce(nmx[:, t:t + 1], part, AX.X, ALU.max, negate=True)
                elif h.type == "X":
                    last = nc.vector.tensor_reduce(nmx[:, 0:2], bank.rearrange("p (t k) -> p t k", t=NT), AX.X,
                                                   ALU.max, negate=True)
                else:
                    last = nc.vector.tensor_reduce(nmx[:, 0:2], spsum[:, :, :], AX.X, ALU.max, negate=True)
                last.then_inc(S["mx_ready"], 1)

            def prob_parts(h):
                return {"C": [pbuf[:, 0:P], pbuf[:, P:384]], "X": [pbuf[:, 0:T], pbuf[:, T:2 * T]],
                        "G": [p2[:, 0, :], p2[:, 1, :]]}[h.type]

            def scores_late(st):
                wait(("exp_ready", st.on["exp_ready"]))
                if st.h.type == "A":
                    p = pbuf[:, :].rearrange("p (a k) -> p a k", a=2)
                    link(nc.vector.reciprocal(rinv[:, :], rsum[:, :]))
                    link(ts(rinv[:, 2:4], rinv[:, 2:4], neglam[:, :], None, ALU.mult))
                    link(ts(p[:, 1, 0:P], p[:, 1, 0:P], rinv[:, 2:3], None, ALU.mult))
                    link(ts(p[:, 1, P:384], p[:, 1, P:384], rinv[:, 3:4], None, ALU.mult))
                    stt(p[:, 0, 0:P], p[:, 0, 0:P], rinv[:, 0:1], p[:, 1, 0:P], ALU.mult, ALU.add)
                    stt(p[:, 0, P:384], p[:, 0, P:384], rinv[:, 1:2], p[:, 1, P:384], ALU.mult, ALU.add)\
                        .then_inc(S["p_ready"], 1)
                    return
                link(nc.vector.reciprocal(rinv[:, 0:2], rsum[:, 0:2]))
                for t, part in enumerate(prob_parts(st.h)):
                    last = ts(part, part, rinv[:, t:t + 1], None, ALU.mult)
                last.then_inc(S["p_ready"], 1)

            def to_lo(st, tile):
                wait(("yhi_ready", st.on["yhi_ready"]))
                tt(ylo[:, tile, :], ytmp[:, :], yhi[:, tile, :].bitcast(F32), ALU.subtract).then_inc(S["y_ready"], 1)

            def pv(st):
                h = st.h
                if h.type == "A":
                    wait(("sq_ready", st.on["sq_ready"]))
                    mean(st, NT, P)
                elif h.type == "G":
                    wait(("yhi_ready", st.on["yhi_ready"]))
                    b = h.base
                    tt(ylo[b:b + 64, h.tile, :], opsum[b:b + 64, 0:T], yhi[b:b + 64, h.tile, :].bitcast(F32),
                       ALU.subtract).then_inc(S["y_ready"], 1)
                else:
                    wait(("o_ps", st.on["o_ps"]))
                    wait(("y_ready", st.on["y_ready"] - 1))
                    wait(("gate_ready", st.gate_ready))
                    stt(ytmp[:, :], opsum[:, 0:T], 0.5, gates[:, h.tile, :], ALU.mult, ALU.mult)\
                        .then_inc(S["ytmp_ready"], 1)
                    to_lo(st, h.tile)

            def pv_late(st):
                wait(("rstd_ready", st.on["rstd_ready"]))
                for t in range(NT):
                    last = ts(ytok[:, t * P:(t + 1) * P], opsum[:, t * P:(t + 1) * P], stat(st, 2)[:, t:t + 1],
                              None, ALU.mult)
                last.then_inc(S["on_ready"], 1)

            def oT(st):
                wait(("oT_ps", st.on["oT_ps"]))
                wait(("y_ready", st.on["y_ready"] - 1))
                wait(("gate_ready", st.gate_ready))
                stt(ytmp[:, :], tp[:, 0:T], gain["aon"][:, :], gates[:, st.h.tile, :], ALU.mult, ALU.mult)\
                    .then_inc(S["ytmp_ready"], 1)
                to_lo(st, st.h.tile)

            def mod(st):
                raw_wait(dve, st.raw)
                half = RAWK // 2
                for k in range(st.part * half, st.part * half + half):
                    for v in range(2 if st.ctx else 1):
                        c = scol[:, 8 * v + RAWK * st.u + k:8 * v + RAWK * st.u + k + 1]
                        src = raw[:, st.raw.i % RAW_SLOTS, k, :]
                        if st.u == 0 and k == 0:
                            ins = ts(macc[:, v, :], src, c, None, ALU.mult)
                        else:
                            ins = stt(macc[:, v, :], src, c, macc[:, v, :], ALU.mult, ALU.add)
                        if k % half == half - 1 and v == (1 if st.ctx else 0):
                            ins.then_inc(S["mod_read"], 1)
                            wait(("mod_read", st.on["mod_read"]))
                        elif v == (1 if st.ctx else 0):
                            link(ins)

            def mod_bias(st):
                wait(("bias_in", 16 * st.on["bias_in"]))
                tt(macc[0:1, 0, :], macc[0:1, 0, :], macc[0:1, 1, :], ALU.add).then_inc(S["bias_done"], 1)

            def mod_out(st):
                wait(("mod_ps", st.on["mod_ps"]))
                c = st.chunk
                if st.gate:
                    which = c >= 6
                    dve.wait_ge(S["loaded_post_ffn" if which else "loaded_post_mix"], 16)
                    g = post_gain[which][:, (c % 2) * CW:(c % 2 + 1) * CW]
                    tt(g, tp[:, :], g, ALU.mult).then_inc(S["mod_sb"], 1)
                    return
                for v in range(2 if st.ctx else 1):
                    last = tt(modc[:, v, 4 * c:4 * c + 4], opsum[:, 4 * v:4 * v + 4],
                              cols[:, ROW["b_mod"] + 4 * c:ROW["b_mod"] + 4 * c + 4], ALU.add)
                last.then_inc(S["mod_sb"], 1)

            def mod_cols(st):
                wait(("mod_sb", st.mod_sb))
                for name, v, at, g in ((("mix_A", 0, 8, "pre_mix"), ("ctx_A", 1, 8, "pre_mix"))
                                       if st.which == "mix" else (("ffn_A", 0, 32, "pre_ffn"),)):
                    link(stt(mcol[name][:, :], modc[:, v, at:at + 8], 1.0, cols[:, ROW[g]:ROW[g] + 8],
                             ALU.add, ALU.mult))

            def rope_tables(st):
                dve.wait_ge(S["loaded_rope"], 16 * 3)
                base = ropes["ret"]
                for i, n in enumerate(("q", "k")):
                    g = growb[:, 64 * i:64 * i + 64]

                    def rep(a):
                        return a.unsqueeze(1).to_broadcast([P, NT, a.shape[1]])
                    tt(ropes[n][:, 0, :, :], base[:, 0, :, :], rep(g), ALU.mult)
                    tt(ropes[n][:, 1, :, 0:32], base[:, 1, :, 0:32], rep(g[:, 32:64]), ALU.mult)
                    link(tt(ropes[n][:, 1, :, 32:64], base[:, 1, :, 32:64], rep(g[:, 0:32]), ALU.mult))

            def evac_kv(st):
                ctx_side = st.kind == "evac_ctxkv"
                wait(("sq_ready", st.on["sq_ready"]))
                link(nc.vector.tensor_reduce(stat(st, 0)[:, 0:4], heads_of(scr[:, 0:256], 4, 64), AX.X, ALU.add))
                mean_rstd(st, 4, 64)
                tmp = scr[:, 256:512].rearrange("p (t h d) -> p t h d", t=NT, h=2)
                rs = stat(st, 2)[:, 0:4].rearrange("p (t h) -> p t h", t=NT).unsqueeze(3).to_broadcast([P, NT, 2, 64])
                tt(tmp, acc2(st.acc, P).rearrange("p t (h d) -> p t h d", h=2), rs, ALU.mult)\
                    .then_inc(S["norm_mid"], 1)
                wait(("norm_mid", st.on["norm_mid"]))
                dst = (ctx_k if ctx_side else lat_k).rearrange("p t (h d) -> p t h d", h=2)
                if ctx_side:
                    g = growb[:, 64:128].unsqueeze(1).to_broadcast([P, 4, 64])
                    tt(dst.rearrange("p t h d -> p (t h) d"), tmp.rearrange("p t h d -> p (t h) d"), g, ALU.mult)\
                        .then_inc(S["rope_done"], 1)
                    return
                tb = ropes["k"]

                def rep(a):
                    return a.unsqueeze(2).to_broadcast([P, NT, 2, a.shape[2]])
                tt(dst[:, :, :, 0:32], tmp[:, :, :, 32:64], rep(tb[:, 1, :, 0:32]), ALU.mult)
                link(tt(dst[:, :, :, 32:64], tmp[:, :, :, 0:32], rep(tb[:, 1, :, 32:64]), ALU.mult))
                link(tt(tmp, tmp, rep(tb[:, 0, :, :]), ALU.mult))
                tt(dst, dst, tmp, ALU.add).then_inc(S["rope_done"], 1)

            def evac_rope(st):
                dve.wait_ge(S["sub_done"], st.done)
                wait(st.free["scr"])
                rope_tile(st, 0)

            def evac_rope_late(st):
                rope_tile(st, 1).then_inc(S["rope_done"], 1)

            def rope_tile(st, t):
                tb = ropes["ret"]
                x = acc2(st.acc)[:, t, :].rearrange("p (h d) -> p h d", d=64)
                y = grp(*st.dst)[:, t * CW:(t + 1) * CW].rearrange("p (h d) -> p h d", d=64)
                z = scr[:, t * CW:(t + 1) * CW].rearrange("p (h d) -> p h d", d=64)

                def rep(a):
                    return a.unsqueeze(1).to_broadcast([P, 8, a.shape[1]])
                tt(y[:, :, 0:32], x[:, :, 32:64], rep(tb[:, 1, t, 0:32]), ALU.mult)
                tt(y[:, :, 32:64], x[:, :, 0:32], rep(tb[:, 1, t, 32:64]), ALU.mult)
                link(tt(z, x, rep(tb[:, 0, t, :]), ALU.mult))
                return tt(y, y, z, ALU.add)

            def evac_normrope(st):
                wait(("sq_ready", st.on["sq_ready"]))
                link(nc.vector.tensor_reduce(stat(st, 0)[:, 0:16], heads_of(scr[:, :], 16, 64), AX.X, ALU.add))
                mean(st, 16, 64)

            def evac_normrope_late(st):
                wait(("rstd_ready", st.on["rstd_ready"]))
                tt(heads_of(scr[:, :], 16, 64), acc2(st.acc).rearrange("p t (h d) -> p (t h) d", d=64),
                   across(stat(st, 2)[:, 0:16], [P, 16, 64]), ALU.mult).then_inc(S["norm_mid"], 1)
                wait(("norm_mid", st.on["norm_mid"]))
                tb = ropes["q"]
                for t in range(NT):
                    x = scr[:, t * CW:(t + 1) * CW].rearrange("p (b a d) -> p b a d", b=2, a=4)
                    y = g0[:, t * CW:(t + 1) * CW].rearrange("p (a b d) -> p b a d", b=2, a=4)

                    def rep(a):
                        return a.unsqueeze(1).unsqueeze(1).to_broadcast([P, 2, 4, a.shape[1]])
                    tt(y[:, :, :, 0:32], x[:, :, :, 32:64], rep(tb[:, 1, t, 0:32]), ALU.mult)
                    link(tt(y[:, :, :, 32:64], x[:, :, :, 0:32], rep(tb[:, 1, t, 32:64]), ALU.mult))
                    link(tt(x, x, rep(tb[:, 0, t, :]), ALU.mult))
                    last = tt(y, y, x, ALU.add)
                last.then_inc(S["rope_done"], 1)

            def decays(st):
                wait(("lg_exp", 1))
                for e in range(4):
                    for t in range(NT):
                        last = ts(dec[:, e, t, :], lg[:, 8 * (e % 2):8 * (e % 2) + 8],
                                  const("expo", e * 2 + t, e * 2 + t + 1), None, ALU.mult)
                last.then_inc(S["dec_arg"], 1)

            def decayed(dst, src, e, done):
                for t in range(NT):
                    x = src[:, t * CW:(t + 1) * CW].rearrange("p (h d) -> p h d", d=64)
                    for fb in range(2):
                        last = tt(dst[:, t, :, fb, :], x, across(dec[:, e + fb, t, :], [P, 8, 64]), ALU.mult)
                last.then_inc(S[done], 1)

            def ctx_state(st):
                wait(("dec_exp", 1))
                wait(("v_evac", st.v_evac))
                decayed(kfb, grp("g2", 0), 2, "kfb_ready")

            def ret_q(st):
                wait(("state_ps", 1))
                wait(("rope_done", st.rope_done))
                decayed(qfb, grp("g1", 0), 0, "qfb_ready")

            def ret_decay(st):
                h = st.h
                dve.wait_ge(S["loaded_ret"], 16)
                m = dmat[:, h % 2, :]
                wait(("am_ready", st.am_read))
                link(ts(m, rett[:, 1, :], lg[:, 8 + h:9 + h], None, ALU.mult))
                stt(m, rett[:, 0, :], lg[:, h:h + 1], m, ALU.mult, ALU.add).then_inc(S["m_arg"], 1)

            def ret_scores(st):
                wait(("s_ps", st.on["s_ps"]))
                wait(("m_ready", st.m_ready))
                wait(("o_ps", st.prev_o))
                tt(am[:, st.h % 2, :], spsum[:, st.h % 2, :], dmat[:, st.h % 2, :], ALU.mult)\
                    .then_inc(S["am_ready"], 1)

            def ret_norm(st):
                r = ret[:, :, st.half * T:(st.half + 1) * T].rearrange("p t (h d) -> p t h d", d=64)
                mu = stat(st, 0)[:, 0:8]

                def each(a):
                    return a.rearrange("p (t h) -> p t h", t=NT).unsqueeze(3).to_broadcast([P, NT, 4, 64])
                wait(("ret_sb", st.ret_sb))
                link(nc.vector.tensor_reduce(mu.rearrange("p (t h) -> p t h", t=NT), r, AX.X, ALU.add))
                link(ts(mu, mu, 1.0 / 64, None, ALU.mult))
                tt(r, r, each(mu), ALU.subtract).then_inc(S["ret_mid"], 1)
                wait(("sq_ready", st.on["sq_ready"]))
                link(nc.vector.tensor_reduce(mu, heads_of(scr[:, 0:512], 8, 64), AX.X, ALU.add))
                mean_rstd(st, 8, 64)
                tt(r, r, each(stat(st, 2)[:, 0:8]), ALU.mult).then_inc(S["rn_ready"], 1)

            def ret_out(st):
                wait(("rt_ps", st.on["rt_ps"]))
                z = scr[:, 0:512].rearrange("p (k t) -> p k t", t=T)
                wait(("gate_ready", st.gate_ready))
                k = 4 + 2 * st.half
                stt(z, tp[:, :].rearrange("p (k t) -> p k t", t=T), 0.5, gates[:, k:k + 2, :], ALU.mult, ALU.mult)\
                    .then_inc(S["ytmp_ready"], 1)
                wait(("yhi_ready", st.on["yhi_ready"]))
                tt(ylo[:, k:k + 2, :], z, yhi[:, k:k + 2, :].bitcast(F32), ALU.subtract).then_inc(S["y_ready"], 1)

            def evac_mix(st):
                dve.wait_ge(S["sub_done"], st.done)
                wait(("mod_sb", st.mod_sb))
                c = slice(st.c * CW, (st.c + 1) * CW)
                tt(mixed[:, 1, c], acc2(st.acc)[:, 1, :], post_gain[st.which][:, c], ALU.mult).then_inc(S["v_evac"], 1)
                wait(("sq_ready", st.on["sq_ready"] - 1))
                tt(mixed[:, 0, c], acc2(st.acc)[:, 0, :], post_gain[st.which][:, c], ALU.mult).then_inc(S["v_evac"], 1)

            def post(st):
                wait(("sq_ready", st.sq_ready))
                link(tt(stat(st, 0)[:, 0:NT], mixsq[:, 0, :], mixsq[:, 1, :], ALU.add))
                mean_rstd(st, NT, D)
                wait(("v_evac", st.v_evac))
                for t in range(NT):
                    stt(h_res[:, t, :], mixed[:, t, :], stat(st, 2)[:, t:t + 1], h_res[:, t, :],
                        ALU.mult, ALU.add).then_inc(S["post_done"], 1)

            def evac_ffb(st):
                dve.wait_ge(S["sub_done"], st.done)
                wait(st.free["scr"])
                n = len(st.tiles)
                z = scr[:, 0:n * T].rearrange("p (k t) -> p k t", t=T)
                wait(("gate_ready", st.gate))
                stt(z, gates[:, st.gate_tile:st.gate_tile + n, :], 0.5, acct(st.acc, n), ALU.mult, ALU.mult)\
                    .then_inc(S["ytmp_ready"], 1)
                wait(("yhi_ready", st.on["yhi_ready"]))
                tt(y_part(st.tiles[0], n, 1), z, y_part(st.tiles[0], n, 0).bitcast(F32), ALU.subtract)\
                    .then_inc(S["y_ready"], 1)

            does_late = {"evac_norm": evac_norm_late, "evac_rope": evac_rope_late,
                         "evac_normrope": evac_normrope_late, "scores": scores_late, "pv": pv_late}
            does = {"setup": setup, "setup_gains": setup_gains, "split": split, "rows_norm": rows_norm,
                    "rows_T": rows_T, "evac_norm": evac_norm, "evac_gate": evac_gate, "evac_conv_z": evac_gate, "evac_ffa": evac_gate,
                    "evac_conv_c": evac_conv_c, "conv_taps": conv_taps, "late_half": late_half, "conv": conv, "evac_resid": evac_resid,
                    "evac_forget": evac_forget, "forget_log": forget_log, "forget_sum": forget_sum, "scores": scores, "pv": pv, "oT": oT,
                    "mod": mod, "mod_bias": mod_bias, "mod_out": mod_out, "mod_cols": mod_cols,
                    "rope_tables": rope_tables, "evac_ctxkv": evac_kv, "evac_latkv": evac_kv,
                    "evac_rope": evac_rope, "evac_normrope": evac_normrope, "decays": decays,
                    "ctx_state": ctx_state, "ret_q": ret_q, "ret_decay": ret_decay, "ret_scores": ret_scores,
                    "ret_norm": ret_norm, "ret_out": ret_out, "evac_mix": evac_mix, "post": post, "evac_ffb": evac_ffb}
            for st in pl.steps:
                if st.kind in does:
                    does[st.kind](st)

        @block.gpsimd
        def _(pool):
            def wait(pair):
                if pair and pair[1] > 0:
                    pool.wait_ge(S[pair[0]], pair[1])

            groups_of = {"rows_norm": NT, "evac_norm": 16, "evac_normrope": 16, "evac_ctxkv": 4, "evac_latkv": 4,
                         "pv": NT, "ret_norm": 8, "post": NT}

            def rstd(st):
                n = 1024 // st.gs if st.kind == "evac_norm" else groups_of[st.kind]
                i = 3 * (st.on["rstd_ready"] % 3)
                wait(("ms_ready", st.on["ms_ready"]))
                nc.gpsimd.tensor_tensor(small[:, i + 2, 0:n], small[:, i + 1, 0:n],
                                        half_neg[:, 0:n], ALU.pow).then_inc(S["rstd_ready"], 1)

            def forget_sum(st):
                wait(("cum_sb2", 1))
                pool.dma_start(scratch, cumT).then_inc(S["cum_out"], 16)

            def forget_rows(st):
                wait(("s_rd", st.prev))
                wait(("cum_out", 16))
                pool.dma_start(negcum[:, :, :], scratch[4 * st.g:4 * st.g + 4, :].unsqueeze(0).to_broadcast([P, 4, T]))\
                    .then_inc(S["rows_in"], 16)
                wait(("rows_in", 16 * st.on["rows_in"]))
                for dst, src, name in ((negcum0[:, :, :], negcum[:, :, 0:P], "mask0"),
                                       (negcum[:, :, P:T], negcum[:, :, P:T], "mask1")):
                    nc.gpsimd.affine_select(out=dst, in_=src, pattern=[[0, 4], [-1, P]], compare_op=ALU.is_ge,
                                            fill=BIG, base=0, channel_multiplier=1).then_inc(S[name], 1)

            def load(st):
                wait(("o_ps", st.after))
                wait(("rt_ps", st.rows))
                s = S["loaded_" + st.what]
                if st.what == "x":
                    pool.dma_start(h_res[:, :, :], w["x"].rearrange("b (t p) d -> p (b t) d", p=P)).then_inc(s, 16)
                elif st.what == "ctx":
                    pool.dma_start(rows_of["g2"], w["ctx_2"].rearrange("b (t p) d -> p (b t) d", p=P)).then_inc(s, 16)
                elif st.what == "rope":
                    pool.dma_start(g2[:, 2048:2304], w["const_rope"]).then_inc(s, 16)
                    pool.dma_start(growb[:, 0:64], w["q_norm_g_2"].to_broadcast([P, 64])).then_inc(s, 16)
                    pool.dma_start(growb[:, 64:128], w["k_norm_g_2"].to_broadcast([P, 64])).then_inc(s, 16)
                elif st.what == "ret":
                    pool.dma_start(rett[:, :, :].rearrange("p a n -> p (a n)"), w["const_ret"]).then_inc(s, 16)
                else:
                    i = st.what == "post_ffn"
                    pool.dma_start(post_gain[i], w["g_post_ffn_2" if i else "g_post_mix_2"].to_broadcast([P, D]))\
                        .then_inc(s, 16)

            def mod_bias_in(st):
                wait(("mod_ps", st.prev))
                pool.dma_start(macc[0:1, 1, :], w["b_mod_2"][:, st.chunk * CW:(st.chunk + 1) * CW])\
                    .then_inc(S["bias_in"], 16)

            def ret_decay(st):
                wait(("m_exp", st.on["m_exp"]))
                m = dmat[:, st.h % 2, :]
                nc.gpsimd.tensor_tensor(m, m, rett[:, 2, :], ALU.mult).then_inc(S["m_ready"], 1)

            pool.dma_start(h_res[:, :, :], w["mem"].rearrange("b (t p) d -> p (b t) d", p=P))\
                .then_inc(S["loaded_h"], 16)
            nc.gpsimd.memset(half_neg[:, :], -0.5).then_inc(S["setup_pool"], 1)
            pool.wait_ge(S["setup_pool"], 1)
            does = {"forget_sum": forget_sum, "forget_rows": forget_rows, "load": load, "mod_bias_in": mod_bias_in,
                    "ret_decay": ret_decay}
            for st in pl.steps:
                if st.kind in does:
                    does[st.kind](st)
                if st.kind in groups_of and "rstd_ready" in st.on:
                    rstd(st)



_INS = ["x", "mem", "e_norm_g", "e_w_in", "e_w_out", "e_a_q_norm_g", "e_a_k_norm_g", "e_a_lambda",
        "e_a_out_norm_g", "e_b_conv_w", "e_b_conv_b", "e_x_q_norm_g", "e_x_k_norm_g", "e_mem_norm_g",
        "e_w_mem_kv", "o_norm_g", "o_w_in", "o_w_out", "o_c_q_norm_g", "o_c_k_norm_g", "o_c_forget_b",
        "o_x_q_norm_g", "o_x_k_norm_g", "o_mem_norm_g", "o_w_mem_kv", "c_2", "ctx_2", "c_ctx_2", "w_mod_2",
        "b_mod_2", "g_pre_mix_2", "g_post_mix_2", "g_pre_ffn_2", "g_post_ffn_2", "w_in_2", "q_norm_g_2",
        "k_norm_g_2", "ret_decay_fwd_2", "ret_decay_bwd_2", "w_out_2", "w_ffn_in_2", "w_ffn_out_2"]
_ROWS = ["e_norm_g", "e_mem_norm_g", "o_norm_g", "o_mem_norm_g", "g_pre_mix_2", "g_pre_ffn_2", "b_mod_2", "c_2",
         "c_ctx_2", "e_b_conv_w", "e_b_conv_b"]
_HALF_ROWS = ["e_a_q_norm_g", "e_a_k_norm_g"]
_MORE_ROWS = ["e_a_out_norm_g", "e_x_q_norm_g", "e_x_k_norm_g", "o_c_q_norm_g", "o_c_k_norm_g", "o_x_q_norm_g",
              "o_x_k_norm_g"]
_EVERYWHERE = ["e_a_lambda", "o_c_forget_b", "ret_decay_fwd_2", "ret_decay_bwd_2"]
_MATRICES = {"e_w_in": "e_w_in", "e_w_out": "e_w_out", "e_w_mem_kv": "e_w_mem_kv", "o_w_in": "o_w_in",
             "o_w_out": "o_w_out", "o_w_mem_kv": "o_w_mem_kv", "w_mod": "w_mod_2", "w_in_2": "w_in_2",
             "w_out_2": "w_out_2", "w_ffn_in": "w_ffn_in_2", "w_ffn_out": "w_ffn_out_2"}


def kernel(**inputs):
    import concourse.bacc as bacc
    from concourse.bass_utils import run_bass_kernel_spmd

    nc = bacc.Bacc("TRN2", target_bir_lowering=False, num_devices=1)
    first_c, ret_c, rope_c = constants()
    arrays, w = {}, {}
    named = {name: np.ascontiguousarray(inputs[name]) for name in _INS}
    flat = [named[n].reshape(-1) for n in _ROWS]
    flat += [np.tile(named[n].reshape(-1), 2) for n in _HALF_ROWS] + [named[n].reshape(-1) for n in _MORE_ROWS]
    named["vec_rows"] = np.concatenate(flat).reshape(-1, P)
    named["vec_all"] = np.concatenate([named[n].reshape(-1) for n in _EVERYWHERE]).reshape(1, -1)
    for n in _ROWS + _HALF_ROWS + _MORE_ROWS + _EVERYWHERE:
        if n != "b_mod_2":
            del named[n]
    named.update(const_first=first_c, const_ret=ret_c, const_rope=rope_c)
    for name, a in named.items():
        arrays["in_" + name] = a
        w[name] = nc.dram_tensor("in_" + name, a.shape, mybir.dt.from_np(a.dtype), kind="ExternalInput").ap()
    for short, name in _MATRICES.items():
        w[short] = w[name].rearrange("a k n -> (a k) n")
    out = nc.dram_tensor("out_0", (1, T, D), F32, kind="ExternalOutput").ap()
    program(nc, w, out)
    r = run_bass_kernel_spmd(nc, [arrays], core_ids=[0])
    return r.results[0]["out_0"]
```
